# Optimizing a Trainium2 kernel written in Bass

```python
import math
import jax
import jax.numpy as jnp
from jax import lax
import numpy as np
import jax, jax.numpy as jnp

D_MODEL = 1024
BATCH = 1
SEQ = 256
DEPTH = 1

HEAD_DIM = 64
BRANCH_WIDTH = D_MODEL // 2
N_BRANCHES = 4
N_HEADS = BRANCH_WIDTH // HEAD_DIM
SSM_HEADS = N_HEADS
SSM_GROUPS = 2
SSM_STATE = 128
SSM_CONV = 4
SSM_CHUNK = 256
SSM_BC = SSM_GROUPS * SSM_STATE
SSM_CONV_DIM = BRANCH_WIDTH + 2 * SSM_BC
MOBA_BLOCK = 256
MOBA_TOPK = 3
MOBA_Q_CHUNK = 64
FOX_Q_BLOCK = 128
SWA_WINDOW = 128
SWA_KV_HEADS = 2
REL_BUCKETS = 32
REL_MAX_EXACT = REL_BUCKETS // 2
REL_MAX_DISTANCE = 1024
N_BIAS_HEADS = 2 * N_HEADS
D_FF = 256 * math.ceil(8 * D_MODEL / 3 / 256)
NORM_EPS = 1e-6
SPLIT_SIZES = (
    BRANCH_WIDTH,
    SSM_CONV_DIM,
    SSM_HEADS,
    3 * BRANCH_WIDTH,
    3 * BRANCH_WIDTH,
    N_HEADS,
    BRANCH_WIDTH,
    2 * SWA_KV_HEADS * HEAD_DIM,
    N_BRANCHES * D_MODEL,
)
D_IN_PROJ = sum(SPLIT_SIZES)
SPLIT_POINTS = [int(v) for v in np.cumsum(SPLIT_SIZES)[:-1]]


def rmsnorm(x, w):
    xf = x.astype(jnp.float32)
    y = xf * lax.rsqrt(jnp.mean(xf * xf, axis=-1, keepdims=True) + NORM_EPS)
    return (y * w.astype(jnp.float32)).astype(x.dtype)

def rel_bucket(dist):
    dist = jnp.maximum(dist, 0)
    d = jnp.maximum(dist, 1).astype(jnp.float32)
    large = REL_MAX_EXACT + (jnp.log(d / REL_MAX_EXACT) / math.log(REL_MAX_DISTANCE / REL_MAX_EXACT)
                             * (REL_BUCKETS - REL_MAX_EXACT)).astype(jnp.int32)
    large = jnp.minimum(large, REL_BUCKETS - 1)
    return jnp.where(dist < REL_MAX_EXACT, dist, large)

def causal_depthwise_conv(u, w, b):
    c = u.shape[-1]
    out = lax.conv_general_dilated(u, w.astype(u.dtype)[:, None, :], window_strides=(1,),
                                   padding=((w.shape[0] - 1, 0),),
                                   dimension_numbers=('NWC', 'WIO', 'NWC'),
                                   feature_group_count=c)
    return out + b.astype(u.dtype)

def ssd_chunked_scan(xs, bm, cm, dt_raw, dt_bias, a_log, d_skip):
    f32 = jnp.float32
    bsz, s_len, n_h, p_dim = xs.shape
    n_g, n_s = bm.shape[2], bm.shape[3]
    r = n_h // n_g
    lc = SSM_CHUNK
    nc = -(-s_len // lc)
    pad = nc * lc - s_len
    xs, bm, cm = xs.astype(f32), bm.astype(f32), cm.astype(f32)
    dt = jax.nn.softplus(dt_raw.astype(f32) + dt_bias.astype(f32))
    a = dt * (-jnp.exp(a_log.astype(f32)))

    def padseq(u):
        return jnp.pad(u, [(0, 0), (0, pad)] + [(0, 0)] * (u.ndim - 2))

    xc = padseq(xs * dt[..., None]).reshape(bsz, nc, lc, n_g, r, p_dim)
    bc = padseq(bm).reshape(bsz, nc, lc, n_g, n_s)
    cc = padseq(cm).reshape(bsz, nc, lc, n_g, n_s)
    acum_l = jnp.cumsum(padseq(a).reshape(bsz, nc, lc, n_g, r), axis=2)
    acum = jnp.moveaxis(acum_l, 2, -1)
    causal = jnp.tril(jnp.ones((lc, lc), dtype=bool))
    decay_in = jnp.exp(jnp.where(causal, acum[..., :, None] - acum[..., None, :], -jnp.inf))
    cb = jnp.einsum('bclgn,bcsgn->bcgls', cc, bc)
    y_diag = jnp.einsum('bcgrls,bcsgrp->bclgrp', cb[:, :, :, None] * decay_in, xc)
    decay_to_end = jnp.exp(acum_l[:, :, -1:] - acum_l)
    states = jnp.einsum('bclgn,bclgrp->bcgrpn', bc, xc * decay_to_end[..., None])
    chunk_decay = jnp.exp(acum[..., -1])

    def step(h, inp):
        st, dec = inp
        return h * dec[..., None, None] + st, h

    h0 = jnp.zeros((bsz, n_g, r, p_dim, n_s), f32)
    _, h_in = lax.scan(step, h0, (jnp.moveaxis(states, 1, 0), jnp.moveaxis(chunk_decay, 1, 0)))
    h_in = jnp.moveaxis(h_in, 0, 1)
    y_off = jnp.einsum('bclgn,bcgrpn->bclgrp', cc, h_in) * jnp.exp(acum_l)[..., None]
    y = (y_diag + y_off).reshape(bsz, nc * lc, n_h, p_dim)[:, :s_len]
    return y + d_skip.astype(f32)[:, None] * xs

def mamba2_branch(z, xbc, dt_raw, conv_w, conv_b, dt_bias, a_log, d_skip, norm_w):
    bsz, s_len, _ = z.shape
    xbc = jax.nn.silu(causal_depthwise_conv(xbc, conv_w, conv_b))
    xs, bm, cm = jnp.split(xbc, [BRANCH_WIDTH, BRANCH_WIDTH + SSM_BC], axis=-1)
    y = ssd_chunked_scan(xs.reshape(bsz, s_len, SSM_HEADS, HEAD_DIM),
                         bm.reshape(bsz, s_len, SSM_GROUPS, SSM_STATE),
                         cm.reshape(bsz, s_len, SSM_GROUPS, SSM_STATE),
                         dt_raw, dt_bias, a_log, d_skip)
    y = y.reshape(bsz, s_len, BRANCH_WIDTH).astype(z.dtype)
    return rmsnorm(y * jax.nn.silu(z), norm_w)

def moba_attention(q, k, v, bias_tab):
    f32 = jnp.float32
    bsz, s_len, n_h, hd = q.shape
    nblk = -(-s_len // MOBA_BLOCK)
    s_pad = nblk * MOBA_BLOCK
    topk = min(MOBA_TOPK, nblk)
    scale = hd ** -0.5
    qh = q.transpose(0, 2, 1, 3)

    def blocks(u):
        u = jnp.pad(u, ((0, 0), (0, s_pad - s_len), (0, 0), (0, 0)))
        return u.reshape(bsz, nblk, MOBA_BLOCK, n_h, hd).transpose(0, 3, 1, 2, 4)

    kb, vb = blocks(k), blocks(v)
    k_mean = jnp.mean(kb.astype(f32), axis=3)
    q_blk = jnp.arange(s_len) // MOBA_BLOCK
    gate = jnp.einsum('bhsd,bhnd->bhsn', qh.astype(f32), k_mean)
    fully_past = jnp.arange(nblk)[None, :] < q_blk[:, None]
    gate = jnp.where(fully_past, gate, -jnp.inf)
    _, sel = lax.top_k(gate, topk)
    sel_valid = jnp.arange(topk)[None, :] < q_blk[:, None]
    bias_ht = bias_tab.T.astype(f32)
    b_idx = jnp.arange(bsz)[:, None, None, None]
    h_idx = jnp.arange(n_h)[None, :, None, None]
    blk_off = jnp.arange(MOBA_BLOCK)

    def chunk(c):
        start = c * MOBA_Q_CHUNK
        qc = lax.dynamic_slice_in_dim(qh, start, MOBA_Q_CHUNK, axis=2)
        selc = lax.dynamic_slice_in_dim(sel, start, MOBA_Q_CHUNK, axis=2)
        validc = lax.dynamic_slice_in_dim(sel_valid, start, MOBA_Q_CHUNK, axis=0)
        qpos = start + jnp.arange(MOBA_Q_CHUNK)
        kg = kb[b_idx, h_idx, selc]
        vg = vb[b_idx, h_idx, selc]
        s_sel = jnp.einsum('bhqd,bhqkjd->bhqkj', qc, kg).astype(f32) * scale
        kpos = selc[..., None] * MOBA_BLOCK + blk_off
        s_sel = s_sel + bias_ht[h_idx[..., None], rel_bucket(qpos[:, None, None] - kpos)]
        s_sel = jnp.where(validc[None, None, :, :, None], s_sel, -jnp.inf)
        own = start // MOBA_BLOCK
        ko = lax.dynamic_index_in_dim(kb, own, axis=2, keepdims=False)
        vo = lax.dynamic_index_in_dim(vb, own, axis=2, keepdims=False)
        dist_own = qpos[:, None] - (own * MOBA_BLOCK + blk_off)[None, :]
        s_own = jnp.einsum('bhqd,bhjd->bhqj', qc, ko).astype(f32) * scale
        s_own = s_own + bias_ht[:, rel_bucket(dist_own)][None]
        s_own = jnp.where(dist_own >= 0, s_own, -jnp.inf)
        logits = jnp.concatenate([s_sel.reshape(bsz, n_h, MOBA_Q_CHUNK, topk * MOBA_BLOCK), s_own], axis=-1)
        p = jax.nn.softmax(logits, axis=-1)
        p_sel = p[..., :topk * MOBA_BLOCK].reshape(bsz, n_h, MOBA_Q_CHUNK, topk, MOBA_BLOCK).astype(v.dtype)
        p_own = p[..., topk * MOBA_BLOCK:].astype(v.dtype)
        return (jnp.einsum('bhqkj,bhqkjd->bhqd', p_sel, vg)
                + jnp.einsum('bhqj,bhjd->bhqd', p_own, vo))

    out = lax.map(chunk, jnp.arange(s_len // MOBA_Q_CHUNK))
    return out.transpose(1, 0, 3, 2, 4).reshape(bsz, s_len, n_h * hd)

def forgetting_attention(q, k, v, f_logit):
    f32 = jnp.float32
    bsz, s_len, n_h, hd = q.shape
    scale = hd ** -0.5
    cum = jnp.cumsum(jax.nn.log_sigmoid(f_logit.astype(f32)), axis=1).transpose(0, 2, 1)
    qh, kh, vh = (u.transpose(0, 2, 1, 3) for u in (q, k, v))
    kpos = jnp.arange(s_len)

    def block(i):
        start = i * FOX_Q_BLOCK
        qb = lax.dynamic_slice_in_dim(qh, start, FOX_Q_BLOCK, axis=2)
        cq = lax.dynamic_slice_in_dim(cum, start, FOX_Q_BLOCK, axis=2)
        s = (jnp.einsum('bhqd,bhkd->bhqk', qb, kh).astype(f32) * scale
             + (cq[..., :, None] - cum[..., None, :]))
        causal = (start + jnp.arange(FOX_Q_BLOCK))[:, None] >= kpos[None, :]
        p = jax.nn.softmax(jnp.where(causal, s, -jnp.inf), axis=-1)
        return jnp.einsum('bhqk,bhkd->bhqd', p.astype(v.dtype), vh)

    out = lax.map(block, jnp.arange(s_len // FOX_Q_BLOCK))
    return out.transpose(1, 0, 3, 2, 4).reshape(bsz, s_len, n_h * hd)

def sliding_window_attention(q, k, v, sinks, bias_tab):
    f32 = jnp.float32
    bsz, s_len, n_q, hd = q.shape
    n_kv = k.shape[2]
    grp = n_q // n_kv
    w = SWA_WINDOW
    nb = s_len // w
    scale = hd ** -0.5
    qb = q.reshape(bsz, nb, w, n_kv, grp, hd)

    def band(u):
        ub = u.reshape(bsz, nb, w, n_kv, hd)
        prev = jnp.pad(ub, ((0, 0), (1, 0), (0, 0), (0, 0), (0, 0)))[:, :-1]
        return jnp.concatenate([prev, ub], axis=2)

    kk, vv = band(k), band(v)
    s = jnp.einsum('bnqkgd,bnjkd->bnkgqj', qb, kk).astype(f32) * scale
    qi = jnp.arange(w)[:, None]
    kj = jnp.arange(2 * w)[None, :]
    dist = qi + w - kj
    in_window = (dist >= 0) & (dist < w)
    key_pos = jnp.arange(nb)[:, None, None] * w + kj[None] - w
    mask = in_window[None] & (key_pos >= 0)
    bias = bias_tab.astype(f32)[rel_bucket(dist)].transpose(2, 0, 1).reshape(n_kv, grp, w, 2 * w)
    s = jnp.where(mask[None, :, None, None], s + bias, -jnp.inf)
    sink = jnp.broadcast_to(sinks.astype(f32).reshape(n_kv, grp, 1, 1), s.shape[:-1] + (1,))
    p = jax.nn.softmax(jnp.concatenate([s, sink], axis=-1), axis=-1)[..., :-1]
    out = jnp.einsum('bnkgqj,bnjkd->bnqkgd', p.astype(v.dtype), vv)
    return out.reshape(bsz, s_len, n_q * hd)

def hybrid_mixer(h, w_in, conv_w, conv_b, dt_bias, a_log, d_skip, ssm_norm_w,
                 forget_bias, sinks, rel_bias, w_branch, w_out):
    bsz, s_len, _ = h.shape
    proj = h @ w_in
    (m_z, m_xbc, m_dt, b_qkv, c_qkv, c_f, d_q, d_kv, gate_logits) = jnp.split(proj, SPLIT_POINTS, axis=-1)

    def heads(u, n):
        return u.reshape(bsz, s_len, n, HEAD_DIM)

    y_a = mamba2_branch(m_z, m_xbc, m_dt, conv_w, conv_b, dt_bias, a_log, d_skip, ssm_norm_w)
    bq, bk, bv = jnp.split(b_qkv, 3, axis=-1)
    y_b = moba_attention(heads(bq, N_HEADS), heads(bk, N_HEADS), heads(bv, N_HEADS), rel_bias[:, :N_HEADS])
    cq, ck, cv = jnp.split(c_qkv, 3, axis=-1)
    y_c = forgetting_attention(heads(cq, N_HEADS), heads(ck, N_HEADS), heads(cv, N_HEADS), c_f + forget_bias)
    dk, dv = jnp.split(d_kv, 2, axis=-1)
    y_d = sliding_window_attention(heads(d_q, N_HEADS), heads(dk, SWA_KV_HEADS), heads(dv, SWA_KV_HEADS),
                                   sinks, rel_bias[:, N_HEADS:])
    branches = jnp.stack([y_a, y_b, y_c, y_d], axis=2)
    branch_out = jnp.einsum('bsiw,iwd->bsid', branches, w_branch)
    gates = jax.nn.sigmoid(gate_logits.reshape(bsz, s_len, N_BRANCHES, D_MODEL))
    return jnp.sum(gates * branch_out, axis=2) @ w_out

def swiglu(h, w_gate, w_up, w_down):
    return (jax.nn.silu(h @ w_gate) * (h @ w_up)) @ w_down

def first_inputs(seed: int = 0) -> dict:
    key = jax.random.key(seed)
    ks = jax.random.split(key, 20)
    nrm = jax.random.normal
    x = nrm(ks[0], (BATCH, SEQ, D_MODEL), jnp.float32)
    w_in = nrm(ks[1], (DEPTH, D_MODEL, D_IN_PROJ), jnp.float32) * D_MODEL ** -0.5
    conv_w = nrm(ks[2], (DEPTH, SSM_CONV, SSM_CONV_DIM), jnp.float32) * SSM_CONV ** -0.5
    conv_b = 0.02 * nrm(ks[3], (DEPTH, SSM_CONV_DIM), jnp.float32)
    dt0 = jnp.exp(jax.random.uniform(ks[4], (DEPTH, SSM_HEADS), jnp.float32,
                                     minval=math.log(1e-3), maxval=math.log(1e-1)))
    dt_bias = dt0 + jnp.log(-jnp.expm1(-dt0))
    a_log = jnp.log(jax.random.uniform(ks[5], (DEPTH, SSM_HEADS), jnp.float32, minval=1.0, maxval=16.0))
    d_skip = 1.0 + 0.1 * nrm(ks[6], (DEPTH, SSM_HEADS), jnp.float32)
    ssm_norm_w = 1.0 + 0.05 * nrm(ks[7], (DEPTH, BRANCH_WIDTH), jnp.float32)
    forget_bias = jax.random.uniform(ks[8], (DEPTH, N_HEADS), jnp.float32, minval=1.0, maxval=6.0)
    sinks = nrm(ks[9], (DEPTH, N_HEADS), jnp.float32)
    rel_bias = 0.3 * nrm(ks[10], (REL_BUCKETS, N_BIAS_HEADS), jnp.float32)
    w_branch = nrm(ks[11], (DEPTH, N_BRANCHES, BRANCH_WIDTH, D_MODEL), jnp.float32) * BRANCH_WIDTH ** -0.5
    w_out = nrm(ks[12], (DEPTH, D_MODEL, D_MODEL), jnp.float32) * D_MODEL ** -0.5
    norm_mix = 1.0 + 0.05 * nrm(ks[13], (DEPTH, D_MODEL), jnp.float32)
    norm_ffn = 1.0 + 0.05 * nrm(ks[14], (DEPTH, D_MODEL), jnp.float32)
    w_ffn_gate = nrm(ks[15], (DEPTH, D_MODEL, D_FF), jnp.float32) * D_MODEL ** -0.5
    w_ffn_up = nrm(ks[16], (DEPTH, D_MODEL, D_FF), jnp.float32) * D_MODEL ** -0.5
    w_ffn_down = nrm(ks[17], (DEPTH, D_FF, D_MODEL), jnp.float32) * D_FF ** -0.5
    norm_final = 1.0 + 0.05 * nrm(ks[18], (D_MODEL,), jnp.float32)
    return {'x': x, 'w_in': w_in, 'conv_w': conv_w, 'conv_b': conv_b, 'dt_bias': dt_bias,
            'a_log': a_log, 'd_skip': d_skip, 'ssm_norm_w': ssm_norm_w, 'forget_bias': forget_bias,
            'sinks': sinks, 'rel_bias': rel_bias, 'w_branch': w_branch, 'w_out': w_out,
            'norm_mix': norm_mix, 'norm_ffn': norm_ffn, 'w_ffn_gate': w_ffn_gate,
            'w_ffn_up': w_ffn_up, 'w_ffn_down': w_ffn_down, 'norm_final': norm_final}

def first_block(x, w_in, conv_w, conv_b, dt_bias, a_log, d_skip, ssm_norm_w, forget_bias,
              sinks, rel_bias, w_branch, w_out, norm_mix, norm_ffn, w_ffn_gate,
              w_ffn_up, w_ffn_down, norm_final):
    for l in range(DEPTH):
        h = rmsnorm(x, norm_mix[l])
        x = x + hybrid_mixer(h, w_in[l], conv_w[l], conv_b[l], dt_bias[l], a_log[l], d_skip[l],
                             ssm_norm_w[l], forget_bias[l], sinks[l], rel_bias, w_branch[l], w_out[l])
        h = rmsnorm(x, norm_ffn[l])
        x = x + swiglu(h, w_ffn_gate[l], w_ffn_up[l], w_ffn_down[l])
    return rmsnorm(x, norm_final)


D_CONV = 1024
CONV_WIDTH = 31
RWKV_HEAD = 64
RWKV_HEADS = D_MODEL // RWKV_HEAD
D_RWKV = RWKV_HEADS * RWKV_HEAD
DECAY_LORA = 64
AAA_LORA = 64
TS_WIDTH = 3 * D_RWKV + DECAY_LORA + AAA_LORA
SPLITS = (D_CONV, 2 * D_CONV, 3 * D_CONV, 3 * D_CONV + TS_WIDTH, 3 * D_CONV + TS_WIDTH + D_RWKV, 3 * D_CONV + TS_WIDTH + D_RWKV + D_MODEL)
D_IN = 3 * D_CONV + TS_WIDTH + D_RWKV + 2 * D_MODEL
RWKV_SPLITS = (D_RWKV, 2 * D_RWKV, 3 * D_RWKV, 3 * D_RWKV + DECAY_LORA)

RMS_EPS = 1e-6
LN_EPS = 1e-5
GN_EPS = 64e-5
L2_EPS = 1e-12


def _rmsnorm(x, g):
    xf = x.astype(jnp.float32)
    y = xf * lax.rsqrt(jnp.mean(xf * xf, axis=-1, keepdims=True) + RMS_EPS)
    return (y * g.astype(jnp.float32)).astype(x.dtype)

def _layernorm(x, g, b, eps):
    xf = x.astype(jnp.float32)
    mu = jnp.mean(xf, axis=-1, keepdims=True)
    var = jnp.mean(jnp.square(xf - mu), axis=-1, keepdims=True)
    y = (xf - mu) * lax.rsqrt(var + eps) * g.astype(jnp.float32) + b.astype(jnp.float32)
    return y.astype(x.dtype)

def _causal_depthwise_conv(u, w, b):
    y = lax.conv_general_dilated(
        u, w[:, None, :].astype(u.dtype), window_strides=(1,),
        padding=((CONV_WIDTH - 1, 0),), dimension_numbers=('NWC', 'WIO', 'NWC'),
        feature_group_count=u.shape[-1])
    return y + b

def _token_shift(z, mu):
    prev = jnp.pad(z, ((0, 0), (1, 0), (0, 0)))[:, :-1]
    return z + mu * (prev - z)

def _rwkv7_scan(r, decay, k, v, kk, b):
    bsz, _, h, n = r.shape

    def step(state, inp):
        r_t, w_t, k_t, v_t, kk_t, b_t = inp
        sk = jnp.einsum('bhvk,bhk->bhv', state, kk_t)
        state = (state * w_t[:, :, None, :] - sk[..., None] * b_t[:, :, None, :]
                 + v_t[..., None] * k_t[:, :, None, :])
        return state, jnp.einsum('bhvk,bhk->bhv', state, r_t)

    xs = tuple(jnp.moveaxis(t, 1, 0) for t in (r, decay, k, v, kk, b))
    s0 = jnp.zeros((bsz, h, n, n), jnp.float32)
    _, out = lax.scan(step, s0, xs)
    return jnp.moveaxis(out, 0, 1)

def _rwkv7_branch(ts, og, mu, w0, w2, a0, a2, k_k, k_a, r_k, gn_g, gn_b, w_o):
    f32 = jnp.float32
    bsz, seq, _ = ts.shape
    hd = (bsz, seq, RWKV_HEADS, RWKV_HEAD)
    r, k, v, w_low, a_low = jnp.split(_token_shift(ts, mu), RWKV_SPLITS, axis=-1)
    w_pre = (w0 + jnp.tanh(w_low) @ w2).astype(f32)
    decay = jnp.exp(-jnp.exp(-jax.nn.softplus(-w_pre) - 0.5))
    a = jax.nn.sigmoid((a0 + a_low @ a2).astype(f32))
    kk = (k * k_k).astype(f32).reshape(hd)
    kk = kk / jnp.maximum(jnp.sqrt(jnp.sum(kk * kk, axis=-1, keepdims=True)), L2_EPS)
    k = (k.astype(f32) * (1.0 + (a - 1.0) * k_a.astype(f32))).reshape(hd)
    r = r.astype(f32).reshape(hd)
    v = v.astype(f32).reshape(hd)
    a = a.reshape(hd)
    o = _rwkv7_scan(r, decay.reshape(hd), k, v, kk, kk * a)
    o = _layernorm(o, gn_g.reshape(RWKV_HEADS, RWKV_HEAD), gn_b.reshape(RWKV_HEADS, RWKV_HEAD), GN_EPS)
    o = o + jnp.sum(r * k * r_k.astype(f32), axis=-1, keepdims=True) * v
    o = o.reshape(bsz, seq, D_RWKV).astype(og.dtype) * jax.nn.silu(og)
    return o @ w_o

def _conv_branch(val, gate, og, conv_k, conv_b, ln_g, ln_b, w_o):
    u = val * jax.nn.sigmoid(gate)
    u = _causal_depthwise_conv(u, conv_k, conv_b)
    u = _layernorm(u, ln_g, ln_b, LN_EPS)
    u = jax.nn.silu(u) * jax.nn.silu(og)
    return u @ w_o

def second_inputs(seed: int = 0) -> dict:
    key = jax.random.key(seed)
    ks = jax.random.split(key, 24)
    f32 = jnp.float32
    nrm = lambda k, shape, s: jax.random.normal(k, shape, f32) * s
    L = DEPTH
    return {
        'x': nrm(ks[0], (BATCH, SEQ, D_MODEL), 1.0),
        'c': nrm(ks[1], (BATCH, D_MODEL), 1.0),
        'ada_w': nrm(ks[2], (L, D_MODEL, 3 * D_MODEL), 0.5 * D_MODEL ** -0.5),
        'ada_b': nrm(ks[3], (L, 3 * D_MODEL), 0.01),
        'norm_g': 1.0 + nrm(ks[4], (L, D_MODEL), 0.1),
        'w_in': nrm(ks[5], (L, D_MODEL, D_IN), D_MODEL ** -0.5),
        'conv_k': nrm(ks[6], (L, CONV_WIDTH, D_CONV), CONV_WIDTH ** -0.5),
        'conv_b': nrm(ks[7], (L, D_CONV), 0.01),
        'conv_ln_g': 1.0 + nrm(ks[8], (L, D_CONV), 0.1),
        'conv_ln_b': nrm(ks[9], (L, D_CONV), 0.01),
        'w_conv_out': nrm(ks[10], (L, D_CONV, D_MODEL), D_CONV ** -0.5),
        'rwkv_mu': jax.random.uniform(ks[11], (L, TS_WIDTH), f32, 0.0, 1.0),
        'rwkv_w0': jax.random.uniform(ks[12], (L, D_RWKV), f32, -6.0, -1.0),
        'rwkv_w2': nrm(ks[13], (L, DECAY_LORA, D_RWKV), 0.1 * DECAY_LORA ** -0.5),
        'rwkv_a0': nrm(ks[14], (L, D_RWKV), 0.1),
        'rwkv_a2': nrm(ks[15], (L, AAA_LORA, D_RWKV), 0.5 * AAA_LORA ** -0.5),
        'rwkv_k_k': 0.85 + nrm(ks[16], (L, D_RWKV), 0.05),
        'rwkv_k_a': 1.0 + nrm(ks[17], (L, D_RWKV), 0.05),
        'rwkv_r_k': nrm(ks[18], (L, RWKV_HEADS, RWKV_HEAD), 0.1),
        'rwkv_gn_g': 1.0 + nrm(ks[19], (L, D_RWKV), 0.1),
        'rwkv_gn_b': nrm(ks[20], (L, D_RWKV), 0.01),
        'w_rwkv_out': nrm(ks[21], (L, D_RWKV, D_MODEL), D_RWKV ** -0.5),
        'w_out': nrm(ks[22], (L, D_MODEL, D_MODEL), D_MODEL ** -0.5),
        'final_g': 1.0 + nrm(ks[23], (D_MODEL,), 0.1),
    }

def second_block(x, c, ada_w, ada_b, norm_g, w_in, conv_k, conv_b, conv_ln_g, conv_ln_b, w_conv_out,
              rwkv_mu, rwkv_w0, rwkv_w2, rwkv_a0, rwkv_a2, rwkv_k_k, rwkv_k_a, rwkv_r_k,
              rwkv_gn_g, rwkv_gn_b, w_rwkv_out, w_out, final_g):
    for l in range(DEPTH):
        mod = jnp.einsum('bd,de->be', jax.nn.silu(c), ada_w[l]) + ada_b[l]
        shift, scale, gate = jnp.split(mod, 3, axis=-1)
        h = _rmsnorm(x, norm_g[l]) * (1.0 + scale[:, None, :]) + shift[:, None, :]
        p = jnp.einsum('bsd,de->bse', h, w_in[l])
        c_val, c_gate, c_og, ts, r_og, g_conv, g_rwkv = jnp.split(p, SPLITS, axis=-1)
        y_conv = _conv_branch(c_val, c_gate, c_og, conv_k[l], conv_b[l], conv_ln_g[l], conv_ln_b[l],
                              w_conv_out[l])
        y_rwkv = _rwkv7_branch(ts, r_og, rwkv_mu[l], rwkv_w0[l], rwkv_w2[l], rwkv_a0[l], rwkv_a2[l],
                               rwkv_k_k[l], rwkv_k_a[l], rwkv_r_k[l], rwkv_gn_g[l], rwkv_gn_b[l],
                               w_rwkv_out[l])
        m = jax.nn.sigmoid(g_conv) * y_conv + jax.nn.sigmoid(g_rwkv) * y_rwkv
        out = jnp.einsum('bsd,de->bse', m, w_out[l])
        x = x + gate[:, None, :] * out
    return _rmsnorm(x, final_g)


def setup_inputs(seed=0):
    out = dict(first_inputs(seed))
    for name, value in second_inputs(seed + 1).items():
        if name != "x":
            out[name + "_2"] = value
    return out


def reference(
    x, w_in, conv_w, conv_b, dt_bias, a_log, d_skip, ssm_norm_w, forget_bias, sinks, rel_bias,
    w_branch, w_out, norm_mix, norm_ffn, w_ffn_gate, w_ffn_up, w_ffn_down, norm_final, c_2,
    ada_w_2, ada_b_2, norm_g_2, w_in_2, conv_k_2, conv_b_2, conv_ln_g_2, conv_ln_b_2,
    w_conv_out_2, rwkv_mu_2, rwkv_w0_2, rwkv_w2_2, rwkv_a0_2, rwkv_a2_2, rwkv_k_k_2, rwkv_k_a_2,
    rwkv_r_k_2, rwkv_gn_g_2, rwkv_gn_b_2, w_rwkv_out_2, w_out_2, final_g_2,
):
    x = first_block(
        x, w_in, conv_w, conv_b, dt_bias, a_log, d_skip, ssm_norm_w, forget_bias, sinks,
        rel_bias, w_branch, w_out, norm_mix, norm_ffn, w_ffn_gate, w_ffn_up, w_ffn_down,
        norm_final,
    )
    return second_block(
        x, c_2, ada_w_2, ada_b_2, norm_g_2, w_in_2, conv_k_2, conv_b_2, conv_ln_g_2,
        conv_ln_b_2, w_conv_out_2, rwkv_mu_2, rwkv_w0_2, rwkv_w2_2, rwkv_a0_2, rwkv_a2_2,
        rwkv_k_k_2, rwkv_k_a_2, rwkv_r_k_2, rwkv_gn_g_2, rwkv_gn_b_2, w_rwkv_out_2, w_out_2,
        final_g_2,
    )


_drawn_inputs = setup_inputs


def setup_inputs(seed=0):
    import zlib

    import numpy as np

    out = dict(_drawn_inputs(seed))
    spreads = {}
    factors = {'conv_b': 4.322,
     'sinks': 4.054,
     'ada_b_2': 8.0,
     'conv_b_2': 8.0,
     'conv_ln_g_2': 6.812,
     'conv_ln_b_2': 64.0,
     'rwkv_w2_2': 8.0,
     'rwkv_a0_2': 8.0,
     'rwkv_k_k_2': 18.558,
     'rwkv_k_a_2': 6.25,
     'rwkv_gn_g_2': 4.464,
     'rwkv_gn_b_2': 59.559}
    for name, (base, spread) in spreads.items():
        noise = np.random.default_rng([zlib.crc32(name.encode()), seed]).standard_normal(out[name].shape)
        drawn = base * np.exp(spread * noise) if base else spread * noise
        out[name] = jnp.asarray(drawn.astype(out[name].dtype))
    for name, factor in factors.items():
        out[name] = (out[name] * factor).astype(out[name].dtype)
    return out
```

```python
import math
from contextlib import ExitStack

import numpy as np

import concourse.bass as bass
from concourse import mybir

F32 = mybir.dt.float32
ACT = mybir.ActivationFunctionType
ALU = mybir.AluOpType
AX = mybir.AxisListType

T = 256
D = 1024
P = 128
KT = D // P
TT = T // P
W = 512
HD = 64
NH = W // HD
PAIRS = NH // 2
N_BR = 4
GROUPS = 2
D_FF = 2816
FF_TILES = D_FF // P
REL_BUCKETS, REL_EXACT, REL_MAX = 32, 16, 1024
SWA_WINDOW = 128
CONV1 = 4
CONV2 = 31
R_PAIRS = D // P
LEVELS = 7
NEG = -1e30
LOGIT = T + 1
SROW = P + 1 + LOGIT
DECAY = math.exp(-0.5)
MID = 0.5 * P * DECAY

Z0, X0, B0, C0 = 0, 512, 1024, 1280
DT0, BQ0, CQ0, F0, DQ0, DK0, DV0, G0 = 1536, 1544, 3080, 4616, 4624, 5136, 5264, 5392
VAL0, GATE0, OG0, TS0, ROG0, GC0, GR0 = 0, 1024, 2048, 3072, 6272, 7296, 8320

def columns(*fields):
    at, out = 0, {}
    for name, n in fields:
        out[name] = at
        at += n
    return out, at


PCOL, NPCOL = columns(("norm_mix", KT), ("norm_ffn", KT), ("norm_final", KT), ("norm_g", KT),
                      ("final_g", KT), ("conv_w", 8 * CONV1), ("conv_b", 8), ("d_skip", PAIRS),
                      ("ssm_norm", PAIRS), ("ada_b", 24), ("c", KT), ("conv_k", KT * CONV2),
                      ("conv_b2", KT), ("ln_g", KT), ("ln_b", KT), ("mu", 25), ("a0", KT), ("k_k", KT),
                      ("k_a", KT), ("r_k", KT), ("gn_g", KT), ("gn_b", KT))
RCOL, NRCOL = columns(("dt_bias", NH), ("forget_bias", NH), ("a_log", NH), ("sinks", NH))
CCOL, NCCOL = columns(("ident", P), ("flip", P), ("upper", P), ("ones", P), ("upper2", P),
                      ("strict", P), ("pair", P), ("pick", NH), ("mid", 2),
                      ("onehot", 3 * P), ("gmask", 3 * P), ("off_first", P), ("off", LEVELS * P))
NKEPT = CCOL["onehot"]
NFIRST = CCOL["off_first"]


def shape_constants():
    c = np.zeros((P, NCCOL), np.float32)
    r, q = np.arange(P)[:, None], np.arange(P)[None, :]

    def put(name, a):
        c[:a.shape[0], CCOL[name]:CCOL[name] + a.shape[1]] = a

    put("ident", r == q)
    put("flip", r == P - 1 - q)
    put("upper", r <= q)
    put("ones", np.ones((P, P)))
    put("upper2", r <= q)
    put("strict", r < q)
    put("pair", r // HD == q // HD)
    put("off_first", (r == q + 1) & (r % 2 == 1))
    for l in range(LEVELS):
        s = 1 << l
        c[:, CCOL["off"] + l * P:CCOL["off"] + (l + 1) * P] = \
            (r // (2 * s) == q // (2 * s)) & (r // s % 2 == 0) & (q // s % 2 == 1)
    dist = T - 1 - np.arange(3 * P)
    d = np.maximum(dist, 1).astype(np.float32)
    large = REL_EXACT + (np.log(d / np.float32(REL_EXACT)) / np.float32(math.log(REL_MAX / REL_EXACT))
                         * np.float32(REL_BUCKETS - REL_EXACT)).astype(np.int32)
    bucket = np.where(dist < REL_EXACT, np.maximum(dist, 0), np.minimum(large, REL_BUCKETS - 1))
    put("onehot", np.arange(REL_BUCKETS)[:, None] == bucket[None, :])
    gmask = np.zeros((2 * NH + 1, 3 * P))
    gmask[:, dist < 0] = NEG
    gmask[NH:2 * NH, dist >= SWA_WINDOW] = NEG
    put("gmask", gmask)
    put("pick", np.eye(40, NH) + np.eye(40, NH, -32))
    put("mid", np.tile(np.array([[-MID, MID]]), (P, 1)))
    return c


class Step:
    def __init__(self, phase, engine, index, emit, after, prev, sem):
        self.phase, self.engine, self.index, self.emit = phase, engine, index, emit
        self.after, self.prev, self.sem = after, prev, sem


class Phase:
    def __init__(self, name, trips):
        self.name, self.trips, self.steps, self.per, self.base = name, trips, [], {}, {}


class Program:
    ENGINES = ("pe", "act", "dve", "pool", "sp")
    START = 256

    def __init__(self, sems, new_sem):
        self.sems, self.new_sem, self.phases, self.named = sems, new_sem, [], {}

    def phase(self, name, trips=None):
        self.phases.append(Phase(name, trips))

    def add(self, engine, name, emit, after=(), prev=()):
        ph = self.phases[-1]
        after = (after,) if isinstance(after, str) else tuple(after)
        prev = (prev,) if isinstance(prev, str) else tuple(prev)
        ph.per[engine] = ph.per.get(engine, 0) + 1
        step = Step(ph, engine, ph.per[engine], emit, after, prev, self.sems[engine])
        assert name not in self.named, name
        self.named[name] = step
        ph.steps.append(step)

    def dma(self, name, emit, after=(), prev=(), engine="sp"):
        self.add(engine, name, emit, after, prev)
        ph = self.phases[-1]
        ph.per[engine] -= 1
        self.named[name].sem, self.named[name].index = self.new_sem("got_" + name.replace(".", "_")), None

    def run(self, engine, eng):
        sem = self.sems[engine]
        eng.sem_inc(sem, self.START)
        base = {e: self.START for e in self.ENGINES}
        for ph in self.phases:
            ph.base = dict(base)
            for e in self.ENGINES:
                base[e] += ph.per.get(e, 0) * (ph.trips or 1)
            steps = [s for s in ph.steps if s.engine == engine]
            if not steps:
                continue
            if ph.trips is None:
                self.emit(eng, steps, 0)
            else:
                with eng.Fori(0, ph.trips) as i:
                    self.emit(eng, steps, i)

    def emit(self, eng, steps, i):
        seen = {}
        for s in steps:
            if s.engine in ("act", "dve", "pool") and s.index is not None:
                ph, own = s.phase, s.engine
                eng.wait_ge(self.sems[own], i * ph.per[own] + (ph.base[own] + s.index - 1))
                seen[id(self.sems[own])] = (1, s.index - 1)
            for names, back in ((s.after, 0), (s.prev, 1)):
                for name in names:
                    t = self.named[name]
                    here = t.phase is s.phase
                    assert here or not back, name
                    count = t.index if t.index is not None else 16
                    per = t.phase.per.get(t.engine, 0) if t.index is not None else 16
                    base = t.phase.base[t.engine] if t.index is not None else 0
                    if here and t.phase.trips is not None:
                        rank = (1 - back, count)
                        value = i * per + (base + count - back * per)
                    else:
                        rank = (-1, base + count + ((t.phase.trips or 1) - 1) * per)
                        value = rank[1]
                    key = id(t.sem)
                    if seen.get(key, (-9, 0)) >= rank and not (rank[0] == -1 and seen[key][0] == 0):
                        continue
                    eng.wait_ge(t.sem, value)
                    seen[key] = max(seen.get(key, (-9, 0)), rank)
            last = s.emit(eng, i)
            last.then_inc(s.sem, 1 if s.index is not None else 16)


def build(nc, a, out):
    with ExitStack() as ctx:
        def sb(name, *shape):
            return ctx.enter_context(nc.sbuf_tensor(name, list(shape), F32))

        def sem(name):
            return ctx.enter_context(nc.semaphore(name))

        cst = sb("cst", P, NKEPT)
        par = sb("par", P, NPCOL)
        row = sb("row", 1, NRCOL)
        bank = [ctx.enter_context(nc.psum_tensor(f"bank{n}", [P, 512], F32)) for n in range(8)]
        N_SLOTS = 12
        slot = [sb(f"slot{n}", P, D) for n in range(N_SLOTS)]
        hT = sb("hT", P, KT, T)
        x = sb("x", P, TT, D)
        x3T = x[:, :, :].rearrange("p t d -> p (t d)").rearrange("p (k n) -> p k n", n=T)
        adaA = sb("adaA", P, 3 * D)
        stat = sb("stat", P, 64)

        def C(name, n=P, rows=P, off=0):
            return cst[0:rows, CCOL[name] + off:CCOL[name] + off + n]

        def PC(name, j=0):
            return par[:, PCOL[name] + j:PCOL[name] + j + 1]

        ident, flip, ones = C("ident"), C("flip"), C("ones")

        ARENA = 30800
        arena = sb("arena", P, ARENA)
        used = [0]

        def carve(*shape, rows=P):
            n = int(np.prod(shape))
            v = arena[0:rows, used[0]:used[0] + n]
            used[0] += n
            assert used[0] <= ARENA, used[0]
            if len(shape) == 2:
                v = v.rearrange("p (a b) -> p a b", a=shape[0])
            elif len(shape) == 3:
                v = v.rearrange("p (a b c) -> p a b c", a=shape[0], b=shape[1])
            return v

        p = Program({e: sem("steps_of_" + e) for e in Program.ENGINES}, sem)

        def view3(ap, n):
            return ap.rearrange("p (a b) -> p a b", b=n)

        freed = {}

        def load(name, n, src, after=(), prev=(), rows=P, width=D):
            p.dma(name, lambda e, i: e.dma_start(slot[n][0:rows, 0:width], src(i)),
                  after=tuple(after) + ((freed[n],) if n in freed else ()), prev=prev)

        def project(psum, w, rhs, kt=KT):
            def emit(e, i):
                for k in range(kt):
                    last = e.matmul(psum, w[:, k * P:(k + 1) * P], rhs[:, k, :], start=k == 0, stop=k == kt - 1)
                return last
            return emit

        def project_tokens(psum, w):
            def emit(e, i):
                for t in range(TT):
                    for k in range(KT):
                        last = e.matmul(psum[:, t * P:(t + 1) * P], hT[:, k, t * P:(t + 1) * P],
                                        w[:, k * P:(k + 1) * P], start=k == 0, stop=k == KT - 1)
                return last
            return emit

        def half(n):
            return bank[n][:, 0:T]

        def act(name, o, i_, f, after=(), prev=(), **kw):
            p.add("act", name, lambda e, i: e.activation(
                o(i) if callable(o) else o, i_(i) if callable(i_) else i_, f,
                **{k: v(i) if callable(v) else v for k, v in kw.items()}), after, prev)

        def on(v, i):
            return v(i) if callable(v) else v

        def copy(eng, name, o, i_, after=(), prev=()):
            p.add(eng, name, lambda e, i: e.tensor_copy(on(o, i), on(i_, i)), after, prev)

        def tt(name, o, x0, x1, op, after=(), prev=(), eng="dve"):
            p.add(eng, name, lambda e, i: e.tensor_tensor(on(o, i), on(x0, i), on(x1, i), op), after, prev)

        def ts(name, o, x0, s1, s2, op0, op1=None, after=(), prev=(), eng="dve"):
            p.add(eng, name, lambda e, i: e.tensor_scalar(on(o, i), on(x0, i), on(s1, i), on(s2, i), op0,
                                                          **({"op1": op1} if op1 is not None else {})), after, prev)

        def stt(name, o, x0, s, x1, op0, op1, after=(), prev=()):
            p.add("dve", name, lambda e, i: e.scalar_tensor_tensor(
                out=on(o, i), in0=on(x0, i), scalar=on(s, i), in1=on(x1, i), op0=op0, op1=op1), after, prev)

        def bc(ap, shape):
            return ap.to_broadcast(list(shape))

        p.phase("setup")
        p.dma("x", lambda e, i: e.dma_start(x[:, :, :], a["x"].rearrange("(t p) d -> p t d", p=P)))
        p.dma("cst", lambda e, i: e.dma_start(cst[:, :], a["cst"][:, 0:NKEPT]), engine="act")
        p.dma("par", lambda e, i: e.dma_start(par[:, :], a["par"]), engine="act")
        p.dma("row", lambda e, i: e.dma_start(row[:, :], a["row"]), engine="act")
        relb = sb("relb", REL_BUCKETS, 2 * NH + 1)
        p.add("pool", "relb.zero", lambda e, i: e.memset(relb[:, :], 0.0))
        p.dma("relb", lambda e, i: e.dma_start(relb[:, 0:2 * NH], a["rel_bias"]), after="relb.zero")
        p.add("pool", "ada.zero", lambda e, i: e.memset(adaA[:, :], 0.0))
        sc = sb("sc", P, KT)
        cT = par[:, PCOL["c"]:PCOL["c"] + KT]
        act("sc.tanh", sc[:, :], cT, ACT.Tanh, after=("par",), scale=0.5)
        stt("sc.x", sc[:, :], sc[:, :], 1.0, cT, ALU.add, ALU.mult, after=("sc.tanh",))
        ts("sc", sc[:, :], sc[:, :], 0.5, None, ALU.mult, after=("sc.x",))

        xn = arena[:, 8 * T:8 * T + TT * D].rearrange("p (t d) -> p t d", t=TT)

        def token_norm(tag, weight, target, after):
            ss, sd, rs = stat[:, 0:2], stat[:, 2:4], stat[:, 4:6]
            for t in range(TT):
                act(f"{tag}.sq{t}", xn[:, t, :], x[:, t, :], ACT.Square, after=after, accum_out=ss[:, t:t + 1])
            ts(f"{tag}.ms", sd, ss, 1.0 / D, 1e-6, ALU.mult, ALU.add, after=(f"{tag}.sq{TT - 1}",))
            act(f"{tag}.sd", sd, sd, ACT.Sqrt, after=(f"{tag}.ms",))
            p.add("dve", f"{tag}.rs", lambda e, i: e.reciprocal(rs, sd), after=(f"{tag}.sd",))
            for t in range(TT):
                ts(f"{tag}.xn{t}", xn[:, t, :], x[:, t, :], rs[:, t:t + 1], None, ALU.mult, after=(f"{tag}.rs",))
            for k in range(KT):
                def turn(e, i, k=k):
                    for t in range(TT):
                        last = e.transpose(half(k % 4)[:, t * P:(t + 1) * P], xn[:, t, k * P:(k + 1) * P], ident)
                    return last
                p.add("pe", f"{tag}.turn{k}", turn, after=(f"{tag}.xn1", "cst") + ((f"{tag}.h{k - 4}",) if k >= 4 else ()))
                ts(f"{tag}.h{k}", target[:, k, :], half(k % 4), PC(weight, k), None, ALU.mult,
                   after=(f"{tag}.turn{k}", "par"))

        token_norm("norm1", "norm_mix", hT, after=("x",))

        p.phase("pre")
        padA = sb("padA", P, 30 + T)
        pad1 = padA[:, 0:CONV1 - 1 + T]
        conv = sb("conv", P, T)
        th = sb("th", P, T)
        gates = carve(N_BR * KT, T)
        YT = [carve(W // P, T) for _ in range(N_BR)]
        Hk = carve(2 * NH + 1, LOGIT)
        CBT = carve(PAIRS, 3 * P)
        BCT = gates[:, 0:4, :]
        dk = carve(PAIRS, T)
        dv = carve(PAIRS, TT, HD)
        dtc = carve(TT, NH)
        acum = carve(TT, NH)
        acumT = carve(T)
        fcumT = carve(T)
        cwh = carve(8 * CONV1 + 8)
        wsm = carve(KT, 2 * NH)
        lf, rf = carve(T), carve(T)
        block1_end = used[0]
        LF = carve(TT, 40)
        LA = carve(TT, NH)
        sp = [carve(TT, 2 * NH) for _ in range(6)]
        expA = carve(NH)
        gsb = carve(3 * P)
        cst1 = carve(NFIRST - NKEPT)
        onehot, gmask = cst1[0:REL_BUCKETS, 0:3 * P], cst1[0:2 * NH + 1, 3 * P:6 * P]
        p.dma("cst1", lambda e, i: e.dma_start(cst1, a["cst"][:, NKEPT:NFIRST]), engine="act")

        p.dma("wsm", lambda e, i: e.dma_start(wsm.rearrange("p a b -> p (a b)"), a["w_small"]))
        for n in range(7):
            load(f"pre.w{n}", n, lambda i, n=n: a["w_pre"][n, :, :])
        ts("cwh", cwh, par[:, PCOL["conv_w"]:PCOL["conv_w"] + 40], 0.5, None, ALU.mult, after=("par",))
        p.add("pool", "padA.zero", lambda e, i: e.memset(padA[:, :], 0.0))
        p.add("pool", "fcumT.zero", lambda e, i: e.memset(fcumT, 0.0))
        p.add("pool", "lf.zero", lambda e, i: e.memset(lf, 0.0))
        p.add("pool", "rf.zero", lambda e, i: e.memset(rf, 0.0))
        p.add("pool", "lf.ones", lambda e, i: e.memset(lf[0:NH, :], 1.0), after=("rf.zero",))
        p.add("pool", "rf.ones", lambda e, i: e.memset(rf[32:40, :], 1.0))
        p.add("pool", "LF.zero", lambda e, i: e.memset(LF, 0.0))

        p.add("pe", "g.mm", lambda e, i: e.matmul(bank[7][0:2 * NH + 1, 0:3 * P], relb[:, :],
              onehot, start=True, stop=True), after=("relb", "cst1"))
        tt("g.mask", gsb[0:2 * NH + 1, :], bank[7][0:2 * NH + 1, 0:3 * P], gmask, ALU.add,
           after=("g.mm",))
        g_dram = nc.dram_tensor("g_scratch", [2 * NH + 1, 3 * P], F32, kind="Internal")
        p.dma("g.out", lambda e, i: e.dma_start(g_dram.ap(), gsb[0:2 * NH + 1, :]), after=("g.mask",))
        shifted = bass.AP(g_dram, 0, [[1, P], [3 * P, 2 * NH + 1], [1, T]])
        p.dma("g.in", lambda e, i: e.dma_start(Hk[:, :, 0:T], shifted), after=("g.out",))
        p.add("dve", "sink.none", lambda e, i: e.memset(Hk[:, :, T:LOGIT], NEG))
        p.add("pe", "sink.mm", lambda e, i: e.matmul(bank[7][:, 0:NH], ones[0:1, :],
              row[0:1, RCOL["sinks"]:RCOL["sinks"] + NH], start=True, stop=True), after=("row", "g.mask"))
        copy("dve", "sink", Hk[:, NH:2 * NH, T:LOGIT], bank[7][:, 0:NH].unsqueeze(2), after=("sink.mm", "sink.none"))

        def small(e, i):
            for t in range(TT):
                e.matmul(bank[6][:, t * 16:(t + 1) * 16], ones[0:1, :], row[0:1, 0:2 * NH], start=True, stop=False)
                for k in range(KT):
                    last = e.matmul(bank[6][:, t * 16:(t + 1) * 16], hT[:, k, t * P:(t + 1) * P], wsm[:, k, :],
                                    start=False, stop=k == KT - 1)
            return last
        p.add("pe", "small", small, after=("wsm", "row", "norm1.h7"))
        rowA = row[0:1, RCOL["a_log"]:RCOL["a_log"] + NH]
        act("expA.row", rowA, rowA, ACT.Exp, after=("row",))
        p.add("pe", "expA.mm", lambda e, i: e.matmul(bank[6][:, 64:64 + NH], ones[0:1, :], rowA, start=True, stop=True),
              after=("expA.row",))
        v, nb, u, w1, d1, soft = sp
        ps_small = view3(bank[6][:, 0:32], 16)
        copy("dve", "expA", expA, bank[6][:, 64:64 + NH], after=("expA.mm",))
        copy("dve", "sp.v0", v[:, :, 0:NH], ps_small[:, :, 0:NH], after=("small",))
        ts("sp.v1", v[:, :, NH:], ps_small[:, :, NH:], -1.0, None, ALU.mult)
        stt("sp.nb", nb, v, -1.0, v, ALU.mult, ALU.min, after=("sp.v1",))
        act("sp.u", u, nb, ACT.Exp, after=("sp.nb",))
        ts("sp.w1", w1, u, 1.0, None, ALU.add, after=("sp.u",))
        act("sp.ln", soft, w1, ACT.Ln, after=("sp.w1",))
        ts("sp.d1", d1, w1, -1.0, 1e-30, ALU.add, ALU.max, after=("sp.w1",))
        p.add("dve", "sp.rd", lambda e, i: e.reciprocal(d1, d1), after=("sp.d1",))
        tt("sp.lnu", soft, soft, u, ALU.mult, after=("sp.ln",))
        tt("sp.lnr", soft, soft, d1, ALU.mult, after=("sp.lnu", "sp.rd"))
        stt("sp.tiny", u, w1, 1.0, u, ALU.is_equal, ALU.mult, after=("sp.lnr",))
        tt("sp.log1p", soft, soft, u, ALU.add, after=("sp.tiny",))
        stt("sp.soft", soft, v, 0.0, soft, ALU.max, ALU.add, after=("sp.log1p",))
        copy("dve", "dt", dtc, soft[:, :, 0:NH], after=("sp.soft",))
        stt("LA", LA, soft[:, :, 0:NH], -1.0, bc(expA.unsqueeze(1), (P, TT, NH)), ALU.mult, ALU.mult,
            after=("sp.soft", "expA"))
        copy("dve", "LF0", LF[:, :, 0:NH], soft[:, :, NH:], after=("LF.zero", "sp.soft"))
        ts("LF1", LF[:, :, 32:40], soft[:, :, NH:], -1.0, None, ALU.mult)

        def cumulate(e, i):
            up, up1 = C("upper"), C("upper", 2 * P)
            e.matmul(bank[5][:, 0:NH], up, LA[:, 0, :], start=True, stop=True)
            e.matmul(bank[5][:, NH:2 * NH], ones, LA[:, 0, :], start=True, stop=False)
            e.matmul(bank[5][:, NH:2 * NH], up, LA[:, 1, :], start=False, stop=True)
            e.matmul(bank[5][0:NH, 256:512], LA[:, 0, :], up1, start=True, stop=False)
            e.matmul(bank[5][0:NH, 384:512], LA[:, 1, :], up, start=False, stop=True)
            e.matmul(bank[6][0:40, 256:512], LF[:, 0, :], up1, start=True, stop=False)
            return e.matmul(bank[6][0:40, 384:512], LF[:, 1, :], up, start=False, stop=True)
        p.add("pe", "cum", cumulate, after=("LA", "LF1"))
        copy("dve", "acum", acum, view3(bank[5][:, 0:2 * NH], NH), after=("cum",))
        copy("dve", "acumT", acumT[0:NH, :], bank[5][0:NH, 256:512])
        copy("dve", "fcumT", fcumT[0:40, :], bank[6][0:40, 256:512], after=("fcumT.zero",))

        def conv_tile(tag, tile, evac_after, target, wcol, eng_after=()):
            ts(f"{tag}.tap0", conv[:, :], pad1[:, 0:T], lambda i: cwh[:, wcol(i, 0)], lambda i: cwh[:, wcol(i, None)], ALU.mult, ALU.add, after=evac_after + ("cwh",))
            for j in range(1, CONV1):
                stt(f"{tag}.tap{j}", conv[:, :], pad1[:, j:j + T],
                    lambda i, j=j: cwh[:, wcol(i, j)], conv[:, :], ALU.mult, ALU.add,
                    after=(f"{tag}.tap{j - 1}",))
            act(f"{tag}.tanh", th[:, :], conv[:, :], ACT.Tanh, after=(f"{tag}.tap{CONV1 - 1}",))
            stt(f"{tag}.silu", target, th[:, :], 1.0, conv[:, :], ALU.add, ALU.mult, after=(f"{tag}.tanh",))

        last = None
        for n in range(4):
            p.add("pe", f"bc{n}", project(half(n), slot[n], hT), after=(f"pre.w{n}", "norm1.h7"))
        for n in range(4):
            act(f"bc{n}.pad", pad1[:, CONV1 - 1:], half(n), ACT.Copy,
                after=(f"bc{n}", "padA.zero") + ((f"bc{n - 1}.tap3",) if n else ()))
            conv_tile(f"bc{n}", n, (f"bc{n}.pad",), BCT[:, n, :],
                      lambda i, j, n=n: bass.ds(8 * CONV1 + 4 + n if j is None else (4 + n) * CONV1 + j, 1))
        for g in range(GROUPS):
            p.add("pe", f"dk{g}", project(half(4), slot[4 + g], hT),
                  after=(f"pre.w{4 + g}",) + (("dk01",) if g else ()))
            for n in range(2):
                act(f"dk{g}{n}", dk[:, 2 * g + n, :], half(4), ACT.Copy, after=(f"dk{g}",))
        p.add("pe", "dv", project_tokens(half(0), slot[6]), after=("pre.w6", "bc0.pad"))
        for n in range(PAIRS):
            act(f"dv{n}", dv[:, n, :, :], view3(half(0), P)[:, :, n // 2 * HD:n // 2 * HD + HD], ACT.Copy, after=("dv",))
        for g in range(GROUPS):
            cb = bank[1 + g][:, 0:3 * P]

            def cb_mm(e, i, g=g, cb=cb):
                e.matmul(cb[:, 0:T], BCT[:, g, 0:P], BCT[:, 2 + g, :], start=True, stop=True)
                return e.matmul(cb[:, T:], BCT[:, g, P:T], BCT[:, 2 + g, P:T], start=True, stop=True)
            p.add("pe", f"cb{g}", cb_mm, after=("bc3.silu",))
            for n in range(2):
                tt(f"cbt{g}{n}", CBT[:, 2 * g + n, :], cb, C("upper", 3 * P), ALU.mult, after=(f"cb{g}",))
        for n in range(4):
            freed[n] = f"bc{n}"
        freed[4], freed[5], freed[6] = "dk0", "dk1", "dv"
        pre_steps = ("bc3.silu", "fcumT", "dv3", "cbt11", "g.in", "sink")

        p.phase("heads", PAIRS)
        used[0] = block1_end
        qs = {b: carve(T) for b in "bcd"}
        ks = {b: carve(T) for b in "bcd"}
        vs = {b: carve(TT, P) for b in "bc"}
        vd = carve(TT, HD)
        am = carve(T)
        Pr = carve(3, SROW)
        PT = [carve(3 * P) for _ in range(3)]
        mx = carve(6)
        sm = carve(6)
        xsT = carve(T)
        xdt = carve(TT, P)
        zs = carve(T)
        zt = carve(T)
        dec = carve(3 * P)
        MT1 = carve(3 * P)
        yx = carve(T)
        adaW = [carve(D) for _ in range(2)]
        heads_end = used[0]

        NW = 17
        BQ, BK, BV, CQ, CK, CV, DQ, XS, ZS = range(9)
        ORDER = (BQ, BK, CQ, CK, DQ, BV, CV, XS, ZS)
        for n in ORDER:
            load(f"w{n}", n, lambda i, n=n: a["w_heads"][i * NW + n, :, :], prev=(f"proj{n}",))

        last_gate = {0: 6, 1: 7, 2: 5}

        def load_gate(j):
            s = 9 + j % 3
            load(f"w{9 + j}", s, lambda i: a["w_heads"][i * NW + (9 + j), :, :],
                 after=(f"proj{9 + j - 3}",) if j >= 3 else (), prev=() if j >= 3 else (f"proj{9 + last_gate[j]}",))
        for j in range(4):
            load_gate(j)
        def load_ada(n):
            p.dma(f"adaw{n}", lambda e, i: e.dma_start(adaW[n % 2], a["ada_w"][i * 6 + n, :, :]),
                  after=(f"ada{n - 2}",) if n >= 2 else (), prev=() if n >= 2 else (f"ada{n + 4}",))
        for n in range(3):
            load_ada(n)
        for j in range(4, 8):
            load_gate(j)
        for n in range(3, 6):
            load_ada(n)

        halves = {}
        count = [0]

        def proj(n, evac, token=False):
            h = count[0] % 2
            count[0] += 1
            s = n if n < 9 else 9 + (n - 9) % 3
            waits = (f"w{n}",) + ((halves[h],) if h in halves else pre_steps)
            p.add("pe", f"proj{n}", project_tokens(half(h), slot[s]) if token else project(half(h), slot[s], hT),
                  after=waits, prev=(last_halves[h],) if h not in halves else ())
            halves[h] = evac
            return half(h)

        last_halves = {0: "gate7", 1: "gate6"}

        def gate(j):
            o = proj(9 + j, f"gate{j}")
            act(f"gate{j}", lambda i: gates[:, bass.ds(i * 8 + j, 1), :], o.unsqueeze(1), ACT.Tanh,
                after=(f"proj{9 + j}",), scale=0.5)

        for b, q, k in (("b", BQ, BK), ("c", CQ, CK)):
            oq = proj(q, f"q{b}")
            act(f"q{b}", qs[b], oq, ACT.Copy, after=(f"proj{q}",), scale=HD ** -0.5)
            ok = proj(k, f"k{b}")
            copy("dve", f"k{b}", ks[b], ok, after=(f"proj{k}",))
        oq = proj(DQ, "qd")
        act("qd", qs["d"], oq, ACT.Copy, after=(f"proj{DQ}",), scale=HD ** -0.5)
        copy("pool", "kd", ks["d"], lambda i: dk[:, bass.ds(i, 1), :].rearrange("p a n -> p (a n)"), prev=("s.d1",),
             after=pre_steps)
        copy("pool", "vd", vd, lambda i: dv[:, bass.ds(i, 1), :, :].rearrange("p a b c -> p (a b) c"), prev=("pv.d1",))
        ov = proj(BV, "vb", token=True)
        copy("dve", "vb", vs["b"], view3(ov, P), after=(f"proj{BV}",))
        ov = proj(CV, "vc", token=True)
        copy("dve", "vc", vs["c"], view3(ov, P), after=(f"proj{CV}",))

        S = {b: bank[2 + n] for n, b in enumerate("bcd")}

        def forget(hh):
            last = (f"s.c{hh - 1}",) if hh else ()
            ts(f"rf{hh}", rf[0:NH, :], fcumT[0:NH, :],
               lambda i: cst[0:NH, bass.ds(i * 2 + (CCOL["pick"] + hh), 1)], None, ALU.mult,
               after=last + ("rf.ones", "lf.ones", "fcumT"), prev=() if hh else ("s.c1",))
            ts(f"lf{hh}", lf[32:40, :], fcumT[32:40, :],
               lambda i: cst[32:40, bass.ds(i * 2 + (CCOL["pick"] + hh), 1)], None, ALU.mult)

        def scores(b, hh):
            lo = hh * HD
            q, k, o = qs[b], ks[b], S[b]

            def emit(e, i):
                r = {"b": i * 2 + hh, "c": 2 * NH, "d": i * 2 + (NH + hh)}[b]
                for t in range(TT):
                    at, n = (0, P) if t == 0 else (P + 1, T)
                    if b == "c":
                        bias = Hk[:, r, T - n:LOGIT]
                    else:
                        bias = Hk[:, bass.ds(r, 1), T - n:LOGIT].rearrange("p a n -> p (a n)")
                    e.matmul(o[:, at:at + n + 1], flip, bias, start=True, stop=False)
                    if b == "c":
                        e.matmul(o[:, at:at + n], lf[:, t * P:(t + 1) * P], rf[:, 0:n], start=False, stop=False)
                    last = e.matmul(o[:, at:at + n], q[lo:lo + HD, t * P:(t + 1) * P], k[lo:lo + HD, 0:n],
                                    start=False, stop=True)
                return last
            ready = {"b": ("qb", "kb"), "c": ("qc", "kc", f"lf{hh}"), "d": ("qd", "kd")}[b]
            free = (f"e.{b}0.1",) if hh else ()
            p.add("pe", f"s.{b}{hh}", emit, after=ready + free + pre_steps, prev=() if hh else (f"e.{b}1.1", "y.ssd"))

        def softmax(hh):
            for n, b in enumerate("bcd"):
                for t in range(TT):
                    cols = S[b][:, 0:P + 1] if t == 0 else S[b][:, P + 1:SROW]
                    p.add("dve", f"mx.{b}{hh}{t}", lambda e, i, n=n, t=t, cols=cols: e.tensor_reduce(
                        mx[:, 2 * n + t:2 * n + t + 1], cols, AX.X, ALU.max, negate=True),
                        after=(f"s.{b}{hh}",) + ((f"e.{b}0.{t}",) if hh else ()), prev=() if hh else (f"e.{b}1.{t}",))
            for n, b in enumerate("bcd"):
                for t in range(TT):
                    cols = slice(0, P + 1) if t == 0 else slice(P + 1, SROW)
                    act(f"e.{b}{hh}.{t}", Pr[:, n, cols], S[b][:, cols], ACT.Exp,
                        after=(f"mx.{b}{hh}1",) + ((f"t.{b}0",) if hh else ()), prev=() if hh else (f"t.{b}1",),
                        bias=mx[:, 2 * n + t:2 * n + t + 1], accum_out=sm[:, 2 * n + t:2 * n + t + 1])
                p.add("dve", f"r.{b}{hh}", lambda e, i, n=n: e.reciprocal(sm[:, 2 * n:2 * n + 2], sm[:, 2 * n:2 * n + 2]),
                      after=(f"e.{b}{hh}.1",))
                for t in range(TT):
                    at, m = (0, P) if t == 0 else (P + 1, T)
                    ts(f"p.{b}{hh}.{t}", Pr[:, n, at:at + m], Pr[:, n, at:at + m], sm[:, 2 * n + t:2 * n + t + 1],
                       None, ALU.mult, after=(f"r.{b}{hh}",))

        def turn_p(hh):
            for n, b in enumerate("bcd"):
                tb = bank[5 + n % 2]

                def emit(e, i, n=n, tb=tb):
                    e.transpose(tb[:, 0:P], Pr[:, n, 0:P], ident)
                    e.transpose(tb[:, P:T], Pr[:, n, P + 1:T + 1], ident)
                    return e.transpose(tb[:, T:3 * P], Pr[:, n, T + 1:SROW - 1], ident)
                before = {0: ("pt.d0", "yt.c0") if hh else (), 1: ("pt.c0", "yt.d0") if hh else (), 2: (f"pt.b{hh}",)}[n]
                back = {0: () if hh else ("pt.d1", "yt.c1"), 1: () if hh else ("pt.c1", "yt.d1"), 2: ()}[n]
                p.add("pe", f"t.{b}{hh}", emit, after=(f"p.{b}{hh}.1",) + before, prev=back)
                o = PT[n]
                if b == "c":
                    copy("dve", f"pt.{b}{hh}", o, tb[:, 0:3 * P], after=(f"t.{b}{hh}",) + ((f"pv.{b}0",) if hh else ()),
                         prev=() if hh else (f"pv.{b}1",))
                else:
                    act(f"pt.{b}{hh}", o, tb[:, 0:3 * P], ACT.Copy, after=(f"t.{b}{hh}",) + ((f"pv.{b}0",) if hh else ()),
                        prev=() if hh else (f"pv.{b}1",))

        O = {"b": bank[7][:, 0:T], "c": bank[5][:, 0:T], "d": bank[6][:, 0:T]}

        def weigh(hh):
            lo = hh * HD
            for n, b in enumerate("bcd"):
                def emit(e, i, n=n, b=b):
                    v0, v1 = (vd[:, 0, :], vd[:, 1, :]) if b == "d" else \
                        (vs[b][:, 0, lo:lo + HD], vs[b][:, 1, lo:lo + HD])
                    e.matmul(O[b][lo:lo + HD, :], v0, PT[n][:, 0:T], start=True, stop=False)
                    return e.matmul(O[b][lo:lo + HD, P:T], v1, PT[n][:, T:3 * P], start=False, stop=True)
                ready = {"b": ("vb",), "c": ("vc", f"pt.d{hh}"), "d": ("vd", f"pt.c{hh}")}[b]
                p.add("pe", f"pv.{b}{hh}", emit, after=(f"pt.{b}{hh}",) + ready, prev=(f"yt.{b}1",) if hh == 0 else ())
                act(f"yt.{b}{hh}", lambda i, n=n: YT[1 + n][lo:lo + HD, bass.ds(i, 1), :], O[b][lo:lo + HD, :].unsqueeze(1),
                    ACT.Copy, after=(f"pv.{b}{hh}",), scale=0.5)

        def ada(n):
            third = adaA[:, n % 3 * D:(n % 3 + 1) * D]
            stt(f"ada{n}", third, adaW[n % 2], lambda i: sc[:, bass.ds(i * 2 + n // 3, 1)], third, ALU.mult, ALU.add,
                after=(f"adaw{n}", "sc", "ada.zero"))

        forget(0)
        for b in "bcd":
            scores(b, 0)
        softmax(0)
        ox = proj(XS, "xpad")
        act("xpad", pad1[:, CONV1 - 1:], ox, ACT.Copy, after=(f"proj{XS}", "bc3.silu"), prev=("xs.tap3",))
        conv_tile("xs", 0, ("xpad",), xsT,
                  lambda i, j: bass.ds(i + 8 * CONV1, 1) if j is None else bass.ds(i * CONV1 + j, 1))
        oz = proj(ZS, "zs")
        act("zt", zt, oz, ACT.Tanh, after=(f"proj{ZS}",), prev=("zs",), scale=0.5)
        stt("zs", zs, zt, 1.0, oz, ALU.add, ALU.mult, after=("zt",))
        gate(0)
        gate(1)
        turn_p(0)
        forget(1)
        for b in "bcd":
            scores(b, 1)
        softmax(1)
        gate(2)
        ada(0)
        ada(1)
        weigh(0)
        gate(3)
        turn_p(1)
        gate(4)
        ada(2)
        ada(3)
        weigh(1)

        def turn_x(e, i):
            e.transpose(bank[2][:, 0:P], xsT[:, 0:P], ident)
            return e.transpose(bank[2][:, P:T], xsT[:, P:T], ident)
        p.add("pe", "turn.x", turn_x, after=("xs.silu", "e.b1.1"))
        for hh in range(2):
            for t in range(TT):
                ts(f"xdt{hh}{t}", xdt[:, t, hh * HD:hh * HD + HD], bank[2][:, t * P + hh * HD:t * P + hh * HD + HD],
                   lambda i, hh=hh, t=t: dtc[:, t, bass.ds(i * 2 + hh, 1)], None, ALU.mult, after=("turn.x",))
        gate(5)
        for hh in range(2):
            lo = hh * HD
            ts(f"am{hh}", am[0:NH, :], acumT[0:NH, :], lambda i, hh=hh: cst[0:NH, bass.ds(i * 2 + (CCOL["pick"] + hh), 1)],
               None, ALU.mult, after=("rowb0",) if hh else (), prev=() if hh else ("rowb1",))
            rb = bank[3][:, 0:T]
            p.add("pe", f"rowb{hh}", lambda e, i, rb=rb: e.matmul(rb, ones[0:NH, :], am[0:NH, :], start=True, stop=True),
                  after=(f"am{hh}", "e.c1.1") + (("d1.0",) if hh else ()))
            for t, (at, n) in enumerate(((0, T), (T, P))):
                ts(f"d{t}.{hh}", dec[:, at:at + n], rb[:, T - n:T], lambda i, hh=hh, t=t: acum[:, t, bass.ds(i * 2 + hh, 1)],
                   0.0, ALU.subtract, ALU.min, after=(f"rowb{hh}",) + (("m0",) if hh else ()))
            act(f"dexp{hh}", dec, dec, ACT.Exp, after=(f"d1.{hh}",))
            tt(f"m{hh}", MT1, dec, lambda i: CBT[:, bass.ds(i, 1), :].rearrange("p a n -> p (a n)"), ALU.mult,
               after=(f"dexp{hh}",) + (("y0",) if hh else ()))
            if hh == 0:
                gate(6)
            else:
                gate(7)

            def y_mm(e, i, lo=lo):
                o = bank[4][lo:lo + HD, 0:T]
                e.matmul(o, xdt[:, 0, lo:lo + HD], MT1[:, 0:T], start=True, stop=False)
                return e.matmul(o[:, P:T], xdt[:, 1, lo:lo + HD], MT1[:, T:3 * P], start=False, stop=True)
            p.add("pe", f"y{hh}", y_mm, after=(f"m{hh}", "xdt11", "e.d1.1"))
        ada(4)
        ada(5)
        stt("yx", yx, xsT, lambda i: par[:, bass.ds(i + PCOL["d_skip"], 1)], bank[4][:, 0:T], ALU.mult, ALU.add, after=("y1",))
        tt("y.ssd", lambda i: YT[0][:, bass.ds(i, 1), :], yx.unsqueeze(1), zs.unsqueeze(1), ALU.mult, after=("yx", "zs"))

        freed.update({n: f"proj{n}" for n in range(9)})
        freed.update({9 + n: f"proj{9 + last_gate[n]}" for n in range(3)})

        p.phase("ssd norm")
        used[0] = block1_end
        sqs = carve(W // P, T)
        rsb = carve(T)
        tt("ya.sq", sqs, YT[0], YT[0], ALU.mult, after=("y.ssd", "pv.d1"))

        def mean_mm(e, i, psum=bank[0][:, 0:T], src=sqs, n=W // P, w=None):
            for k in range(n):
                last = e.matmul(psum, w if w is not None else ones, src[:, k, :], start=k == 0, stop=k == n - 1)
            return last
        p.add("pe", "ya.sum", mean_mm, after=("ya.sq", "gate7"))
        ts("ya.ms", rsb, bank[0][:, 0:T], 1.0 / W, 4e-6, ALU.mult, ALU.add, after=("ya.sum",))
        act("ya.sd", rsb, rsb, ACT.Sqrt, after=("ya.ms",))
        p.add("dve", "ya.rs", lambda e, i: e.reciprocal(rsb, rsb), after=("ya.sd",))
        ts("ya.half", rsb, rsb, 0.5, None, ALU.mult, after=("ya.rs",))
        for k in range(W // P):
            stt(f"ya.y{k}", YT[0][:, k, :], YT[0][:, k, :], PC("ssm_norm", k), rsb, ALU.mult, ALU.mult, after=("ya.half",))

        p.phase("mix", KT)
        mixT = carve(KT, T)
        tb = [carve(T) for _ in range(N_BR)]
        for s in range(4):
            load(f"wb{s}", s, lambda i, s=s: a["w_br"][i * 4 + s, :, :], prev=(f"br{s}",), width=W)
        for b in range(N_BR):
            p.add("pe", f"br{b}", project(half(b), slot[b][:, 0:W], YT[b], kt=W // P), after=(f"wb{b}", "ya.y3", "yt.d1"),
                  prev=(f"br{b}.gate",))
            stt(f"br{b}.gate", tb[b].unsqueeze(1), lambda i, b=b: gates[:, bass.ds(i + b * KT, 1), :], 1.0,
                half(b).unsqueeze(1), ALU.add, ALU.mult, after=(f"br{b}",), prev=("mix",) if b == 0 else ())
        tt("mix01", tb[0], tb[0], tb[1], ALU.add, after=("br1.gate",), eng="pool")
        tt("mix23", tb[2], tb[2], tb[3], ALU.add, after=("br3.gate",), eng="pool")
        tt("mix", lambda i: mixT[:, bass.ds(i, 1), :], tb[0].unsqueeze(1), tb[2].unsqueeze(1), ALU.add, after=("mix23",),
           eng="pool")
        freed.update({s: f"br{s}" for s in range(4)})

        p.phase("w_out")
        quarter = [(t, h) for t in range(TT) for h in range(2)]

        def residual(name, after, banks):
            def emit(e, i):
                for n, (t, h) in enumerate(quarter):
                    last = e.matmul(banks[n][:, :], ident, x[:, t, h * 512:(h + 1) * 512], start=True, stop=False)
                return last
            p.add("pe", name, emit, after=after)

        def rows_times(w, lhs, banks, stop):
            def emit(e, i):
                for n, (t, h) in enumerate(quarter):
                    last = e.matmul(banks[n][:, :], lhs[:, t * P:(t + 1) * P], w[:, h * 512:(h + 1) * 512],
                                    start=False, stop=stop)
                return last
            return emit
        residual("x.in", ("mix",), bank[4:8])
        for k in range(KT):
            s = 4 + k
            load(f"wo{k}", s, lambda i, k=k: a["w_out"][k * P:(k + 1) * P, :])
            p.add("pe", f"out{k}", rows_times(slot[s], mixT[:, k, :], bank[4:8], k == KT - 1), after=(f"wo{k}",))
            freed[s] = f"out{k}"
        for n, (t, h) in enumerate(quarter):
            o = x[:, t, h * 512:(h + 1) * 512]
            if n % 2:
                act(f"x1.{n}", o, bank[4 + n][:, :], ACT.Copy, after=("out7",))
            else:
                copy("dve", f"x1.{n}", o, bank[4 + n][:, :], after=("out7",))

        p.phase("ffn norm")
        token_norm("norm2", "norm_ffn", hT, after=("x1.2", "x1.3"))
        residual("x1.in", ("x1.2", "x1.3"), bank[4:8])
        FF_STEP = 2
        FF_TRIPS = FF_TILES // FF_STEP
        ud = [carve(T) for _ in range(FF_STEP)]
        gu = [carve(T) for _ in range(FF_STEP)]
        tg = [carve(T) for _ in range(FF_STEP)]

        def ffn(z, peeled):
            at = (lambda i: FF_TRIPS - 1) if peeled else (lambda i: i)
            back = (lambda *names: ()) if peeled else (lambda *names: names)
            for f in range(FF_STEP):
                for n, what in enumerate(("g", "u")):
                    load(f"w{what}{f}{z}", 3 * f + n, lambda i, f=f, n=n: a["w_gu"][at(i) * 2 * FF_STEP + (2 * f + n), :, :],
                         prev=back(f"{what}{f}{z}"))
                load(f"wd{f}{z}", 3 * f + 2, lambda i, f=f: a["w_down"][bass.ds(at(i) * FF_STEP * P + f * P, P), :],
                     prev=back(f"down{f}{z}"))
            for f in range(FF_STEP):
                for n, what in enumerate(("g", "u")):
                    free = "tg2." if what == "g" else "ud"
                    p.add("pe", f"{what}{f}{z}", project(half(2 * f + n), slot[3 * f + n], hT),
                          after=(f"w{what}{f}{z}", "norm2.h7") + ((f"{free}{f}",) if peeled else ()),
                          prev=back(f"{free}{f}{z}"))
                act(f"tg{f}{z}", tg[f], half(2 * f), ACT.Tanh, after=(f"g{f}{z}",), prev=back(f"tg2.{f}{z}"), scale=0.5)
                act(f"ud{f}{z}", ud[f], half(2 * f + 1), ACT.Copy, after=(f"u{f}{z}",) + ((f"gu{f}",) if peeled else ()),
                    prev=back(f"gu{f}{z}"), scale=0.5)
                stt(f"tg2.{f}{z}", tg[f], tg[f], 1.0, half(2 * f), ALU.add, ALU.mult, after=(f"tg{f}{z}",))
                tt(f"gu{f}{z}", gu[f], tg[f], ud[f], ALU.mult, after=(f"tg2.{f}{z}", f"ud{f}{z}") + ((f"down{f}",) if peeled else ()),
                   prev=back(f"down{f}{z}"))
            for f in range(FF_STEP):
                p.add("pe", f"down{f}{z}", rows_times(slot[3 * f + 2], gu[f], bank[4:8], peeled and f == FF_STEP - 1),
                      after=(f"wd{f}{z}", f"gu{f}{z}"))
                freed[3 * f], freed[3 * f + 1], freed[3 * f + 2] = f"g{f}{z}", f"u{f}{z}", f"down{f}{z}"
        p.phase("ffn", FF_TRIPS - 1)
        ffn("", False)
        p.phase("ffn end")
        ffn(".end", True)
        p.phase("x2")
        for n, (t, h) in enumerate(quarter):
            o = x[:, t, h * 512:(h + 1) * 512]
            if n % 2:
                act(f"x2.{n}", o, bank[4 + n][:, :], ACT.Copy, after=("down1.end",))
            else:
                copy("dve", f"x2.{n}", o, bank[4 + n][:, :], after=("down1.end",))

        p.phase("block 2 norm")
        used[0] = 0
        YR, CU, OG, GC, GR = (carve(KT, T) for _ in range(5))
        TW, AL = carve(T), carve(T)
        mod = carve(24)
        gs = carve(KT)
        a0h, oka = carve(KT), carve(KT)
        rsc = carve(T)
        w0 = carve(D)
        cst2 = carve(NCCOL - NFIRST)
        padz = carve(1 + T)
        squares = OG
        low = carve(T)
        pads = {n: carve(1 + T) for n in ("r", "k", "v")}
        Az = [carve(T) for _ in range(2)]
        Rz = [carve(T) for _ in range(2)]
        block2_end = used[0]
        p.dma("cst2", lambda e, i: e.dma_start(cst2, a["cst"][:, NFIRST:NCCOL]), after=("x2.2", "x2.3"))
        p.dma("w0row", lambda e, i: e.dma_start(w0[0:1, :], a["w0"]), after=("x2.2", "x2.3"))
        load("wlora", 0, lambda i: a["w_lora"])
        token_norm("norm3", "norm_final", x3T, after=("x2.2", "x2.3"))

        def ada_mm(e, i):
            for j in range(24):
                last = e.matmul(bank[4][:, j:j + 1], adaA[:, j * P:(j + 1) * P], ones[:, 0:1], start=True, stop=True)
            return last
        p.add("pe", "mod.mm", ada_mm, after=("ada5", "x2.2", "x2.3"))
        tt("mod", mod, bank[4][:, 0:24], par[:, PCOL["ada_b"]:PCOL["ada_b"] + 24], ALU.add, after=("mod.mm", "norm3.h7"))
        stt("gs", gs, mod[:, KT:2 * KT], 1.0, par[:, PCOL["norm_g"]:PCOL["norm_g"] + KT], ALU.add, ALU.mult)
        ts("a0h", a0h, par[:, PCOL["a0"]:PCOL["a0"] + KT], 0.5, None, ALU.mult)
        ts("oka", oka, par[:, PCOL["k_a"]:PCOL["k_a"] + KT], -1.0, 1.0, ALU.mult, ALU.add)

        def mean_over_channels(tag, src, b, after):
            def emit(e, i):
                for k in range(KT):
                    last = e.matmul(bank[b][:, 0:T], ones, src[:, k, :], start=k == 0, stop=k == KT - 1)
                return last
            p.add("pe", tag, emit, after=after)

        def channel_rms(tag, src, eps, after, mean=True):
            tt(f"{tag}.sq", squares, src, src, ALU.mult, after=after)
            mean_over_channels(f"{tag}.sum", squares, 5, (f"{tag}.sq",))
            ts(f"{tag}.ms", rsc, bank[5][:, 0:T], 1.0 / D, eps, ALU.mult, ALU.add, after=(f"{tag}.sum",))
            act(f"{tag}.sd", rsc, rsc, ACT.Sqrt, after=(f"{tag}.ms",))
            p.add("dve", f"{tag}.rs", lambda e, i: e.reciprocal(rsc, rsc), after=(f"{tag}.sd",))
        channel_rms("norm4", x3T, 1e-6, ("norm3.h7",))
        for k in range(KT):
            stt(f"norm4.h{k}", hT[:, k, :], x3T[:, k, :], gs[:, k:k + 1], rsc, ALU.mult, ALU.mult, after=("norm4.rs",))
            act(f"norm4.s{k}", hT[:, k, :], hT[:, k, :], ACT.Identity, after=(f"norm4.h{k}",), bias=mod[:, k:k + 1])

        p.add("pool", "TW.zero", lambda e, i: e.memset(TW, 0.0), after=("norm3.h7",))
        p.add("pool", "AL.zero", lambda e, i: e.memset(AL, 0.0))
        for n in "rkv":
            p.add("pool", f"pad.{n}.zero", lambda e, i, n=n: e.memset(pads[n], 0.0))
        for n, z in (("Az", Az), ("Rz", Rz)):
            for hh in range(2):
                p.add("pool", n + ".zero" if hh else n + "0.zero", lambda e, i, z=z, hh=hh: e.memset(z[hh], 0.0))
        p.add("pool", "pad2.zero", lambda e, i: e.memset(padA[:, :], 0.0))
        p.add("pool", "padz.zero", lambda e, i: e.memset(padz, 0.0))
        p.add("pe", "lora", project(half(0), slot[0], hT), after=("wlora", "norm4.s7"))
        freed[0] = "lora"
        act("lora.pad", padz[:, 1:], half(0), ACT.Copy, after=("lora", "padz.zero"))
        tt("lora.d", low, padz[:, 0:T], padz[:, 1:], ALU.subtract, after=("lora.pad",))
        stt("lora.s", low, low, PC("mu", 24), padz[:, 1:], ALU.mult, ALU.add)
        act("TW", TW[0:HD, :], low[0:HD, :], ACT.Tanh, after=("lora.s", "TW.zero"))
        copy("dve", "AL", AL[HD:P, :], low[HD:P, :], after=("AL.zero",))

        p.phase("rwkv", R_PAIRS)
        XW = {n: carve(T) for n in ("r", "k", "v")}
        aT, kkr, kk, rn, t1, kp, bT = (carve(T) for _ in range(7))
        lw = carve(T)
        ex = carve(2 * T)
        en = carve(T)
        eT = carve(1)
        Bf, Kf = carve(T), carve(T)
        Nt, Mt, RBt, RKt = (carve(4, P) for _ in range(4))
        Nm = [carve(4, P) for _ in range(2)]
        Xs, Zs, Gs = (carve(4, P) for _ in range(3))
        tok = carve(4, P)
        Fs, Us, St = carve(P), carve(TT, P), carve(HD)
        bonus, Oc, osq, grs, rg, hv, cth = (carve(T) for _ in range(7))
        lo2 = carve(P)

        def off(l):
            return cst2[:, P + l * P:P + (l + 1) * P]

        def four(ap):
            return ap.unsqueeze(1).to_broadcast([P, 4, P])

        def pi(name, plus=0):
            return lambda i: par[:, bass.ds(i + (PCOL[name] + plus), 1)]

        NR = 9
        Rr, Rk, Rv, VAL, GATE, OGP, ROG, GCP, GRP = range(NR)
        for n in range(NR):
            load(f"rw{n}", n, lambda i, n=n: a["w_rwkv"][i * NR + n, :, :], prev=(f"rp{n}.1",))
            if n == 1:
                p.dma("lo2", lambda e, i: e.dma_start(lo2, a["lora2"][i, :, :]), after=("AL",), prev=("lw.mm",))
        turn_of = [0]
        bank_reader = {}
        final_reader = {0: "gr", 1: "gc"}

        def rproj(n, evac):
            b = turn_of[0] % 2
            turn_of[0] += 1
            before = (bank_reader[b],) if b in bank_reader else ()
            back = () if b in bank_reader else (final_reader[b],)
            bank_reader[b] = evac

            def part(h):
                def emit(e, i):
                    for k in range(h * 4, h * 4 + 4):
                        last = e.matmul(half(b), slot[n][:, k * P:(k + 1) * P], hT[:, k, :], start=k == 0, stop=k == KT - 1)
                    return last
                p.add("pe", f"rp{n}.{h}", emit, after=(f"rw{n}", "norm4.s7", "lora.pad") + before, prev=back if h == 0 else ())
            return half(b), part

        for j, n in enumerate("rkv"):
            o, part = rproj(j, f"pad.{n}")
            part(0)
            part(1)
            act(f"pad.{n}", pads[n][:, 1:], o, ACT.Copy, after=(f"rp{j}.1",), prev=(f"sh.{n}",))
            tt(f"sd.{n}", XW[n], pads[n][:, 0:T], pads[n][:, 1:], ALU.subtract, after=(f"pad.{n}", "pad.v.zero"),
               prev=("bonus", "turn.tok"))
            stt(f"sh.{n}", XW[n], XW[n], pi("mu", 8 * j), pads[n][:, 1:], ALU.mult, ALU.add)
        rT, kT, vT = XW["r"], XW["k"], XW["v"]

        p.add("pe", "a.mm", lambda e, i: e.matmul(bank[2][:, 0:T], lo2, AL, start=True, stop=True),
              after=("lo2", "AL"), prev=("U1",))

        def lw_mm(e, i):
            for t in range(TT):
                o = bank[3][:, t * P:(t + 1) * P]
                e.matmul(o, TW[:, t * P:(t + 1) * P], lo2, start=True, stop=False)
                last = e.matmul(o, ones[0:1, :], w0[0:1, bass.ds(i * P, P)], start=False, stop=True)
            return last
        p.add("pe", "lw.mm", lw_mm, after=("TW", "w0row"), prev=("U1",))
        act("a.tanh", aT, bank[2][:, 0:T], ACT.Tanh, after=("a.mm",), bias=lambda i: a0h[:, bass.ds(i, 1)], scale=0.5)
        ts("a", aT, aT, 0.5, 0.5, ALU.mult, ALU.add, after=("a.tanh",))
        act("lw.tanh", lw, bank[3][:, 0:T], ACT.Tanh, after=("lw.mm",), scale=0.5)
        ts("lw", lw, lw, -0.5 * DECAY, -0.5 * DECAY, ALU.mult, ALU.add, after=("lw.tanh",))

        def cw_mm(e, i):
            for m, tri in enumerate((C("upper"), C("strict"))):
                for c in range(TT):
                    last = e.matmul(bank[4][:, m * T + c * P:m * T + c * P + P], lw[:, c * P:(c + 1) * P], tri,
                                    start=True, stop=True)
            return last
        p.add("pe", "cw.mm", cw_mm, after=("lw",), prev=("RK",))
        mid = cst[:, CCOL["mid"]:CCOL["mid"] + 2]
        act("ex", ex, bank[4][:, :], ACT.Exp, after=("cw.mm",), prev=("R1",), bias=mid[:, 1:2])
        act("en", en, bank[4][:, 0:T], ACT.Exp, bias=mid[:, 0:1], scale=-1.0)
        act("eT", eT, bank[4][:, P - 1:P], ACT.Exp, prev=("St",))

        o, val = rproj(VAL, "hv")
        val(0)
        val(1)
        act("hv", hv, o, ACT.Copy, after=(f"rp{VAL}.1",), prev=("conv.u",), scale=0.5)

        ts("kkr", kkr, kT, pi("k_k"), None, ALU.mult, after=("sh.v",))
        tt("kk.sq", rn, kkr, kkr, ALU.mult)
        p.add("pe", "kk.sum", lambda e, i: e.matmul(bank[5][:, 0:T], C("pair"), rn, start=True, stop=True),
              after=("kk.sq",), prev=("gn.rs", "gn.ms"))
        act("kk.norm", rn, bank[5][:, 0:T], ACT.Sqrt, after=("kk.sum",))
        ts("t1", t1, aT, pi("k_a"), lambda i: oka[:, bass.ds(i, 1)], ALU.mult, ALU.add)
        tt("kp", kp, kT, t1, ALU.mult)
        stt("rkr", t1, rT, pi("r_k"), kp, ALU.mult, ALU.mult)
        ts("kk.max", rn, rn, 1e-12, None, ALU.max, after=("kk.norm",))
        p.add("dve", "kk.rn", lambda e, i: e.reciprocal(rn, rn))
        tt("kk", kk, kkr, rn, ALU.mult)
        tt("b", bT, kk, aT, ALU.mult)
        eI, eE = ex[:, 0:T], ex[:, T:2 * T]
        for hh in range(2):
            r = slice(hh * HD, hh * HD + HD)
            stt(f"A{hh}", Az[hh][r, :], kk[r, :], -1.0, eE[r, :], ALU.mult, ALU.mult, after=("en", "Az.zero", "Rz.zero"))
        tt("B", Bf, bT, en, ALU.mult)
        tt("K", Kf, kp, en, ALU.mult)
        for hh in range(2):
            r = slice(hh * HD, hh * HD + HD)
            tt(f"R{hh}", Rz[hh][r, :], rT[r, :], eI[r, :], ALU.mult)
        p.add("pe", "bonus.sum", lambda e, i: e.matmul(bank[5][:, 0:T], C("pair"), t1, start=True, stop=True),
              after=("rkr", "kk.norm"))
        tt("bonus", bonus, vT, bank[5][:, 0:T], ALU.mult, after=("bonus.sum",))
        o, gt = rproj(GATE, "conv.th")
        gt(0)
        gt(1)
        act("conv.th", cth, o, ACT.Tanh, after=(f"rp{GATE}.1",), prev=("conv.u",), scale=0.5)

        def products(name, b, lhs, rhs, after, prev=()):
            def emit(e, i):
                for q in range(4):
                    hh, c = q // 2, slice(q % 2 * P, q % 2 * P + P)
                    l = lhs[hh] if isinstance(lhs, list) else lhs
                    r = rhs[hh] if isinstance(rhs, list) else rhs
                    last = e.matmul(bank[b][:, q * P:(q + 1) * P], l[:, c], r[:, c], start=True, stop=True)
                return last
            p.add("pe", name, emit, after=after, prev=prev)

        def quad(b):
            return view3(bank[b][:, :], P)
        products("N.mm", 2, Bf, Az, ("K", "a.tanh"), ())
        products("N1.mm", 3, Az, Bf, ("lw.tanh",))
        products("M.mm", 6, Kf, Az, (), ("St",))
        products("RB.mm", 7, Bf, Rz, ("R1",), ("O.copy",))
        products("RK.mm", 4, Kf, Rz, ("eT",))
        act("N", Nt, quad(2), ACT.Copy, after=("N.mm",), prev=("Nm6",))
        tt("X0.m", Xs, quad(3), four(cst2[:, 0:P]), ALU.mult, after=("N1.mm",))
        tt("X0", Xs, Xs, four(ident), ALU.add)
        tt("Z0.m", Zs, Nt, four(off(0)), ALU.mult, after=("N",))
        tt("Z0", Zs, Zs, four(ident), ALU.add)
        tt("M", Mt, quad(6), four(C("strict")), ALU.mult, after=("M.mm",))

        def turn_tok(e, i):
            for n, src in enumerate((Bf[:, 0:P], Kf[:, 0:P], vT[:, 0:P], vT[:, P:T])):
                last = e.transpose(bank[5][:, n * P:(n + 1) * P], src, ident)
            return last
        p.add("pe", "turn.tok", turn_tok, after=("bonus", "K"))
        act("tok", tok, quad(5), ACT.Copy, after=("turn.tok",))

        def mask(l):
            tt(f"Nm{l}", Nm[l % 2], Nt, four(off(l)), ALU.mult, after=("N",) + ((f"G{l - 2}.mm",) if l > 2 else ()),
               prev=(f"G{l + 4}.mm",) if l <= 2 else (), eng="pool")
        mask(1)
        mask(2)
        o, ogp = rproj(OGP, "og")
        def evac_og():
            act("og.th", lambda i: OG[:, bass.ds(i, 1), :], o_og.unsqueeze(1), ACT.Tanh, after=(f"rp{OGP}.1",), scale=0.5)
            stt("og", lambda i: OG[:, bass.ds(i, 1), :], lambda i: OG[:, bass.ds(i, 1), :], 1.0, o_og.unsqueeze(1),
                ALU.add, ALU.mult, after=("og.th",))
        o_og = o
        o_rog, rog = rproj(ROG, "rg")
        o_gc, gcp = rproj(GCP, "gc")
        o_gr, grp = rproj(GRP, "gr")
        fill = [(lambda: ogp(0), lambda: (ogp(1), evac_og())),
                (lambda: rog(0), lambda: (rog(1),
                    act("rg.th", rg, o_rog, ACT.Tanh, after=(f"rp{ROG}.1",), prev=("YR",), scale=0.5),
                    stt("rg", rg, rg, 1.0, o_rog, ALU.add, ALU.mult, after=("rg.th",)))),
                (lambda: gcp(0), lambda: (gcp(1),
                    act("gc", lambda i: GC[:, bass.ds(i, 1), :], o_gc.unsqueeze(1), ACT.Tanh, after=(f"rp{GCP}.1",), scale=0.5))),
                (lambda: grp(0), lambda: (grp(1),
                    act("gr", lambda i: GR[:, bass.ds(i, 1), :], o_gr.unsqueeze(1), ACT.Tanh, after=(f"rp{GRP}.1",), scale=0.5))),
                (lambda: None, lambda: None), (lambda: None, lambda: None)]

        def tap(j):
            w = lambda i: par[:, bass.ds(i * CONV2 + (PCOL["conv_k"] + j), 1)]
            o = lambda i: CU[:, bass.ds(i, 1), :]
            src = padA[:, j:j + T].unsqueeze(1)
            if j == 0:
                ts("tap0", o, src, w, pi("conv_b2"), ALU.mult, ALU.add)
            else:
                stt(f"tap{j}", o, src, w, o, ALU.mult, ALU.add)
        stt("conv.u", padA[:, CONV2 - 1:], cth, 1.0, hv, ALU.add, ALU.mult, after=("conv.th", "hv", "pad2.zero"))
        taps = list(range(CONV2))

        for l in range(1, LEVELS):
            def g_mm(e, i, l=l):
                for q in range(4):
                    last = e.matmul(bank[2][:, q * P:(q + 1) * P], Nm[l % 2][:, q, :], Xs[:, q, :], start=True, stop=True)
                return last
            p.add("pe", f"G{l}.mm", g_mm, after=(f"Nm{l}", "N") + (("X0", "Z0") if l == 1 else (f"X{l - 1}", f"G{l - 1}")))
            fill[l - 1][0]()
            tt(f"G{l}", Gs, quad(2), four(ident), ALU.add, after=(f"G{l}.mm",))
            if l + 2 < LEVELS:
                mask(l + 2)

            def xz_mm(e, i, l=l):
                if l < LEVELS - 1:
                    for q in range(4):
                        e.matmul(bank[3][:, q * P:(q + 1) * P], Zs[:, q, :], Gs[:, q, :], start=True, stop=True)
                for q in range(4):
                    last = e.matmul(bank[6][:, q * P:(q + 1) * P], Gs[:, q, :], Zs[:, q, :], start=True, stop=True)
                return last
            p.add("pe", f"XZ{l}.mm", xz_mm, after=(f"G{l}", "M") + (("X0", "Z0") if l == 1 else (f"X{l - 1}", f"Z{l - 1}")))
            fill[l - 1][1]()
            if l < LEVELS - 1:
                act(f"X{l}", Xs, quad(3), ACT.Copy, after=(f"XZ{l}.mm",))
            copy("dve", f"Z{l}", Zs, quad(6), after=(f"XZ{l}.mm",))
            if l == 1:
                tt("RB", RBt, quad(7), four(C("upper")), ALU.mult, after=("RB.mm",))
            if l == 2:
                tt("RK", RKt, quad(4), four(C("upper")), ALU.mult, after=("RK.mm",))
            for _ in range(6):
                if taps:
                    tap(taps.pop(0))
        while taps:
            tap(taps.pop(0))

        def V(c, hh):
            return tok[:, 2 + c, hh * HD:hh * HD + HD]

        for c in range(TT):
            def f_mm(e, i, c=c):
                for hh in range(2):
                    o = bank[2][:, hh * HD:hh * HD + HD]
                    if c:
                        e.matmul(o, Az[hh][:, P:T], St, start=True, stop=False)
                    last = e.matmul(o, Mt[:, 2 * hh + c, :], V(c, hh), start=not c, stop=True)
                return last
            p.add("pe", f"F{c}.mm", f_mm, after=("M", "tok", "G6") + (("St",) if c else ()))
            copy("dve", f"F{c}", Fs, bank[2][:, 0:P], after=(f"F{c}.mm",))

            def u_mm(e, i, c=c):
                for hh in range(2):
                    last = e.matmul(bank[3][:, hh * HD:hh * HD + HD], Zs[:, 2 * hh + c, :], Fs[:, hh * HD:hh * HD + HD],
                                    start=True, stop=True)
                return last
            p.add("pe", f"U{c}.mm", u_mm, after=(f"F{c}", "Z6", "X5"))
            copy("dve", f"U{c}", Us[:, c, :], bank[3][:, 0:P], after=(f"U{c}.mm",))
            if c == 0:
                def s_mm(e, i):
                    for hh in range(2):
                        r = slice(hh * HD, hh * HD + HD)
                        e.matmul(bank[6][r, 0:HD], tok[:, 0, r], Us[:, 0, r], start=True, stop=False)
                        last = e.matmul(bank[6][r, 0:HD], tok[:, 1, r], V(0, hh), start=False, stop=True)
                    return last
                p.add("pe", "S.mm", s_mm, after=("U0", "Z6"))
                ts("St", St, bank[6][:, 0:HD], eT, None, ALU.mult, after=("S.mm", "eT"))

        def o_mm(e, i):
            for c in range(TT):
                for hh in range(2):
                    r = slice(hh * HD, hh * HD + HD)
                    o = bank[7][r, c * P:(c + 1) * P]
                    e.matmul(o, V(c, hh), RKt[:, 2 * hh + c, :], start=True, stop=False)
                    if c:
                        e.matmul(o, St, Rz[hh][:, P:T], start=False, stop=False)
                    last = e.matmul(o, Us[:, c, r], RBt[:, 2 * hh + c, :], start=False, stop=True)
            return last
        p.add("pe", "O.mm", o_mm, after=("U1", "RK", "RB"))

        act("O.copy", Oc, bank[7][:, 0:T], ACT.Copy, after=("O.mm",))
        p.add("pe", "gn.sum", lambda e, i: e.matmul(bank[5][:, 0:T], C("pair"), Oc, start=True, stop=True),
              after=("O.copy", "tok"))
        stt("gn.c", Oc, bank[5][:, 0:T], -1.0 / HD, Oc, ALU.mult, ALU.add, after=("gn.sum",))
        tt("gn.sq", osq, Oc, Oc, ALU.mult)
        p.add("pe", "gn.var", lambda e, i: e.matmul(bank[5][:, 0:T], C("pair"), osq, start=True, stop=True), after=("gn.sq",))
        ts("gn.ms", grs, bank[5][:, 0:T], 1.0 / HD, 64e-5, ALU.mult, ALU.add, after=("gn.var",))
        act("gn.sd", grs, grs, ACT.Sqrt, after=("gn.ms",))
        p.add("dve", "gn.rs", lambda e, i: e.reciprocal(grs, grs), after=("gn.sd",))
        stt("gn.y", Oc, Oc, pi("gn_g"), grs, ALU.mult, ALU.mult)
        stt("gn.b", Oc, Oc, pi("gn_b"), bonus, ALU.add, ALU.add)
        tt("YR", lambda i: YR[:, bass.ds(i, 1), :], Oc.unsqueeze(1), rg.unsqueeze(1), ALU.mult, after=("rg",))
        for n in range(NR):
            freed[n] = f"rp{n}.1"

        p.phase("conv norm")
        used[0] = block2_end
        mean = carve(T)
        cv2 = carve(KT, T)
        mT = carve(KT, T)
        mean_over_channels("ln.sum", CU, 5, (f"tap{CONV2 - 1}", "gn.ms"))
        ts("ln.mean", mean, bank[5][:, 0:T], 1.0 / D, None, ALU.mult, after=("ln.sum",))
        tt("ln.c", CU, CU, mean.unsqueeze(1).to_broadcast([P, KT, T]), ALU.subtract)
        tt("ln.sq", cv2, CU, CU, ALU.mult)
        mean_over_channels("ln.var", cv2, 5, ("ln.sq",))
        ts("ln.ms", rsc, bank[5][:, 0:T], 1.0 / D, 1e-5, ALU.mult, ALU.add, after=("ln.var",))
        act("ln.sd", rsc, rsc, ACT.Sqrt, after=("ln.ms",))
        p.add("dve", "ln.rs", lambda e, i: e.reciprocal(rsc, rsc), after=("ln.sd",))
        for k in range(KT):
            stt(f"ln.g{k}", CU[:, k, :], CU[:, k, :], PC("ln_g", k), rsc, ALU.mult, ALU.mult)
            ts(f"ln.b{k}", CU[:, k, :], CU[:, k, :], PC("ln_b", k), None, ALU.add)
            act(f"ln.th{k}", cv2[:, k, :], CU[:, k, :], ACT.Tanh, after=(f"ln.b{k}",), scale=0.5)
            stt(f"ln.si{k}", CU[:, k, :], cv2[:, k, :], 1.0, CU[:, k, :], ALU.add, ALU.mult, after=(f"ln.th{k}",))
            tt(f"ln.y{k}", CU[:, k, :], CU[:, k, :], OG[:, k, :], ALU.mult)

        p.phase("gated", KT)
        m0, m1 = carve(T), carve(T)
        for n, (src, g, done, f) in enumerate(((CU, GC, "ln.y7", 0.125), (YR, GR, "YR", 0.25))):
            load(f"wy{n}", n, lambda i, n=n: a["w_y"][i * 2 + n, :, :], prev=(f"y{n}.mm",))
            p.add("pe", f"y{n}.mm", project(half(n), slot[n], src), after=(f"wy{n}", done, "gr", "gc"), prev=(f"gy{n}",))
            stt(f"gy{n}", (m0, m1)[n].unsqueeze(1), lambda i, g=g: g[:, bass.ds(i, 1), :], 1.0, half(n).unsqueeze(1),
                ALU.add, ALU.mult, after=(f"y{n}.mm",))
            ts(f"gf{n}", (m0, m1)[n], (m0, m1)[n], f, None, ALU.mult)
        tt("m", lambda i: mT[:, bass.ds(i, 1), :], m0.unsqueeze(1), m1.unsqueeze(1), ALU.add)
        freed[0], freed[1] = "y0.mm", "y1.mm"

        p.phase("w_out2", KT // 2)
        for n in range(2):
            load(f"wz{n}", 2 + n, lambda i, n=n: a["w_out2"][i * 2 + n, :, :], prev=(f"z{n}.mm",))
            p.add("pe", f"z{n}.mm", project(half(2 + n), slot[2 + n], mT), after=(f"wz{n}", "m"), prev=(f"z{n}",))
            xk = lambda i, n=n: x3T[:, bass.ds(i * 2 + n, 1), :]
            stt(f"z{n}", xk, half(2 + n).unsqueeze(1), lambda i, n=n: mod[:, bass.ds(i * 2 + (16 + n), 1)], xk,
                ALU.mult, ALU.add, after=(f"z{n}.mm",))

        p.phase("final")
        channel_rms("norm5", x3T, 1e-6, ("z1",))
        ytok = hT[:, :, :].rearrange("p k n -> p (k n)").rearrange("p (t d) -> p t d", t=TT)
        for k in range(KT):
            stt(f"fin{k}", CU[:, k, :], x3T[:, k, :], PC("final_g", k), rsc, ALU.mult, ALU.mult, after=("norm5.rs",))

            def turn_back(e, i, k=k):
                for t in range(TT):
                    last = e.transpose(bank[k % 4][:, t * P:(t + 1) * P], CU[:, k, t * P:(t + 1) * P], ident)
                return last
            p.add("pe", f"fin.turn{k}", turn_back, after=(f"fin{k}",) + ((f"fin.y{k - 4}",) if k >= 4 else ()))
            act(f"fin.y{k}", ytok[:, :, k * P:(k + 1) * P], view3(half(k % 4), P), ACT.Copy, after=(f"fin.turn{k}",))
        p.dma("out", lambda e, i: e.dma_start(out.rearrange("(t p) d -> p t d", p=P), ytok), after=("fin.y7",))

        block = ctx.enter_context(nc.Block())

        @block.tensor
        def _(e):
            p.run("pe", e)

        @block.scalar
        def _(e):
            p.run("act", e)

        @block.vector
        def _(e):
            p.run("dve", e)

        @block.gpsimd
        def _(e):
            p.run("pool", e)

        @block.sync
        def _(e):
            p.run("sp", e)
            e.wait_ge(p.named["out"].sem, 16)


def col_slices(w, starts):
    k = w.shape[0] // P
    return np.stack([np.ascontiguousarray(w[:, s:s + P].reshape(k, P, P).transpose(1, 0, 2)).reshape(P, k * P)
                     for s in starts])


def by_partition(v):
    return np.ascontiguousarray(v.reshape(-1, P).T)


def layouts(w):
    o = {"x": w["x"][0], "cst": shape_constants(), "rel_bias": w["rel_bias"]}
    par = np.zeros((P, NPCOL), np.float32)
    convw = np.stack([w["conv_w"][0][j].reshape(8, P) for j in range(CONV1)], 1)
    convk = np.stack([w["conv_k_2"][0][j].reshape(KT, P) for j in range(CONV2)], 1)
    for name, v in (("norm_mix", by_partition(w["norm_mix"][0])), ("norm_ffn", by_partition(w["norm_ffn"][0])),
                    ("norm_final", by_partition(w["norm_final"])), ("norm_g", by_partition(w["norm_g_2"][0])),
                    ("final_g", by_partition(w["final_g_2"])), ("conv_w", convw.reshape(8 * CONV1, P).T),
                    ("conv_b", by_partition(w["conv_b"][0])), ("d_skip", by_partition(np.repeat(w["d_skip"][0], HD))),
                    ("ssm_norm", by_partition(w["ssm_norm_w"][0])), ("ada_b", by_partition(w["ada_b_2"][0])),
                    ("c", by_partition(w["c_2"][0])), ("conv_k", convk.reshape(KT * CONV2, P).T),
                    ("conv_b2", by_partition(w["conv_b_2"][0])), ("ln_g", by_partition(w["conv_ln_g_2"][0])),
                    ("ln_b", by_partition(w["conv_ln_b_2"][0])), ("mu", by_partition(w["rwkv_mu_2"][0])),
                    ("a0", by_partition(w["rwkv_a0_2"][0])), ("k_k", by_partition(w["rwkv_k_k_2"][0])),
                    ("k_a", by_partition(w["rwkv_k_a_2"][0])), ("r_k", by_partition(w["rwkv_r_k_2"][0].reshape(-1))),
                    ("gn_g", by_partition(w["rwkv_gn_g_2"][0])), ("gn_b", by_partition(w["rwkv_gn_b_2"][0]))):
        par[:, PCOL[name]:PCOL[name] + v.shape[1]] = v
    o["par"] = par
    o["row"] = np.concatenate([w["dt_bias"][0], w["forget_bias"][0], w["a_log"][0], w["sinks"][0]])[None, :]
    o["w0"] = w["rwkv_w0_2"]
    wi = w["w_in"][0]
    both = lambda s: np.concatenate([wi[:, s:s + HD]] * 2, 1)
    o["w_pre"] = np.concatenate([col_slices(wi, (B0, B0 + P, C0, C0 + P)), col_slices(both(DK0), (0,)),
                                 col_slices(both(DK0 + HD), (0,)), col_slices(wi, (DV0,))])
    ws = np.concatenate([wi[:, DT0:DT0 + NH], wi[:, F0:F0 + NH]], 1)
    o["w_small"] = np.ascontiguousarray(ws.reshape(KT, P, 2 * NH).transpose(1, 0, 2)).reshape(P, -1)
    starts = []
    for i in range(PAIRS):
        starts += [s + i * P for s in (BQ0, BQ0 + W, BQ0 + 2 * W, CQ0, CQ0 + W, CQ0 + 2 * W, DQ0, X0, Z0)]
        starts += [G0 + i * D + j * P for j in range(KT)]
    o["w_heads"] = col_slices(wi, starts)
    wb = [col_slices(w["w_branch"][0, b], range(0, D, P)) for b in range(N_BR)]
    o["w_br"] = np.stack(wb, 1).reshape(KT * N_BR, P, W)
    o["w_out"] = w["w_out"][0]
    g, u = (col_slices(w[n][0], range(0, D_FF, P)) for n in ("w_ffn_gate", "w_ffn_up"))
    o["w_gu"] = np.stack([g, u], 1).reshape(2 * FF_TILES, P, D)
    o["w_down"] = w["w_ffn_down"][0]
    o["ada_w"] = np.ascontiguousarray(
        w["ada_w_2"][0].reshape(KT, P, 3, D).transpose(0, 2, 1, 3)).reshape(3 * KT, P, D)
    wi = w["w_in_2"][0]
    starts = []
    for i in range(R_PAIRS):
        starts += [s + i * P for s in (TS0, TS0 + D, TS0 + 2 * D, VAL0, GATE0, OG0, ROG0, GC0, GR0)]
    o["w_rwkv"] = col_slices(wi, starts)
    o["w_lora"] = col_slices(wi, (TS0 + 3 * D,))[0]
    lo = np.concatenate([w["rwkv_w2_2"][0], w["rwkv_a2_2"][0]], 0)
    o["lora2"] = np.ascontiguousarray(lo.reshape(P, KT, P).transpose(1, 0, 2))
    y = [col_slices(w[n][0], range(0, D, P)) for n in ("w_conv_out_2", "w_rwkv_out_2")]
    o["w_y"] = np.stack(y, 1).reshape(2 * KT, P, D)
    o["w_out2"] = col_slices(w["w_out_2"][0], range(0, D, P))
    return {k: np.ascontiguousarray(v) for k, v in o.items()}


def kernel(**inputs):
    import concourse.bacc as bacc
    from concourse.bass_utils import run_bass_kernel_spmd

    arrays = layouts({k: np.asarray(v) for k, v in inputs.items()})
    nc = bacc.Bacc("TRN2", target_bir_lowering=False, num_devices=1)
    aps = {n: nc.dram_tensor("in_" + n, v.shape, mybir.dt.from_np(v.dtype), kind="ExternalInput").ap() for n, v in arrays.items()}
    out = nc.dram_tensor("out_y", (T, D), F32, kind="ExternalOutput").ap()
    build(nc, aps, out)
    r = run_bass_kernel_spmd(nc, [{"in_" + n: v for n, v in arrays.items()}], core_ids=[0])
    return r.results[0]["out_y"].reshape(1, T, D)
```

```python
import math
from contextlib import ExitStack

import numpy as np

import concourse.bass as bass
from concourse import mybir

F32 = mybir.dt.float32
ACT = mybir.ActivationFunctionType
ALU = mybir.AluOpType
AX = mybir.AxisListType

T = 256
D = 1024
P = 128
KT = D // P
TT = T // P
W = 512
HD = 64
NH = W // HD
PAIRS = NH // 2
N_BR = 4
GROUPS = 2
D_FF = 2816
FF_TILES = D_FF // P
REL_BUCKETS, REL_EXACT, REL_MAX = 32, 16, 1024
SWA_WINDOW = 128
CONV1 = 4
CONV2 = 31
R_PAIRS = D // P
LEVELS = 7
NEG = -1e30
LOGIT = T + 1
SROW = P + 1 + LOGIT
DECAY = math.exp(-0.5)
MID = 0.5 * P * DECAY

Z0, X0, B0, C0 = 0, 512, 1024, 1280
DT0, BQ0, CQ0, F0, DQ0, DK0, DV0, G0 = 1536, 1544, 3080, 4616, 4624, 5136, 5264, 5392
VAL0, GATE0, OG0, TS0, ROG0, GC0, GR0 = 0, 1024, 2048, 3072, 6272, 7296, 8320

def columns(*fields):
    at, out = 0, {}
    for name, n in fields:
        out[name] = at
        at += n
    return out, at


PCOL, NPCOL = columns(("norm_mix", KT), ("norm_ffn", KT), ("norm_final", KT), ("norm_g", KT),
                      ("final_g", KT), ("conv_w", 8 * CONV1), ("conv_b", 8), ("d_skip", PAIRS),
                      ("ssm_norm", PAIRS), ("ada_b", 24), ("c", KT), ("conv_k", KT * CONV2),
                      ("conv_b2", KT), ("ln_g", KT), ("ln_b", KT), ("mu", 25), ("a0", KT), ("k_k", KT),
                      ("k_a", KT), ("r_k", KT), ("gn_g", KT), ("gn_b", KT))
RCOL, NRCOL = columns(("dt_bias", NH), ("forget_bias", NH), ("a_log", NH), ("sinks", NH))
CCOL, NCCOL = columns(("ident", P), ("flip", P), ("upper", P), ("ones", P), ("upper2", P),
                      ("strict", P), ("pair", P), ("pick", NH), ("mid", 2),
                      ("onehot", 3 * P), ("gmask", 3 * P), ("off_first", P), ("off", LEVELS * P))
NKEPT = CCOL["onehot"]
NFIRST = CCOL["off_first"]


def shape_constants():
    c = np.zeros((P, NCCOL), np.float32)
    r, q = np.arange(P)[:, None], np.arange(P)[None, :]

    def put(name, a):
        c[:a.shape[0], CCOL[name]:CCOL[name] + a.shape[1]] = a

    put("ident", r == q)
    put("flip", r == P - 1 - q)
    put("upper", r <= q)
    put("ones", np.ones((P, P)))
    put("upper2", r <= q)
    put("strict", r < q)
    put("pair", r // HD == q // HD)
    put("off_first", (r == q + 1) & (r % 2 == 1))
    for l in range(LEVELS):
        s = 1 << l
        c[:, CCOL["off"] + l * P:CCOL["off"] + (l + 1) * P] = \
            (r // (2 * s) == q // (2 * s)) & (r // s % 2 == 0) & (q // s % 2 == 1)
    dist = T - 1 - np.arange(3 * P)
    d = np.maximum(dist, 1).astype(np.float32)
    large = REL_EXACT + (np.log(d / np.float32(REL_EXACT)) / np.float32(math.log(REL_MAX / REL_EXACT))
                         * np.float32(REL_BUCKETS - REL_EXACT)).astype(np.int32)
    bucket = np.where(dist < REL_EXACT, np.maximum(dist, 0), np.minimum(large, REL_BUCKETS - 1))
    put("onehot", np.arange(REL_BUCKETS)[:, None] == bucket[None, :])
    gmask = np.zeros((2 * NH + 1, 3 * P))
    gmask[:, dist < 0] = NEG
    gmask[NH:2 * NH, dist >= SWA_WINDOW] = NEG
    put("gmask", gmask)
    put("pick", np.eye(40, NH) + np.eye(40, NH, -32))
    put("mid", np.tile(np.array([[-MID, MID]]), (P, 1)))
    return c


class Step:
    def __init__(self, phase, engine, index, emit, after, prev, sem, lag):
        self.phase, self.engine, self.index, self.emit = phase, engine, index, emit
        self.after, self.prev, self.sem, self.lag = after, prev, sem, lag


class Phase:
    def __init__(self, name, trips, at, peel):
        self.name, self.trips, self.at, self.peel = name, trips, at, peel
        self.steps, self.per, self.base = [], {}, {}


class Program:
    ENGINES = ("pe", "act", "dve", "pool", "sp")
    START = 256

    def __init__(self, sems, new_sem):
        self.sems, self.new_sem, self.phases, self.named = sems, new_sem, [], {}

    def phase(self, name, trips=None, at=0, peel=""):
        self.phases.append(Phase(name, trips, at, peel))

    def add(self, engine, name, emit, after=(), prev=(), lag=1):
        ph = self.phases[-1]
        after = (after,) if isinstance(after, str) else tuple(after)
        prev = (prev,) if isinstance(prev, str) else tuple(prev)
        if ph.peel:
            after = tuple(n + ph.peel if n + ph.peel in self.named else n for n in after)
            after += tuple(n for n in prev if n in self.named)
            prev = ()
        ph.per[engine] = ph.per.get(engine, 0) + 1
        step = Step(ph, engine, ph.per[engine], emit, after, prev, self.sems[engine], lag)
        name += ph.peel
        assert name not in self.named, name
        self.named[name] = step
        ph.steps.append(step)
        return name

    def dma(self, name, emit, after=(), prev=(), engine="sp"):
        name = self.add(engine, name, emit, after, prev)
        self.phases[-1].per[engine] -= 1
        self.named[name].sem, self.named[name].index = self.new_sem("got_" + name.replace(".", "_")), None

    def run(self, engine, eng):
        sem = self.sems[engine]
        eng.sem_inc(sem, self.START)
        base = {e: self.START for e in self.ENGINES}
        for ph in self.phases:
            ph.base = dict(base)
            for e in self.ENGINES:
                base[e] += ph.per.get(e, 0) * (ph.trips or 1)
            steps = [s for s in ph.steps if s.engine == engine]
            if not steps:
                continue
            if ph.trips is None:
                self.emit(eng, steps, ph.at)
            else:
                with eng.Fori(0, ph.trips) as i:
                    self.emit(eng, steps, i)

    def emit(self, eng, steps, i):
        seen = {}
        for s in steps:
            ph, own = s.phase, s.engine
            if own in ("act", "dve", "pool") and s.index is not None:
                before = ph.base[own] + s.index - s.lag
                eng.wait_ge(self.sems[own], before if ph.trips is None else i * ph.per[own] + before)
                seen[id(self.sems[own])] = (1, s.index - s.lag)
            for names, back in ((s.after, 0), (s.prev, 1)):
                for name in names:
                    t = self.named[name]
                    here = t.phase is ph
                    assert here or not back, name
                    count, per, base = (16, 16, 0) if t.index is None else \
                        (t.index, t.phase.per[t.engine], t.phase.base[t.engine])
                    if here and ph.trips is not None:
                        rank = (1 - back, count)
                        value = i * per + (base + count - back * per)
                    else:
                        value = base + count + ((t.phase.trips or 1) - 1) * per
                        rank = (-1, value)
                    known = seen.get(id(t.sem), (-9, 0))
                    if known >= rank and not (rank[0] == -1 and known[0] == 0):
                        continue
                    eng.wait_ge(t.sem, value)
                    seen[id(t.sem)] = max(known, rank)
            s.emit(eng, i).then_inc(s.sem, 1 if s.index is not None else 16)


def build(nc, a, out):
    with ExitStack() as ctx:
        def sb(name, *shape):
            return ctx.enter_context(nc.sbuf_tensor(name, list(shape), F32))

        def sem(name):
            return ctx.enter_context(nc.semaphore(name))

        cst = sb("cst", P, NKEPT)
        par = sb("par", P, NPCOL)
        row = sb("row", 1, NRCOL)
        bank = [ctx.enter_context(nc.psum_tensor(f"bank{n}", [P, 512], F32)) for n in range(8)]
        N_SLOTS = 12
        slot = [sb(f"slot{n}", P, D) for n in range(N_SLOTS)]
        hT = sb("hT", P, KT, T)
        x = sb("x", P, TT, D)
        x3T = x[:, :, :].rearrange("p t d -> p (t d)").rearrange("p (k n) -> p k n", n=T)
        adaA = sb("adaA", P, 3 * D)
        stat = sb("stat", P, 6)
        small = sb("small", P, 48)

        def C(name, n=P, rows=P, off=0):
            return cst[0:rows, CCOL[name] + off:CCOL[name] + off + n]

        def PC(name, j=0):
            return par[:, PCOL[name] + j:PCOL[name] + j + 1]

        ident, flip, ones = C("ident"), C("flip"), C("ones")

        ARENA = 30800
        arena = sb("arena", P, ARENA)
        used = [0]

        def carve(*shape, rows=P):
            n = int(np.prod(shape))
            v = arena[0:rows, used[0]:used[0] + n]
            used[0] += n
            assert used[0] <= ARENA, used[0]
            if len(shape) == 2:
                v = v.rearrange("p (a b) -> p a b", a=shape[0])
            elif len(shape) == 3:
                v = v.rearrange("p (a b c) -> p a b c", a=shape[0], b=shape[1])
            return v

        p = Program({e: sem("steps_of_" + e) for e in Program.ENGINES}, sem)

        def view3(ap, n):
            return ap.rearrange("p (a b) -> p a b", b=n)

        freed = {}

        def load(name, n, src, after=(), prev=(), rows=P, width=D):
            p.dma(name, lambda e, i: e.dma_start(slot[n][0:rows, 0:width], src(i)),
                  after=tuple(after) + ((freed[n],) if n in freed else ()), prev=prev)

        def project(psum, w, rhs, kt=KT):
            def emit(e, i):
                for k in range(kt):
                    last = e.matmul(psum, w[:, k * P:(k + 1) * P], rhs[:, k, :], start=k == 0, stop=k == kt - 1)
                return last
            return emit

        def project_tokens(psum, w):
            def emit(e, i):
                for t in range(TT):
                    for k in range(KT):
                        last = e.matmul(psum[:, t * P:(t + 1) * P], hT[:, k, t * P:(t + 1) * P],
                                        w[:, k * P:(k + 1) * P], start=k == 0, stop=k == KT - 1)
                return last
            return emit

        def half(n):
            return bank[n][:, 0:T]

        def act(name, o, i_, f, after=(), prev=(), **kw):
            p.add("act", name, lambda e, i: e.activation(
                o(i) if callable(o) else o, i_(i) if callable(i_) else i_, f,
                **{k: v(i) if callable(v) else v for k, v in kw.items()}), after, prev)

        def on(v, i):
            return v(i) if callable(v) else v

        def copy(eng, name, o, i_, after=(), prev=()):
            p.add(eng, name, lambda e, i: e.tensor_copy(on(o, i), on(i_, i)), after, prev)

        def tt(name, o, x0, x1, op, after=(), prev=(), eng="dve", lag=1):
            p.add(eng, name, lambda e, i: e.tensor_tensor(on(o, i), on(x0, i), on(x1, i), op), after, prev, lag)

        def ts(name, o, x0, s1, s2, op0, op1=None, after=(), prev=(), eng="dve", lag=1):
            p.add(eng, name, lambda e, i: e.tensor_scalar(on(o, i), on(x0, i), on(s1, i), on(s2, i), op0,
                                                          **({"op1": op1} if op1 is not None else {})), after, prev, lag)

        def stt(name, o, x0, s, x1, op0, op1, after=(), prev=(), lag=1):
            p.add("dve", name, lambda e, i: e.scalar_tensor_tensor(
                out=on(o, i), in0=on(x0, i), scalar=on(s, i), in1=on(x1, i), op0=op0, op1=op1), after, prev, lag)

        def bc(ap, shape):
            return ap.to_broadcast(list(shape))

        p.phase("setup")
        p.dma("x", lambda e, i: e.dma_start(x[:, :, :], a["x"].rearrange("(t p) d -> p t d", p=P)))
        p.dma("cst", lambda e, i: e.dma_start(cst[:, :], a["cst"][:, 0:NKEPT]), engine="act")
        p.dma("par", lambda e, i: e.dma_start(par[:, :], a["par"]), engine="act")
        p.dma("row", lambda e, i: e.dma_start(row[:, :], a["row"]), engine="act")
        relb = sb("relb", REL_BUCKETS, 2 * NH + 1)
        p.add("pool", "relb.zero", lambda e, i: e.memset(relb[:, :], 0.0))
        p.dma("relb", lambda e, i: e.dma_start(relb[:, 0:2 * NH], a["rel_bias"]), after="relb.zero")
        p.add("pool", "ada.zero", lambda e, i: e.memset(adaA[:, :], 0.0))
        sc = sb("sc", P, KT)
        cT = par[:, PCOL["c"]:PCOL["c"] + KT]
        act("sc.tanh", sc[:, :], cT, ACT.Tanh, after=("par",), scale=0.5)
        stt("sc.x", sc[:, :], sc[:, :], 1.0, cT, ALU.add, ALU.mult, after=("sc.tanh",))
        ts("sc", sc[:, :], sc[:, :], 0.5, None, ALU.mult, after=("sc.x",))

        xn = arena[:, 8 * T:8 * T + TT * D].rearrange("p (t d) -> p t d", t=TT)

        def token_norm(tag, weight, target, after):
            ss, sd, rs = stat[:, 0:2], stat[:, 2:4], stat[:, 4:6]
            for t in range(TT):
                act(f"{tag}.sq{t}", xn[:, t, :], x[:, t, :], ACT.Square, after=after, accum_out=ss[:, t:t + 1])
            ts(f"{tag}.ms", sd, ss, 1.0 / D, 1e-6, ALU.mult, ALU.add, after=(f"{tag}.sq{TT - 1}",))
            act(f"{tag}.sd", sd, sd, ACT.Sqrt, after=(f"{tag}.ms",))
            p.add("dve", f"{tag}.rs", lambda e, i: e.reciprocal(rs, sd), after=(f"{tag}.sd",))
            for t in range(TT):
                ts(f"{tag}.xn{t}", xn[:, t, :], x[:, t, :], rs[:, t:t + 1], None, ALU.mult, after=(f"{tag}.rs",))
            for k in range(KT):
                def turn(e, i, k=k):
                    for t in range(TT):
                        last = e.transpose(half(k % 4)[:, t * P:(t + 1) * P], xn[:, t, k * P:(k + 1) * P], ident)
                    return last
                p.add("pe", f"{tag}.turn{k}", turn, after=(f"{tag}.xn1", "cst") + ((f"{tag}.h{k - 4}",) if k >= 4 else ()))
                ts(f"{tag}.h{k}", target[:, k, :], half(k % 4), PC(weight, k), None, ALU.mult,
                   after=(f"{tag}.turn{k}", "par"))

        token_norm("norm1", "norm_mix", hT, after=("x",))

        p.phase("pre")
        padA = sb("padA", P, 30 + T)
        pad1 = padA[:, 0:CONV1 - 1 + T]
        conv = sb("conv", P, T)
        th = sb("th", P, T)
        gates = carve(N_BR * KT, T)
        YT = [carve(W // P, T) for _ in range(N_BR)]
        Hk = carve(2 * NH + 1, LOGIT)
        CBT = carve(PAIRS, 3 * P)
        BCT = gates[:, 0:4, :]
        dk = carve(PAIRS, T)
        dv = carve(PAIRS, TT, HD)
        dtc = carve(TT, NH)
        acum = carve(TT, NH)
        acumT = carve(T)
        fcumT = carve(T)
        cwh = carve(8 * CONV1 + 8)
        wsm = carve(KT, 2 * NH)
        lf, rf = carve(T), carve(T)
        block1_end = used[0]
        LF = carve(TT, 40)
        LA = carve(TT, NH)
        sp = [carve(TT, 2 * NH) for _ in range(6)]
        expA = carve(NH)
        gsb = carve(3 * P)
        cst1 = carve(NFIRST - NKEPT)
        onehot, gmask = cst1[0:REL_BUCKETS, 0:3 * P], cst1[0:2 * NH + 1, 3 * P:6 * P]
        p.dma("cst1", lambda e, i: e.dma_start(cst1, a["cst"][:, NKEPT:NFIRST]), engine="act")

        p.dma("wsm", lambda e, i: e.dma_start(wsm.rearrange("p a b -> p (a b)"), a["w_small"]))
        for n in range(7):
            load(f"pre.w{n}", n, lambda i, n=n: a["w_pre"][n, :, :])
        ts("cwh", cwh, par[:, PCOL["conv_w"]:PCOL["conv_w"] + 40], 0.5, None, ALU.mult, after=("par",))
        p.add("pool", "padA.zero", lambda e, i: e.memset(padA[:, :], 0.0))
        p.add("pool", "fcumT.zero", lambda e, i: e.memset(fcumT, 0.0))
        p.add("pool", "lf.zero", lambda e, i: e.memset(lf, 0.0))
        p.add("pool", "rf.zero", lambda e, i: e.memset(rf, 0.0))
        p.add("pool", "lf.ones", lambda e, i: e.memset(lf[0:NH, :], 1.0), after=("rf.zero",))
        p.add("pool", "rf.ones", lambda e, i: e.memset(rf[32:40, :], 1.0))
        p.add("pool", "LF.zero", lambda e, i: e.memset(LF, 0.0))

        p.add("pe", "g.mm", lambda e, i: e.matmul(bank[7][0:2 * NH + 1, 0:3 * P], relb[:, :],
              onehot, start=True, stop=True), after=("relb", "cst1"))
        tt("g.mask", gsb[0:2 * NH + 1, :], bank[7][0:2 * NH + 1, 0:3 * P], gmask, ALU.add,
           after=("g.mm",))
        g_dram = nc.dram_tensor("g_scratch", [2 * NH + 1, 3 * P], F32, kind="Internal")
        p.dma("g.out", lambda e, i: e.dma_start(g_dram.ap(), gsb[0:2 * NH + 1, :]), after=("g.mask",))
        shifted = bass.AP(g_dram, 0, [[1, P], [3 * P, 2 * NH + 1], [1, T]])
        p.dma("g.in", lambda e, i: e.dma_start(Hk[:, :, 0:T], shifted), after=("g.out",))
        p.add("dve", "sink.none", lambda e, i: e.memset(Hk[:, :, T:LOGIT], NEG))
        p.add("pe", "sink.mm", lambda e, i: e.matmul(bank[7][:, 0:NH], ones[0:1, :],
              row[0:1, RCOL["sinks"]:RCOL["sinks"] + NH], start=True, stop=True), after=("row", "g.mask"))
        copy("dve", "sink", Hk[:, NH:2 * NH, T:LOGIT], bank[7][:, 0:NH].unsqueeze(2), after=("sink.mm", "sink.none"))

        def small_mm(e, i):
            for t in range(TT):
                e.matmul(bank[6][:, t * 16:(t + 1) * 16], ones[0:1, :], row[0:1, 0:2 * NH], start=True, stop=False)
                for k in range(KT):
                    last = e.matmul(bank[6][:, t * 16:(t + 1) * 16], hT[:, k, t * P:(t + 1) * P], wsm[:, k, :],
                                    start=False, stop=k == KT - 1)
            return last
        p.add("pe", "small", small_mm, after=("wsm", "row", "norm1.h7"))
        rowA = row[0:1, RCOL["a_log"]:RCOL["a_log"] + NH]
        act("expA.row", rowA, rowA, ACT.Exp, after=("row",))
        p.add("pe", "expA.mm", lambda e, i: e.matmul(bank[6][:, 64:64 + NH], ones[0:1, :], rowA, start=True, stop=True),
              after=("expA.row",))
        v, nb, u, w1, d1, soft = sp
        ps_small = view3(bank[6][:, 0:32], 16)
        copy("dve", "expA", expA, bank[6][:, 64:64 + NH], after=("expA.mm",))
        copy("dve", "sp.v0", v[:, :, 0:NH], ps_small[:, :, 0:NH], after=("small",))
        ts("sp.v1", v[:, :, NH:], ps_small[:, :, NH:], -1.0, None, ALU.mult)
        stt("sp.nb", nb, v, -1.0, v, ALU.mult, ALU.min, after=("sp.v1",))
        act("sp.u", u, nb, ACT.Exp, after=("sp.nb",))
        ts("sp.w1", w1, u, 1.0, None, ALU.add, after=("sp.u",))
        act("sp.ln", soft, w1, ACT.Ln, after=("sp.w1",))
        ts("sp.d1", d1, w1, -1.0, 1e-30, ALU.add, ALU.max, after=("sp.w1",))
        p.add("dve", "sp.rd", lambda e, i: e.reciprocal(d1, d1), after=("sp.d1",))
        tt("sp.lnu", soft, soft, u, ALU.mult, after=("sp.ln",))
        tt("sp.lnr", soft, soft, d1, ALU.mult, after=("sp.lnu", "sp.rd"))
        stt("sp.tiny", u, w1, 1.0, u, ALU.is_equal, ALU.mult, after=("sp.lnr",))
        tt("sp.log1p", soft, soft, u, ALU.add, after=("sp.tiny",))
        stt("sp.soft", soft, v, 0.0, soft, ALU.max, ALU.add, after=("sp.log1p",))
        copy("dve", "dt", dtc, soft[:, :, 0:NH], after=("sp.soft",))
        stt("LA", LA, soft[:, :, 0:NH], -1.0, bc(expA.unsqueeze(1), (P, TT, NH)), ALU.mult, ALU.mult,
            after=("sp.soft", "expA"))
        copy("dve", "LF0", LF[:, :, 0:NH], soft[:, :, NH:], after=("LF.zero", "sp.soft"))
        ts("LF1", LF[:, :, 32:40], soft[:, :, NH:], -1.0, None, ALU.mult)

        def conv_tile(tag, tile, evac_after, target, wcol, eng_after=()):
            ts(f"{tag}.tap0", conv[:, :], pad1[:, 0:T], lambda i: cwh[:, wcol(i, 0)], lambda i: cwh[:, wcol(i, None)], ALU.mult, ALU.add, after=evac_after + ("cwh",))
            for j in range(1, CONV1):
                stt(f"{tag}.tap{j}", conv[:, :], pad1[:, j:j + T],
                    lambda i, j=j: cwh[:, wcol(i, j)], conv[:, :], ALU.mult, ALU.add,
                    after=(f"{tag}.tap{j - 1}",))
            act(f"{tag}.tanh", th[:, :], conv[:, :], ACT.Tanh, after=(f"{tag}.tap{CONV1 - 1}",))
            stt(f"{tag}.silu", target, th[:, :], 1.0, conv[:, :], ALU.add, ALU.mult, after=(f"{tag}.tanh",))

        last = None
        for n in range(4):
            p.add("pe", f"bc{n}", project(half(n), slot[n], hT), after=(f"pre.w{n}", "norm1.h7"))
        for n in range(4):
            act(f"bc{n}.pad", pad1[:, CONV1 - 1:], half(n), ACT.Copy,
                after=(f"bc{n}", "padA.zero") + ((f"bc{n - 1}.tap3",) if n else ()))
            conv_tile(f"bc{n}", n, (f"bc{n}.pad",), BCT[:, n, :],
                      lambda i, j, n=n: bass.ds(8 * CONV1 + 4 + n if j is None else (4 + n) * CONV1 + j, 1))
        for g in range(GROUPS):
            p.add("pe", f"dk{g}", project(half(4), slot[4 + g], hT),
                  after=(f"pre.w{4 + g}",) + (("dk01",) if g else ()))
            for n in range(2):
                act(f"dk{g}{n}", dk[:, 2 * g + n, :], half(4), ACT.Copy, after=(f"dk{g}",))
        p.add("pe", "dv", project_tokens(half(0), slot[6]), after=("pre.w6", "bc0.pad"))
        for n in range(PAIRS):
            act(f"dv{n}", dv[:, n, :, :], view3(half(0), P)[:, :, n // 2 * HD:n // 2 * HD + HD], ACT.Copy, after=("dv",))
        def cumulate(e, i):
            up, up1 = C("upper"), C("upper", 2 * P)
            e.matmul(bank[5][:, 0:NH], up, LA[:, 0, :], start=True, stop=True)
            e.matmul(bank[5][:, NH:2 * NH], ones, LA[:, 0, :], start=True, stop=False)
            e.matmul(bank[5][:, NH:2 * NH], up, LA[:, 1, :], start=False, stop=True)
            e.matmul(bank[5][0:NH, 256:512], LA[:, 0, :], up1, start=True, stop=False)
            e.matmul(bank[5][0:NH, 384:512], LA[:, 1, :], up, start=False, stop=True)
            e.matmul(bank[6][0:40, 256:512], LF[:, 0, :], up1, start=True, stop=False)
            return e.matmul(bank[6][0:40, 384:512], LF[:, 1, :], up, start=False, stop=True)
        p.add("pe", "cum", cumulate, after=("LA", "LF1"))
        copy("dve", "acum", acum, view3(bank[5][:, 0:2 * NH], NH), after=("cum",))
        copy("dve", "acumT", acumT[0:NH, :], bank[5][0:NH, 256:512])
        copy("dve", "fcumT", fcumT[0:40, :], bank[6][0:40, 256:512], after=("fcumT.zero",))

        for g in range(GROUPS):
            cb = bank[1 + g][:, 0:3 * P]

            def cb_mm(e, i, g=g, cb=cb):
                e.matmul(cb[:, 0:T], BCT[:, g, 0:P], BCT[:, 2 + g, :], start=True, stop=True)
                return e.matmul(cb[:, T:], BCT[:, g, P:T], BCT[:, 2 + g, P:T], start=True, stop=True)
            p.add("pe", f"cb{g}", cb_mm, after=("bc3.silu",))
            for n in range(2):
                tt(f"cbt{g}{n}", CBT[:, 2 * g + n, :], cb, C("upper", 3 * P), ALU.mult, after=(f"cb{g}",))
        for n in range(4):
            freed[n] = f"bc{n}"
        freed[4], freed[5], freed[6] = "dk0", "dk1", "dv"
        pre_steps = ("bc3.silu", "fcumT", "dv3", "cbt11", "g.in", "sink")

        p.phase("heads", PAIRS)
        used[0] = block1_end
        qs = {b: carve(T) for b in "bcd"}
        ks = {b: carve(T) for b in "bcd"}
        vs = {b: carve(TT, P) for b in "bc"}
        vd = carve(TT, HD)
        am = carve(T)
        Pr = carve(3, SROW)
        PT = [carve(3 * P) for _ in range(3)]
        mx = carve(6)
        sm = carve(6)
        xsT = carve(T)
        xdt = carve(TT, P)
        zs = carve(T)
        zt = carve(T)
        dec = carve(3 * P)
        MT1 = carve(3 * P)
        yx = carve(T)
        adaW = [carve(D) for _ in range(2)]
        heads_end = used[0]

        NW = 17
        BQ, BK, BV, CQ, CK, CV, DQ, XS, ZS = range(9)
        ORDER = (BQ, BK, CQ, CK, DQ, BV, CV, XS, ZS)
        for n in ORDER:
            load(f"w{n}", n, lambda i, n=n: a["w_heads"][i * NW + n, :, :], prev=(f"proj{n}",))

        last_gate = {0: 6, 1: 7, 2: 5}

        def load_gate(j):
            s = 9 + j % 3
            load(f"w{9 + j}", s, lambda i: a["w_heads"][i * NW + (9 + j), :, :],
                 after=(f"proj{9 + j - 3}",) if j >= 3 else (), prev=() if j >= 3 else (f"proj{9 + last_gate[j]}",))
        for j in range(4):
            load_gate(j)
        def load_ada(n):
            p.dma(f"adaw{n}", lambda e, i: e.dma_start(adaW[n % 2], a["ada_w"][i * 6 + n, :, :]),
                  after=(f"ada{n - 2}",) if n >= 2 else (), prev=() if n >= 2 else (f"ada{n + 4}",))
        for n in range(3):
            load_ada(n)
        for j in range(4, 8):
            load_gate(j)
        for n in range(3, 6):
            load_ada(n)

        halves = {}
        count = [0]

        def proj(n, evac, token=False):
            h = count[0] % 2
            count[0] += 1
            s = n if n < 9 else 9 + (n - 9) % 3
            waits = (f"w{n}",) + ((halves[h],) if h in halves else pre_steps)
            p.add("pe", f"proj{n}", project_tokens(half(h), slot[s]) if token else project(half(h), slot[s], hT),
                  after=waits, prev=(last_halves[h],) if h not in halves else ())
            halves[h] = evac
            return half(h)

        last_halves = {0: "gate7", 1: "gate6"}

        def gate(j):
            o = proj(9 + j, f"gate{j}")
            act(f"gate{j}", lambda i: gates[:, bass.ds(i * 8 + j, 1), :], o.unsqueeze(1), ACT.Tanh,
                after=(f"proj{9 + j}",), scale=0.5)

        for b, q, k in (("b", BQ, BK), ("c", CQ, CK)):
            oq = proj(q, f"q{b}")
            act(f"q{b}", qs[b], oq, ACT.Copy, after=(f"proj{q}",), scale=HD ** -0.5)
            ok = proj(k, f"k{b}")
            copy("dve", f"k{b}", ks[b], ok, after=(f"proj{k}",))
        oq = proj(DQ, "qd")
        act("qd", qs["d"], oq, ACT.Copy, after=(f"proj{DQ}",), scale=HD ** -0.5)
        copy("pool", "kd", ks["d"], lambda i: dk[:, bass.ds(i, 1), :].rearrange("p a n -> p (a n)"), prev=("s.d1",),
             after=pre_steps)
        copy("pool", "vd", vd, lambda i: dv[:, bass.ds(i, 1), :, :].rearrange("p a b c -> p (a b) c"), prev=("pv.d1",))
        ov = proj(BV, "vb", token=True)
        copy("dve", "vb", vs["b"], view3(ov, P), after=(f"proj{BV}",))
        ov = proj(CV, "vc", token=True)
        copy("dve", "vc", vs["c"], view3(ov, P), after=(f"proj{CV}",))

        S = {b: bank[2 + n] for n, b in enumerate("bcd")}

        def forget(hh):
            last = (f"s.c{hh - 1}",) if hh else ()
            ts(f"rf{hh}", rf[0:NH, :], fcumT[0:NH, :],
               lambda i: cst[0:NH, bass.ds(i * 2 + (CCOL["pick"] + hh), 1)], None, ALU.mult,
               after=last + ("rf.ones", "lf.ones", "fcumT"), prev=() if hh else ("s.c1",))
            ts(f"lf{hh}", lf[32:40, :], fcumT[32:40, :],
               lambda i: cst[32:40, bass.ds(i * 2 + (CCOL["pick"] + hh), 1)], None, ALU.mult)

        def scores(b, hh):
            lo = hh * HD
            q, k, o = qs[b], ks[b], S[b]

            def emit(e, i):
                r = {"b": i * 2 + hh, "c": 2 * NH, "d": i * 2 + (NH + hh)}[b]
                for t in range(TT):
                    at, n = (0, P) if t == 0 else (P + 1, T)
                    if b == "c":
                        bias = Hk[:, r, T - n:LOGIT]
                    else:
                        bias = Hk[:, bass.ds(r, 1), T - n:LOGIT].rearrange("p a n -> p (a n)")
                    e.matmul(o[:, at:at + n + 1], flip, bias, start=True, stop=False)
                    if b == "c":
                        e.matmul(o[:, at:at + n], lf[:, t * P:(t + 1) * P], rf[:, 0:n], start=False, stop=False)
                    last = e.matmul(o[:, at:at + n], q[lo:lo + HD, t * P:(t + 1) * P], k[lo:lo + HD, 0:n],
                                    start=False, stop=True)
                return last
            ready = {"b": ("qb", "kb"), "c": ("qc", "kc", f"lf{hh}"), "d": ("qd", "kd")}[b]
            free = (f"e.{b}0.1", "yx") if hh else ()
            p.add("pe", f"s.{b}{hh}", emit, after=ready + free + pre_steps, prev=() if hh else (f"e.{b}1.1", "y.ssd"))

        def softmax(hh):
            for n, b in enumerate("bcd"):
                for t in range(TT):
                    cols = S[b][:, 0:P + 1] if t == 0 else S[b][:, P + 1:SROW]
                    p.add("dve", f"mx.{b}{hh}{t}", lambda e, i, n=n, t=t, cols=cols: e.tensor_reduce(
                        mx[:, 2 * n + t:2 * n + t + 1], cols, AX.X, ALU.max, negate=True),
                        after=(f"s.{b}{hh}",) + ((f"e.{b}0.{t}",) if hh else ()), prev=() if hh else (f"e.{b}1.{t}",))
            for n, b in enumerate("bcd"):
                for t in range(TT):
                    cols = slice(0, P + 1) if t == 0 else slice(P + 1, SROW)
                    act(f"e.{b}{hh}.{t}", Pr[:, n, cols], S[b][:, cols], ACT.Exp,
                        after=(f"mx.{b}{hh}1",) + ((f"t.{b}0",) if hh else ()), prev=() if hh else (f"t.{b}1",),
                        bias=mx[:, 2 * n + t:2 * n + t + 1], accum_out=sm[:, 2 * n + t:2 * n + t + 1])
                p.add("dve", f"r.{b}{hh}", lambda e, i, n=n: e.reciprocal(sm[:, 2 * n:2 * n + 2], sm[:, 2 * n:2 * n + 2]),
                      after=(f"e.{b}{hh}.1",))
                for t in range(TT):
                    at, m = (0, P) if t == 0 else (P + 1, T)
                    ts(f"p.{b}{hh}.{t}", Pr[:, n, at:at + m], Pr[:, n, at:at + m], sm[:, 2 * n + t:2 * n + t + 1],
                       None, ALU.mult, after=(f"r.{b}{hh}",))

        def turn_p(hh):
            for n, b in enumerate("bcd"):
                tb = bank[5 + n % 2]

                def emit(e, i, n=n, tb=tb):
                    e.transpose(tb[:, 0:P], Pr[:, n, 0:P], ident)
                    e.transpose(tb[:, P:T], Pr[:, n, P + 1:T + 1], ident)
                    return e.transpose(tb[:, T:3 * P], Pr[:, n, T + 1:SROW - 1], ident)
                before = {0: ("pt.d0", "yt.c0") if hh else (), 1: ("pt.c0", "yt.d0") if hh else (), 2: (f"pt.b{hh}",)}[n]
                back = {0: () if hh else ("pt.d1", "yt.c1"), 1: () if hh else ("pt.c1", "yt.d1"), 2: ()}[n]
                p.add("pe", f"t.{b}{hh}", emit, after=(f"p.{b}{hh}.1",) + before, prev=back)
                o = PT[n]
                if b == "c":
                    copy("dve", f"pt.{b}{hh}", o, tb[:, 0:3 * P], after=(f"t.{b}{hh}",) + ((f"pv.{b}0",) if hh else ()),
                         prev=() if hh else (f"pv.{b}1",))
                else:
                    act(f"pt.{b}{hh}", o, tb[:, 0:3 * P], ACT.Copy, after=(f"t.{b}{hh}",) + ((f"pv.{b}0",) if hh else ()),
                        prev=() if hh else (f"pv.{b}1",))

        O = {"b": bank[7][:, 0:T], "c": bank[5][:, 0:T], "d": bank[6][:, 0:T]}

        def weigh(hh):
            lo = hh * HD
            for n, b in enumerate("bcd"):
                def emit(e, i, n=n, b=b):
                    v0, v1 = (vd[:, 0, :], vd[:, 1, :]) if b == "d" else \
                        (vs[b][:, 0, lo:lo + HD], vs[b][:, 1, lo:lo + HD])
                    e.matmul(O[b][lo:lo + HD, :], v0, PT[n][:, 0:T], start=True, stop=False)
                    return e.matmul(O[b][lo:lo + HD, P:T], v1, PT[n][:, T:3 * P], start=False, stop=True)
                ready = {"b": ("vb",), "c": ("vc", f"pt.d{hh}"), "d": ("vd", f"pt.c{hh}")}[b]
                p.add("pe", f"pv.{b}{hh}", emit, after=(f"pt.{b}{hh}",) + ready, prev=(f"yt.{b}1",) if hh == 0 else ())
                act(f"yt.{b}{hh}", lambda i, n=n: YT[1 + n][lo:lo + HD, bass.ds(i, 1), :], O[b][lo:lo + HD, :].unsqueeze(1),
                    ACT.Copy, after=(f"pv.{b}{hh}",), scale=0.5)

        def ada(n):
            third = adaA[:, n % 3 * D:(n % 3 + 1) * D]
            stt(f"ada{n}", third, adaW[n % 2], lambda i: sc[:, bass.ds(i * 2 + n // 3, 1)], third, ALU.mult, ALU.add,
                after=(f"adaw{n}", "sc", "ada.zero"))

        forget(0)
        for b in "bcd":
            scores(b, 0)
        softmax(0)
        ox = proj(XS, "xpad")
        act("xpad", pad1[:, CONV1 - 1:], ox, ACT.Copy, after=(f"proj{XS}", "bc3.silu"), prev=("xs.tap3",))
        conv_tile("xs", 0, ("xpad",), xsT,
                  lambda i, j: bass.ds(i + 8 * CONV1, 1) if j is None else bass.ds(i * CONV1 + j, 1))
        oz = proj(ZS, "zs")
        act("zt", zt, oz, ACT.Tanh, after=(f"proj{ZS}",), prev=("zs",), scale=0.5)
        stt("zs", zs, zt, 1.0, oz, ALU.add, ALU.mult, after=("zt",))
        gate(0)
        turn_p(0)
        def turn_x(e, i):
            e.transpose(bank[2][:, 0:P], xsT[:, 0:P], ident)
            return e.transpose(bank[2][:, P:T], xsT[:, P:T], ident)
        p.add("pe", "turn.x", turn_x, after=("xs.silu", "e.b0.1"))
        for hh in range(2):
            for t in range(TT):
                ts(f"xdt{hh}{t}", xdt[:, t, hh * HD:hh * HD + HD], bank[2][:, t * P + hh * HD:t * P + hh * HD + HD],
                   lambda i, hh=hh, t=t: dtc[:, t, bass.ds(i * 2 + hh, 1)], None, ALU.mult, after=("turn.x",))
        gate(1)
        for hh in range(2):
            lo = hh * HD
            ts(f"am{hh}", am[0:NH, :], acumT[0:NH, :], lambda i, hh=hh: cst[0:NH, bass.ds(i * 2 + (CCOL["pick"] + hh), 1)],
               None, ALU.mult, after=("rowb0",) if hh else (), prev=() if hh else ("rowb1",))
            rb = bank[3][:, 0:T]
            p.add("pe", f"rowb{hh}", lambda e, i, rb=rb: e.matmul(rb, ones[0:NH, :], am[0:NH, :], start=True, stop=True),
                  after=(f"am{hh}", "e.c0.1") + (("d1.0",) if hh else ()))
            for t, (at, n) in enumerate(((0, T), (T, P))):
                ts(f"d{t}.{hh}", dec[:, at:at + n], rb[:, T - n:T], lambda i, hh=hh, t=t: acum[:, t, bass.ds(i * 2 + hh, 1)],
                   0.0, ALU.subtract, ALU.min, after=(f"rowb{hh}",) + (("m0",) if hh else ()))
            act(f"dexp{hh}", dec, dec, ACT.Exp, after=(f"d1.{hh}",))
            tt(f"m{hh}", MT1, dec, lambda i: CBT[:, bass.ds(i, 1), :].rearrange("p a n -> p (a n)"), ALU.mult,
               after=(f"dexp{hh}",) + (("y0",) if hh else ()))
            gate(2 + hh)

            def y_mm(e, i, lo=lo):
                o = bank[4][lo:lo + HD, 0:T]
                e.matmul(o, xdt[:, 0, lo:lo + HD], MT1[:, 0:T], start=True, stop=False)
                return e.matmul(o[:, P:T], xdt[:, 1, lo:lo + HD], MT1[:, T:3 * P], start=False, stop=True)
            p.add("pe", f"y{hh}", y_mm, after=(f"m{hh}", "xdt11", "e.d0.1"))
        ada(0)
        ada(1)
        stt("yx", yx, xsT, lambda i: par[:, bass.ds(i + PCOL["d_skip"], 1)], bank[4][:, 0:T], ALU.mult, ALU.add, after=("y1",))
        tt("y.ssd", lambda i: YT[0][:, bass.ds(i, 1), :], yx.unsqueeze(1), zs.unsqueeze(1), ALU.mult, after=("yx", "zs"))


        forget(1)
        for b in "bcd":
            scores(b, 1)
        softmax(1)
        weigh(0)
        ada(2)
        ada(3)
        gate(4)
        gate(5)
        turn_p(1)
        ada(4)
        ada(5)
        gate(6)
        weigh(1)
        gate(7)
        freed.update({n: f"proj{n}" for n in range(9)})
        freed.update({9 + n: f"proj{9 + last_gate[n]}" for n in range(3)})

        p.phase("ssd norm")
        used[0] = block1_end
        sqs = carve(W // P, T)
        rsb = carve(T)
        mod = small[:, 0:24]
        gs = small[:, 24:32]
        a0h, oka = small[:, 32:40], small[:, 40:48]

        def ada_mm(e, i):
            for j in range(24):
                last = e.matmul(bank[4][:, j:j + 1], adaA[:, j * P:(j + 1) * P], ones[:, 0:1], start=True, stop=True)
            return last
        p.add("pe", "mod.mm", ada_mm, after=("ada5", "y.ssd"))
        tt("mod", mod, bank[4][:, 0:24], par[:, PCOL["ada_b"]:PCOL["ada_b"] + 24], ALU.add, after=("mod.mm",))
        stt("gs", gs, mod[:, KT:2 * KT], 1.0, par[:, PCOL["norm_g"]:PCOL["norm_g"] + KT], ALU.add, ALU.mult)
        ts("a0h", a0h, par[:, PCOL["a0"]:PCOL["a0"] + KT], 0.5, None, ALU.mult)
        ts("oka", oka, par[:, PCOL["k_a"]:PCOL["k_a"] + KT], -1.0, 1.0, ALU.mult, ALU.add)

        tt("ya.sq", sqs, YT[0], YT[0], ALU.mult, after=("y.ssd", "pv.d1"))

        def mean_mm(e, i, psum=bank[0][:, 0:T], src=sqs, n=W // P, w=None):
            for k in range(n):
                last = e.matmul(psum, w if w is not None else ones, src[:, k, :], start=k == 0, stop=k == n - 1)
            return last
        p.add("pe", "ya.sum", mean_mm, after=("ya.sq", "gate7"))
        ts("ya.ms", rsb, bank[0][:, 0:T], 1.0 / W, 4e-6, ALU.mult, ALU.add, after=("ya.sum",))
        act("ya.sd", rsb, rsb, ACT.Sqrt, after=("ya.ms",))
        p.add("dve", "ya.rs", lambda e, i: e.reciprocal(rsb, rsb), after=("ya.sd",))
        ts("ya.half", rsb, rsb, 0.5, None, ALU.mult, after=("ya.rs",))
        for k in range(W // P):
            stt(f"ya.y{k}", YT[0][:, k, :], YT[0][:, k, :], PC("ssm_norm", k), rsb, ALU.mult, ALU.mult, after=("ya.half",))

        p.phase("mix", KT)
        mixT = carve(KT, T)
        tb = [carve(T) for _ in range(N_BR)]
        for s in (1, 2, 3, 0):
            load(f"wb{s}", s, lambda i, s=s: a["w_br"][i * 4 + s, :, :], prev=(f"br{s}",), width=W)
        for b in (1, 2, 3, 0):
            p.add("pe", f"br{b}", project(half(b), slot[b][:, 0:W], YT[b], kt=W // P), after=(f"wb{b}", "yt.d1") + (("ya.y3",) if b == 0 else ()),
                  prev=(f"br{b}.gate",))
            stt(f"br{b}.gate", tb[b].unsqueeze(1), lambda i, b=b: gates[:, bass.ds(i + b * KT, 1), :], 1.0,
                half(b).unsqueeze(1), ALU.add, ALU.mult, after=(f"br{b}",), prev=("mix",) if b == 1 else ())
            if b == 3:
                tt("mix23", tb[2], tb[2], tb[3], ALU.add, after=("br3.gate",), eng="pool")
        tt("mix01", tb[0], tb[0], tb[1], ALU.add, after=("br0.gate",), eng="pool")
        tt("mix", lambda i: mixT[:, bass.ds(i, 1), :], tb[0].unsqueeze(1), tb[2].unsqueeze(1), ALU.add, after=("mix01",),
           eng="pool")
        freed.update({s: f"br{s}" for s in range(4)})

        p.phase("w_out")
        quarter = [(t, h) for t in range(TT) for h in range(2)]

        def residual(name, after, banks):
            def emit(e, i):
                for n, (t, h) in enumerate(quarter):
                    last = e.matmul(banks[n][:, :], ident, x[:, t, h * 512:(h + 1) * 512], start=True, stop=False)
                return last
            p.add("pe", name, emit, after=after)

        def rows_times(w, lhs, banks, stop):
            def emit(e, i):
                for n, (t, h) in enumerate(quarter):
                    last = e.matmul(banks[n][:, :], lhs[:, t * P:(t + 1) * P], w[:, h * 512:(h + 1) * 512],
                                    start=False, stop=stop)
                return last
            return emit
        residual("x.in", ("mix",), bank[4:8])
        for k in range(KT):
            s = 4 + k
            load(f"wo{k}", s, lambda i, k=k: a["w_out"][k * P:(k + 1) * P, :])
            p.add("pe", f"out{k}", rows_times(slot[s], mixT[:, k, :], bank[4:8], k == KT - 1), after=(f"wo{k}",))
            freed[s] = f"out{k}"
        for n, (t, h) in enumerate(quarter):
            o = x[:, t, h * 512:(h + 1) * 512]
            if n % 2:
                act(f"x1.{n}", o, bank[4 + n][:, :], ACT.Copy, after=("out7",))
            else:
                copy("dve", f"x1.{n}", o, bank[4 + n][:, :], after=("out7",))

        p.phase("ffn norm")
        token_norm("norm2", "norm_ffn", hT, after=("x1.2", "x1.3"))
        residual("x1.in", ("x1.2", "x1.3"), bank[4:8])
        FF_STEP = 2
        FF_TRIPS = FF_TILES // FF_STEP
        ud = [carve(T) for _ in range(FF_STEP)]
        gu = [carve(T) for _ in range(FF_STEP)]
        tg = [carve(T) for _ in range(FF_STEP)]

        def ffn(last):
            for f in range(FF_STEP):
                for n, what in enumerate(("g", "u")):
                    load(f"w{what}{f}", 3 * f + n, lambda i, f=f, n=n: a["w_gu"][i * 2 * FF_STEP + (2 * f + n), :, :],
                         prev=(f"{what}{f}",))
                load(f"wd{f}", 3 * f + 2, lambda i, f=f: a["w_down"][bass.ds(i * FF_STEP * P + f * P, P), :],
                     prev=(f"down{f}",))
            for f in range(FF_STEP):
                for n, what in enumerate(("g", "u")):
                    p.add("pe", f"{what}{f}", project(half(2 * f + n), slot[3 * f + n], hT),
                          after=(f"w{what}{f}", "norm2.h7"), prev=(f"tg2.{f}" if what == "g" else f"ud{f}",))
                act(f"tg{f}", tg[f], half(2 * f), ACT.Tanh, after=(f"g{f}",), prev=(f"tg2.{f}",), scale=0.5)
                act(f"ud{f}", ud[f], half(2 * f + 1), ACT.Copy, after=(f"u{f}",), prev=(f"gu{f}",), scale=0.5)
                stt(f"tg2.{f}", tg[f], tg[f], 1.0, half(2 * f), ALU.add, ALU.mult, after=(f"tg{f}",))
                tt(f"gu{f}", gu[f], tg[f], ud[f], ALU.mult, after=(f"tg2.{f}", f"ud{f}"), prev=(f"down{f}",))
            for f in range(FF_STEP):
                p.add("pe", f"down{f}", rows_times(slot[3 * f + 2], gu[f], bank[4:8], last and f == FF_STEP - 1),
                      after=(f"wd{f}", f"gu{f}"))
        p.phase("ffn", FF_TRIPS - 1)
        ffn(False)
        p.phase("ffn end", at=FF_TRIPS - 1, peel=".end")
        ffn(True)
        for f in range(FF_STEP):
            freed[3 * f], freed[3 * f + 1], freed[3 * f + 2] = f"g{f}.end", f"u{f}.end", f"down{f}.end"
        p.phase("x2")
        for n, (t, h) in enumerate(quarter):
            o = x[:, t, h * 512:(h + 1) * 512]
            if n % 2:
                act(f"x2.{n}", o, bank[4 + n][:, :], ACT.Copy, after=("down1.end",))
            else:
                copy("dve", f"x2.{n}", o, bank[4 + n][:, :], after=("down1.end",))

        p.phase("block 2 norm")
        used[0] = 0
        YR, CU, OG, GC, GR = (carve(KT, T) for _ in range(5))
        TW, AL = carve(T), carve(T)
        rsc = carve(T)
        w0 = carve(D)
        cst2 = carve(NCCOL - NFIRST)
        padz = carve(1 + T)
        squares = OG
        low = carve(T)
        pads = {n: carve(1 + T) for n in ("r", "k", "v")}
        Az = [carve(T) for _ in range(2)]
        Rz = [carve(T) for _ in range(2)]
        block2_end = used[0]
        p.dma("cst2", lambda e, i: e.dma_start(cst2, a["cst"][:, NFIRST:NCCOL]), after=("x2.2", "x2.3"))
        p.dma("w0row", lambda e, i: e.dma_start(w0[0:1, :], a["w0"]), after=("x2.2", "x2.3"))
        load("wlora", 0, lambda i: a["w_lora"])
        token_norm("norm3", "norm_final", x3T, after=("x2.2", "x2.3"))

        def mean_over_channels(tag, src, b, after):
            def emit(e, i):
                for k in range(KT):
                    last = e.matmul(bank[b][:, 0:T], ones, src[:, k, :], start=k == 0, stop=k == KT - 1)
                return last
            p.add("pe", tag, emit, after=after)

        for k in range(KT):
            act(f"norm4.sq{k}", squares[:, k, :], x3T[:, k, :], ACT.Square, after=(f"norm3.h{k}",))
            p.add("pe", f"norm4.sum{k}", lambda e, i, k=k: e.matmul(bank[5][:, 0:T], ones, squares[:, k, :],
                  start=k == 0, stop=k == KT - 1), after=(f"norm4.sq{k}",))
        ts("norm4.ms", rsc, bank[5][:, 0:T], 1.0 / D, 1e-6, ALU.mult, ALU.add, after=(f"norm4.sum{KT - 1}",))
        act("norm4.sd", rsc, rsc, ACT.Sqrt, after=("norm4.ms",))
        p.add("dve", "norm4.rs", lambda e, i: e.reciprocal(rsc, rsc), after=("norm4.sd",))
        for k in range(KT):
            stt(f"norm4.h{k}", hT[:, k, :], x3T[:, k, :], gs[:, k:k + 1], rsc, ALU.mult, ALU.mult, after=("norm4.rs",))
            act(f"norm4.s{k}", hT[:, k, :], hT[:, k, :], ACT.Identity, after=(f"norm4.h{k}",), bias=mod[:, k:k + 1])

        p.add("pool", "TW.zero", lambda e, i: e.memset(TW, 0.0), after=("norm3.h7",))
        p.add("pool", "AL.zero", lambda e, i: e.memset(AL, 0.0))
        for n in "rkv":
            p.add("pool", f"pad.{n}.zero", lambda e, i, n=n: e.memset(pads[n], 0.0))
        for n, z in (("Az", Az), ("Rz", Rz)):
            for hh in range(2):
                p.add("pool", n + ".zero" if hh else n + "0.zero", lambda e, i, z=z, hh=hh: e.memset(z[hh], 0.0))
        p.add("pool", "pad2.zero", lambda e, i: e.memset(padA[:, :], 0.0))
        p.add("pool", "padz.zero", lambda e, i: e.memset(padz, 0.0))
        for k in range(KT):
            p.add("pe", f"lora{k}", lambda e, i, k=k: e.matmul(half(0), slot[0][:, k * P:(k + 1) * P], hT[:, k, :],
                  start=k == 0, stop=k == KT - 1), after=("wlora", f"norm4.s{k}"))
        freed[0] = "lora7"
        act("lora.pad", padz[:, 1:], half(0), ACT.Copy, after=("lora7", "padz.zero"))
        tt("lora.d", low, padz[:, 0:T], padz[:, 1:], ALU.subtract, after=("lora.pad",))
        stt("lora.s", low, low, PC("mu", 24), padz[:, 1:], ALU.mult, ALU.add)
        act("TW", TW[0:HD, :], low[0:HD, :], ACT.Tanh, after=("lora.s", "TW.zero"))
        copy("dve", "AL", AL[HD:P, :], low[HD:P, :], after=("AL.zero",))

        XW = {n: carve(T) for n in "rkv"}
        aT, kkr, kk, rn, t1, kp, bT = (carve(T) for _ in range(7))
        lw = carve(T)
        ex = carve(2 * T)
        en = carve(T)
        eT = carve(1)
        odd = carve(T)
        Bf, Kf = carve(T), carve(T)
        Nt, Mt, RBt, RKt = (carve(4, P) for _ in range(4))
        Nm = [carve(4, P) for _ in range(2)]
        Xs, Zs, Gs = (carve(4, P) for _ in range(3))
        tok = carve(4, P)
        Fs, Us, St = carve(P), carve(TT, P), carve(HD)
        bonus, Oc, osq, grs, rg, hv, cth = (carve(T) for _ in range(7))
        lo2 = carve(P)

        def off(l):
            return cst2[:, P + l * P:P + (l + 1) * P]

        def four(ap):
            return ap.unsqueeze(1).to_broadcast([P, 4, P])

        def pi(name, plus=0):
            return lambda i: par[:, bass.ds(i + (PCOL[name] + plus), 1)]

        rT, kT, vT = (XW[n] for n in "rkv")
        eI, eE = ex[:, 0:T], ex[:, T:2 * T]
        mid = cst[:, CCOL["mid"]:CCOL["mid"] + 2]
        NR = 9
        VAL, GATE, OGP, ROG, GCP, GRP = range(3, NR)

        def k_steps(name, n, b, k0, k1, after=(), prev=()):
            def emit(e, i):
                for k in range(k0, k1):
                    last = e.matmul(half(b), slot[n][:, k * P:(k + 1) * P], hT[:, k, :], start=k == 0, stop=k == KT - 1)
                return last
            p.add("pe", name, emit, after=after, prev=prev)

        def low_rank(next_, free):
            def low_mm(e, i):
                for t in range(TT):
                    o = bank[4][:, t * P:(t + 1) * P]
                    e.matmul(o, TW[:, t * P:(t + 1) * P], lo2, start=True, stop=False)
                    e.matmul(o, ones[0:1, :], w0[0:1, bass.ds((i + next_) * P, P)], start=False, stop=True)
                return e.matmul(bank[4][:, T:2 * T], lo2, AL, start=True, stop=True)
            p.add("pe", "low.mm", low_mm, after=("lo2", "TW", "w0row", "AL") + free, prev=("eT",))
            act("lw.tanh", lw, bank[4][:, 0:T], ACT.Tanh, after=("low.mm",), scale=0.5)
            act("a.tanh", aT, bank[4][:, T:2 * T], ACT.Tanh, after=("low.mm",), prev=("b",),
                bias=lambda i: a0h[:, bass.ds(i + next_, 1)], scale=0.5)

        def decays(next_):
            ts("lw", lw, lw, -0.5 * DECAY, -0.5 * DECAY, ALU.mult, ALU.add, after=("lw.tanh",))
            ts("a", aT, aT, 0.5, 0.5, ALU.mult, ALU.add, after=("a.tanh",), lag=2)

            def cw_mm(e, i):
                for m, tri in enumerate((C("upper"), C("strict"))):
                    for c in range(TT):
                        end = e.matmul(bank[4][:, m * T + c * P:m * T + c * P + P], lw[:, c * P:(c + 1) * P], tri,
                                       start=True, stop=True)
                return end
            p.add("pe", "cw.mm", cw_mm, after=("lw", "a.tanh"))
            act("en", en, bank[4][:, 0:T], ACT.Exp, after=("cw.mm",), prev=("B", "K"), bias=mid[:, 0:1], scale=-1.0)
            act("ex", ex, bank[4][:, :], ACT.Exp, prev=("R1", "A1"), bias=mid[:, 1:2])

        def whole_decay(free=()):
            act("eT", eT, bank[4][:, P - 1:P], ACT.Exp, after=("cw.mm",) + free)

        def shifts(next_, free):
            for n in "rkv":
                yield lambda n=n: tt(f"sd.{n}", XW[n], pads[n][:, 0:T], pads[n][:, 1:], ALU.subtract,
                                     after=(f"pad.{n}", "pad.v.zero") + free)
            for j, n in enumerate("rkv"):
                yield lambda j=j, n=n: stt(f"sh.{n}", XW[n], XW[n], lambda i: par[:, bass.ds(i + (next_ + PCOL["mu"] + 8 * j), 1)],
                                           pads[n][:, 1:], ALU.mult, ALU.add)

        def kk_norm(next_, free):
            yield lambda: ts("kkr", kkr, kT, pi("k_k", next_), None, ALU.mult)
            yield lambda: tt("kk.sq", rn, kkr, kkr, ALU.mult)

            def total():
                p.add("pe", "kk.sum", lambda e, i: e.matmul(bank[5][:, 0:T], C("pair"), rn, start=True, stop=True),
                      after=("kk.sq",) + free)
                act("kk.norm", rn, bank[5][:, 0:T], ACT.Sqrt, after=("kk.sum",))
            yield total

        def operands(next_, free_k, free_a):
            yield lambda: ts("t1", t1, aT, pi("k_a", next_), lambda i: oka[:, bass.ds(i + next_, 1)], ALU.mult, ALU.add)
            yield lambda: tt("kp", kp, kT, t1, ALU.mult)
            yield lambda: tt("K", Kf, kp, en, ALU.mult, after=("en",) + free_k)
            yield lambda: ts("kk.max", rn, rn, 1e-12, None, ALU.max, after=("kk.norm",))
            yield lambda: p.add("dve", "kk.rn", lambda e, i: e.reciprocal(rn, rn))
            yield lambda: tt("kk", kk, kkr, rn, ALU.mult)
            yield lambda: tt("b", bT, kk, aT, ALU.mult)
            yield lambda: tt("B", Bf, bT, en, ALU.mult)
            for hh in range(2):
                r = slice(hh * HD, hh * HD + HD)
                yield lambda hh=hh, r=r: stt(f"A{hh}", Az[hh][r, :], kk[r, :], -1.0, eE[r, :], ALU.mult, ALU.mult,
                                             after=("ex", "Az.zero", "Rz.zero") + free_a, lag=2)

        def receptances(free):
            for hh in range(2):
                r = slice(hh * HD, hh * HD + HD)
                tt(f"R{hh}", Rz[hh][r, :], rT[r, :], eI[r, :], ALU.mult, after=("ex", "Rz.zero") + free)

        def mask(l, eng="pool", after=()):
            tt(f"Nm{l}", Nm[l % 2], Nt, four(off(l)), ALU.mult, after=after, eng=eng)

        def n_products(loop):
            products("N.mm", 2, Bf, Az, ("A1", "B") + (("F1",) if loop else ()))
            products("N1.mm", 3, Az, Bf, ("U1",) if loop else ())
            act("N", Nt, quad(2), ACT.Copy, after=("N.mm",) + (("Nm6",) if loop else ()))

        def bonus_operand(next_):
            stt("rkr", t1, rT, pi("r_k", next_), kp, ALU.mult, ALU.mult, lag=2)

        def level_zero(loop):
            tt("X0.m", Xs, quad(3), four(cst2[:, 0:P]), ALU.mult, after=("N1.mm",))
            tt("X0", Xs, Xs, four(ident), ALU.add)
            tt("Z0.m", Zs, Nt, four(off(0)), ALU.mult, after=("N",) + (("U1.mm",) if loop else ()), eng="pool")
            tt("Z0", Zs, Zs, four(ident), ALU.add, eng="pool")
            mask(1, "dve", ("N",) + (("G5.mm",) if loop else ()))
            mask(2, "pool", ("G6.mm",) if loop else ())

        def products(name, b, lhs, rhs, after, prev=()):
            def emit(e, i):
                for q in range(4):
                    hh, c = q // 2, slice(q % 2 * P, q % 2 * P + P)
                    l = lhs[hh] if isinstance(lhs, list) else lhs
                    r = rhs[hh] if isinstance(rhs, list) else rhs
                    last = e.matmul(bank[b][:, q * P:(q + 1) * P], l[:, c], r[:, c], start=True, stop=True)
                return last
            p.add("pe", name, emit, after=after, prev=prev)

        def quad(b):
            return view3(bank[b][:, :], P)

        p.phase("first rkv", peel=".first")
        for j, n in enumerate("rkv"):
            load(f"rw{j}", j, lambda i, j=j: a["w_rwkv"][j, :, :])
            k_steps(f"rp{j}", j, j % 2, 0, KT, after=(f"rw{j}", "norm4.s7", "lora.pad") + (("pad.r",) if j == 2 else ()))
            freed[j] = f"rp{j}.first"
            act(f"pad.{n}", pads[n][:, 1:], half(j % 2), ACT.Copy, after=(f"rp{j}", f"pad.v.zero"))
        p.dma("lo2", lambda e, i: e.dma_start(lo2, a["lora2"][0, :, :]), after=("norm3.h7",))
        low_rank(0, ())
        decays(0)
        whole_decay()
        for step in (*shifts(0, ()), *kk_norm(0, ()), *operands(0, (), ())):
            step()
        n_products(False)
        receptances(())
        products("RK.mm", 4, Kf, Rz, ("K", "R1", "eT"))
        level_zero(False)
        bonus_operand(0)

        def rwkv(last):
            for n in range(3, NR):
                load(f"rw{n}", n, lambda i, n=n: a["w_rwkv"][i * NR + n, :, :], prev=(f"rp{n}.{KT}",))
                if n == 3 and not last:
                    p.dma("lo2", lambda e, i: e.dma_start(lo2, a["lora2"][i + 1, :, :]), after=("low.mm.first",), prev=("low.mm",))
            if not last:
                for n in range(3):
                    load(f"rw{n}", n, lambda i, n=n: a["w_rwkv"][i * NR + (n + NR), :, :], prev=(f"rp{n}.{KT}",))

            queue = []
            reader = {}

            def queued(n, evac, reads):
                b = len(queue) // KT % 2
                for k in range(KT):
                    queue.append((n, b, k, evac if k == KT - 1 else None,
                                  (reader[b],) if b in reader else (), () if b in reader else ({0: "gr", 1: "gc"}[b],)))
                reader[b] = reads

            def fill(n):
                while n and queue:
                    s, b, k, evac, before, back = queue[0]
                    m = min(n, sum(1 for q in queue[:KT] if q[0] == s))
                    first = ("pad.k.first", "pad.v.first") if k == 0 and back else ()
                    k_steps(f"rp{s}.{k + m}", s, b, k, k + m, after=(f"rw{s}",) + before + first, prev=back)
                    evac = queue[m - 1][3]
                    del queue[:m]
                    n -= m
                    if evac:
                        evac(half(b))

            def later(step):
                if last:
                    step()
                else:
                    side.insert(2, step)

            def store_tanh(name, dst, n, then=None):
                def evac(o):
                    act(name if then is None else name + ".th", dst, o.unsqueeze(1), ACT.Tanh, after=(f"rp{n}.{KT}",), scale=0.5)
                    if then:
                        later(lambda: stt(name, dst, dst, 1.0, o.unsqueeze(1), ALU.add, ALU.mult, after=(name + ".th",)))
                return evac

            def gate_evac(o):
                act("conv.th", cth, o, ACT.Tanh, after=(f"rp{GATE}.{KT}",), prev=("conv.u",), scale=0.5)
                stt("conv.u", padA[:, CONV2 - 1:], cth, 1.0, hv, ALU.add, ALU.mult, after=("conv.th", "hv", "pad2.zero"))

            def rog_evac(o):
                act("rg.th", rg, o, ACT.Tanh, after=(f"rp{ROG}.{KT}",), prev=("YR",), scale=0.5)
                later(lambda: stt("rg", rg, rg, 1.0, o, ALU.add, ALU.mult, after=("rg.th",)))
            queued(VAL, lambda o: act("hv", hv, o, ACT.Copy, after=(f"rp{VAL}.{KT}",), prev=("conv.u",), scale=0.5), "hv")
            queued(GATE, gate_evac, "conv.th")
            if not last:
                for j, n in enumerate("rkv"):
                    queued(j, lambda o, j=j, n=n: act(f"pad.{n}", pads[n][:, 1:], o, ACT.Copy, after=(f"rp{j}.{KT}", "sh.v.first"),
                                                     prev=(f"sh.{n}",)), f"pad.{n}")
            queued(OGP, store_tanh("og", lambda i: OG[:, bass.ds(i, 1), :], OGP, True), "og")
            queued(ROG, rog_evac, "rg")
            queued(GCP, store_tanh("gc", lambda i: GC[:, bass.ds(i, 1), :], GCP), "gc")
            queued(GRP, store_tanh("gr", lambda i: GR[:, bass.ds(i, 1), :], GRP), "gr")

            products("M.mm", 6, Kf, Az, ("B.first",), ("St",))

            def turn_tok(e, i):
                for n, src in enumerate((Bf[:, 0:P], Kf[:, 0:P], vT[:, 0:P], vT[:, P:T])):
                    end = e.transpose(bank[5][:, n * P:(n + 1) * P], src, ident)
                return end

            def bonus_products():
                products("RB.mm", 7, Bf, Rz, ("R1.first",), ("O.copy",))
                p.add("pe", "bonus.sum", lambda e, i: e.matmul(bank[5][:, 0:T], C("pair"), t1, start=True, stop=True),
                      after=("rkr.first", "kk.norm.first"), prev=("gn.ms", "rkr"))

            def turn_and_mask():
                tt("M", Mt, quad(6), four(C("strict")), ALU.mult, after=("M.mm",), lag=2)
                tt("bonus", bonus, vT, bank[5][:, 0:T], ALU.mult, after=("bonus.sum",), lag=2)
                p.add("pe", "turn.tok", turn_tok, after=("bonus",))
                act("tok", tok, quad(5), ACT.Copy, after=("turn.tok",))

            def tap(j):
                w = lambda i: par[:, bass.ds(i * CONV2 + (PCOL["conv_k"] + j), 1)]
                o = odd.unsqueeze(1) if j % 2 else lambda i: CU[:, bass.ds(i, 1), :]
                src = padA[:, j:j + T].unsqueeze(1)
                if j == 0:
                    ts("tap0", o, src, w, pi("conv_b2"), ALU.mult, ALU.add)
                elif j == 1:
                    ts("tap1", o, src, w, None, ALU.mult, lag=2)
                else:
                    stt(f"tap{j}", o, src, w, o, ALU.mult, ALU.add, lag=2)
            side = [lambda: tt("RB", RBt, quad(7), four(C("upper")), ALU.mult, after=("RB.mm",)),
                    lambda: tt("RK", RKt, quad(4), four(C("upper")), ALU.mult,
                               after=("RK.mm.first",), prev=("RK.mm",), lag=2)]
            taps = [lambda j=j: tap(j) for j in range(CONV2)]
            taps.append(lambda: tt("taps", lambda i: CU[:, bass.ds(i, 1), :], lambda i: CU[:, bass.ds(i, 1), :],
                                   odd.unsqueeze(1), ALU.add))
            if not last:
                free = ("turn.tok",)
                after_taps = [*shifts(1, free), *kk_norm(1, ("tok",)), *operands(1, (), ("F1.mm",))]
            else:
                after_taps = []

            def aside(n):
                for _ in range(min(n, len(side))):
                    side.pop(0)()

            for l in range(1, LEVELS):
                def g_mm(e, i, l=l):
                    for q in range(4):
                        end = e.matmul(bank[2][:, q * P:(q + 1) * P], Nm[l % 2][:, q, :], Xs[:, q, :], start=True, stop=True)
                    return end
                made = ("X0", "Z0", "Nm1", "Nm2", "N") if l == 1 else ()
                p.add("pe", f"G{l}.mm", g_mm, after=tuple(n + ".first" for n in made) + ((f"Nm{l}",) if l > 2 else ())
                      + ((f"X{l - 1}", f"G{l - 1}") if l > 1 else ()), prev=made)
                if l == 1:
                    bonus_products()
                fill(9 if l == 1 else 3)
                tt(f"G{l}", Gs, quad(2), four(ident), ALU.add, after=(f"G{l}.mm",))
                if l + 2 < LEVELS:
                    mask(l + 2, "pool", (f"G{l}.mm",))
                if l == 2 and not last:
                    decays(1)
                if l == 1:
                    turn_and_mask()
                    fill(6)
                aside(3)

                def xz_mm(e, i, l=l):
                    if l < LEVELS - 1:
                        for q in range(4):
                            e.matmul(bank[3][:, q * P:(q + 1) * P], Zs[:, q, :], Gs[:, q, :], start=True, stop=True)
                    for q in range(4):
                        end = e.matmul(bank[6][:, q * P:(q + 1) * P], Gs[:, q, :], Zs[:, q, :], start=True, stop=True)
                    return end
                p.add("pe", f"XZ{l}.mm", xz_mm, after=(f"G{l}", "M") + ((f"X{l - 1}", f"Z{l - 1}") if l > 1 else ()))
                fill(3)
                if l < LEVELS - 1:
                    act(f"X{l}", Xs, quad(3), ACT.Copy, after=(f"XZ{l}.mm",))
                copy("dve", f"Z{l}", Zs, quad(6), after=(f"XZ{l}.mm",))
                if l == 1:
                    side += taps[:24] + after_taps[:8] + taps[24:28] + after_taps[8:9] + taps[28:] + after_taps[9:]
                    if not last:
                        low_rank(1, ("RK",))
                aside(3)

            def V(c, hh):
                return tok[:, 2 + c, hh * HD:hh * HD + HD]

            for c in range(TT):
                def f_mm(e, i, c=c):
                    for hh in range(2):
                        o = bank[2][:, hh * HD:hh * HD + HD]
                        if c:
                            e.matmul(o, Az[hh][:, P:T], St, start=True, stop=False)
                        end = e.matmul(o, Mt[:, 2 * hh + c, :], V(c, hh), start=not c, stop=True)
                    return end
                p.add("pe", f"F{c}.mm", f_mm, after=("M", "tok", "G6") + (("St",) if c else ()))
                fill(3)
                copy("dve", f"F{c}", Fs, bank[2][:, 0:P], after=(f"F{c}.mm",))
                aside(3)

                def u_mm(e, i, c=c):
                    for hh in range(2):
                        end = e.matmul(bank[3][:, hh * HD:hh * HD + HD], Zs[:, 2 * hh + c, :], Fs[:, hh * HD:hh * HD + HD],
                                       start=True, stop=True)
                    return end
                p.add("pe", f"U{c}.mm", u_mm, after=(f"F{c}", "Z6", "X5"))
                fill(3)
                copy("dve", f"U{c}", Us[:, c, :], bank[3][:, 0:P], after=(f"U{c}.mm",))
                aside(3)
                if c == 0:
                    def s_mm(e, i):
                        for hh in range(2):
                            r = slice(hh * HD, hh * HD + HD)
                            e.matmul(bank[6][r, 0:HD], tok[:, 0, r], Us[:, 0, r], start=True, stop=False)
                            end = e.matmul(bank[6][r, 0:HD], tok[:, 1, r], V(0, hh), start=False, stop=True)
                        return end
                    p.add("pe", "S.mm", s_mm, after=("U0", "Z6"))
                    fill(3)
                    ts("St", St, bank[6][:, 0:HD], eT, None, ALU.mult, after=("S.mm", "eT.first"), prev=("eT",))
                    if not last:
                        whole_decay(("St",))
                    aside(3)

            def o_mm(e, i):
                for c in range(TT):
                    for hh in range(2):
                        r = slice(hh * HD, hh * HD + HD)
                        o = bank[7][r, c * P:(c + 1) * P]
                        e.matmul(o, V(c, hh), RKt[:, 2 * hh + c, :], start=True, stop=False)
                        if c:
                            e.matmul(o, St, Rz[hh][:, P:T], start=False, stop=False)
                        end = e.matmul(o, Us[:, c, r], RBt[:, 2 * hh + c, :], start=False, stop=True)
                return end
            p.add("pe", "O.mm", o_mm, after=("U1", "RK", "RB"))
            fill(5)
            if last:
                aside(99)
                mean_over_channels("ln.sum", CU, 0, ("taps", "gr"))
            aside(99)
            act("O.copy", Oc, bank[7][:, 0:T], ACT.Copy, after=("O.mm",))
            if not last:
                n_products(True)
                receptances(("O.mm",))
            p.add("pe", "gn.sum", lambda e, i: e.matmul(bank[5][:, 0:T], C("pair"), Oc, start=True, stop=True),
                  after=("O.copy", "tok") + (() if last else ("kk.norm",)))
            fill(4)
            if not last:
                products("RK.mm", 4, Kf, Rz, ("K", "R1", "eT"))
            stt("gn.c", Oc, bank[5][:, 0:T], -1.0 / HD, Oc, ALU.mult, ALU.add, after=("gn.sum",))
            tt("gn.sq", osq, Oc, Oc, ALU.mult)
            if not last:
                level_zero(True)
                bonus_operand(1)
            p.add("pe", "gn.var", lambda e, i: e.matmul(bank[5][:, 0:T], C("pair"), osq, start=True, stop=True), after=("gn.sq",))
            ts("gn.ms", grs, bank[5][:, 0:T], 1.0 / HD, 64e-5, ALU.mult, ALU.add, after=("gn.var",))
            act("gn.sd", grs, grs, ACT.Sqrt, after=("gn.ms",))
            p.add("dve", "gn.rs", lambda e, i: e.reciprocal(grs, grs), after=("gn.sd",))
            stt("gn.y", Oc, Oc, pi("gn_g"), grs, ALU.mult, ALU.mult)
            stt("gn.b", Oc, Oc, pi("gn_b"), bonus, ALU.add, ALU.add)
            tt("YR", lambda i: YR[:, bass.ds(i, 1), :], Oc.unsqueeze(1), rg.unsqueeze(1), ALU.mult, after=("rg",))
            assert not queue and not side

        p.phase("rwkv", R_PAIRS - 1)
        rwkv(False)
        p.phase("rwkv end", at=R_PAIRS - 1, peel=".end")
        rwkv(True)
        for n in range(3, NR):
            freed[n] = f"rp{n}.{KT}.end"
        for n in range(3):
            freed[n] = f"rp{n}.{KT}"

        p.phase("conv norm")
        used[0] = block2_end
        mean = carve(T)
        cv2 = carve(KT, T)
        mT = carve(KT, T)
        m0 = carve(T)
        ts("ln.mean", mean, bank[0][:, 0:T], 1.0 / D, None, ALU.mult, after=("ln.sum.end", "YR.end"))
        tt("ln.c", CU, CU, mean.unsqueeze(1).to_broadcast([P, KT, T]), ALU.subtract)
        tt("ln.sq", cv2, CU, CU, ALU.mult)

        QUAD = 4

        def out_products(tag, src, weight, n, after):
            load(f"w{tag}{n}", n, lambda i: weight(i * QUAD + n), prev=(f"{tag}{n}.mm",))
            p.add("pe", f"{tag}{n}.mm", project(half(n), slot[n], src), after=(f"w{tag}{n}",) + after, prev=(f"{tag}{n}",))
            freed[n] = f"{tag}{n}.mm"

        def tile(ap, n):
            return lambda i: ap[:, bass.ds(i * QUAD + n, 1), :]

        def ln_tile(n):
            c, v = tile(CU, n), tile(cv2, n)
            par_col = lambda name: (lambda i: par[:, bass.ds(i * QUAD + (n + PCOL[name]), 1)])
            stt(f"ln.g{n}", c, c, par_col("ln_g"), rsc.unsqueeze(1), ALU.mult, ALU.mult, after=("ln.rs.first",))
            ts(f"ln.b{n}", c, c, par_col("ln_b"), None, ALU.add)
            act(f"ln.th{n}", v, c, ACT.Tanh, after=(f"ln.b{n}",), scale=0.5)
            stt(f"ln.si{n}", c, v, 1.0, c, ALU.add, ALU.mult, after=(f"ln.th{n}",))
            tt(f"ln.y{n}", c, c, tile(OG, n), ALU.mult)

        for half_of, name in enumerate((".first", ".second")):
            p.phase("rwkv out" + name, at=half_of, peel=name)
            for n in range(QUAD):
                out_products("r", YR, lambda j: a["w_y"][j * 2 + 1, :, :], n, ("YR.end", "gr.end", "pad.v", "ln.mean")
                             + ((f"r{n}.first",) if half_of else ()))
                stt(f"r{n}.g", tile(mT, n), tile(GR, n), 1.0, half(n).unsqueeze(1), ALU.add, ALU.mult, after=(f"r{n}.mm", "ln.sq"))
                ts(f"r{n}", tile(mT, n), tile(mT, n), 0.25, None, ALU.mult)
                freed[n] = f"r{n}.mm" + name
                if half_of == 0 and n == 1:
                    mean_over_channels("ln.var", cv2, 5, ("ln.sq", "gn.rs.end"))
                    ts("ln.ms", rsc, bank[5][:, 0:T], 1.0 / D, 1e-5, ALU.mult, ALU.add, after=("ln.var",))
                    act("ln.sd", rsc, rsc, ACT.Sqrt, after=("ln.ms",))
                    p.add("dve", "ln.rs", lambda e, i: e.reciprocal(rsc, rsc), after=("ln.sd",))
            for n in range(QUAD):
                ln_tile(n)
        p.phase("gated", KT // QUAD)
        for n in range(QUAD):
            out_products("c", CU, lambda j: a["w_y"][j * 2, :, :], n, ("ln.y3.second", f"r{n}.second"))
            stt(f"c{n}.g", m0.unsqueeze(1), tile(GC, n), 1.0, half(n).unsqueeze(1), ALU.add, ALU.mult, after=(f"c{n}.mm",))
            stt(f"c{n}", tile(mT, n), m0.unsqueeze(1), 0.125, tile(mT, n), ALU.mult, ALU.add)

        p.phase("w_out2", KT // QUAD)
        for n in range(QUAD):
            out_products("z", mT, lambda j: a["w_out2"][j, :, :], n, ("c3",))
            xk = tile(x3T, n)
            stt(f"z{n}", xk, half(n).unsqueeze(1), lambda i, n=n: mod[:, bass.ds(i * QUAD + (16 + n), 1)], xk,
                ALU.mult, ALU.add, after=(f"z{n}.mm",))
            act(f"z{n}.sq", tile(squares, n), xk, ACT.Square, after=(f"z{n}",))

        p.phase("final")
        mean_over_channels("norm5.sum", squares, 5, ("z3.sq",))
        ts("norm5.ms", rsc, bank[5][:, 0:T], 1.0 / D, 1e-6, ALU.mult, ALU.add, after=("norm5.sum",))
        act("norm5.sd", rsc, rsc, ACT.Sqrt, after=("norm5.ms",))
        p.add("dve", "norm5.rs", lambda e, i: e.reciprocal(rsc, rsc), after=("norm5.sd",))
        ytok = hT[:, :, :].rearrange("p k n -> p (k n)").rearrange("p (t d) -> p t d", t=TT)
        for k in range(KT):
            stt(f"fin{k}", CU[:, k, :], x3T[:, k, :], PC("final_g", k), rsc, ALU.mult, ALU.mult, after=("norm5.rs",))

            def turn_back(e, i, k=k):
                for t in range(TT):
                    last = e.transpose(bank[k % 4][:, t * P:(t + 1) * P], CU[:, k, t * P:(t + 1) * P], ident)
                return last
            p.add("pe", f"fin.turn{k}", turn_back, after=(f"fin{k}",) + ((f"fin.y{k - 4}",) if k >= 4 else ()))
            act(f"fin.y{k}", ytok[:, :, k * P:(k + 1) * P], view3(half(k % 4), P), ACT.Copy, after=(f"fin.turn{k}",))
        p.dma("out", lambda e, i: e.dma_start(out.rearrange("(t p) d -> p t d", p=P), ytok), after=("fin.y7",))

        block = ctx.enter_context(nc.Block())

        @block.tensor
        def _(e):
            p.run("pe", e)

        @block.scalar
        def _(e):
            p.run("act", e)

        @block.vector
        def _(e):
            p.run("dve", e)

        @block.gpsimd
        def _(e):
            p.run("pool", e)

        @block.sync
        def _(e):
            p.run("sp", e)
            e.wait_ge(p.named["out"].sem, 16)


def col_slices(w, starts):
    k = w.shape[0] // P
    return np.stack([np.ascontiguousarray(w[:, s:s + P].reshape(k, P, P).transpose(1, 0, 2)).reshape(P, k * P)
                     for s in starts])


def by_partition(v):
    return np.ascontiguousarray(v.reshape(-1, P).T)


def layouts(w):
    o = {"x": w["x"][0], "cst": shape_constants(), "rel_bias": w["rel_bias"]}
    par = np.zeros((P, NPCOL), np.float32)
    convw = np.stack([w["conv_w"][0][j].reshape(8, P) for j in range(CONV1)], 1)
    convk = np.stack([w["conv_k_2"][0][j].reshape(KT, P) for j in range(CONV2)], 1)
    for name, v in (("norm_mix", by_partition(w["norm_mix"][0])), ("norm_ffn", by_partition(w["norm_ffn"][0])),
                    ("norm_final", by_partition(w["norm_final"])), ("norm_g", by_partition(w["norm_g_2"][0])),
                    ("final_g", by_partition(w["final_g_2"])), ("conv_w", convw.reshape(8 * CONV1, P).T),
                    ("conv_b", by_partition(w["conv_b"][0])), ("d_skip", by_partition(np.repeat(w["d_skip"][0], HD))),
                    ("ssm_norm", by_partition(w["ssm_norm_w"][0])), ("ada_b", by_partition(w["ada_b_2"][0])),
                    ("c", by_partition(w["c_2"][0])), ("conv_k", convk.reshape(KT * CONV2, P).T),
                    ("conv_b2", by_partition(w["conv_b_2"][0])), ("ln_g", by_partition(w["conv_ln_g_2"][0])),
                    ("ln_b", by_partition(w["conv_ln_b_2"][0])), ("mu", by_partition(w["rwkv_mu_2"][0])),
                    ("a0", by_partition(w["rwkv_a0_2"][0])), ("k_k", by_partition(w["rwkv_k_k_2"][0])),
                    ("k_a", by_partition(w["rwkv_k_a_2"][0])), ("r_k", by_partition(w["rwkv_r_k_2"][0].reshape(-1))),
                    ("gn_g", by_partition(w["rwkv_gn_g_2"][0])), ("gn_b", by_partition(w["rwkv_gn_b_2"][0]))):
        par[:, PCOL[name]:PCOL[name] + v.shape[1]] = v
    o["par"] = par
    o["row"] = np.concatenate([w["dt_bias"][0], w["forget_bias"][0], w["a_log"][0], w["sinks"][0]])[None, :]
    o["w0"] = w["rwkv_w0_2"]
    wi = w["w_in"][0]
    both = lambda s: np.concatenate([wi[:, s:s + HD]] * 2, 1)
    o["w_pre"] = np.concatenate([col_slices(wi, (B0, B0 + P, C0, C0 + P)), col_slices(both(DK0), (0,)),
                                 col_slices(both(DK0 + HD), (0,)), col_slices(wi, (DV0,))])
    ws = np.concatenate([wi[:, DT0:DT0 + NH], wi[:, F0:F0 + NH]], 1)
    o["w_small"] = np.ascontiguousarray(ws.reshape(KT, P, 2 * NH).transpose(1, 0, 2)).reshape(P, -1)
    starts = []
    for i in range(PAIRS):
        starts += [s + i * P for s in (BQ0, BQ0 + W, BQ0 + 2 * W, CQ0, CQ0 + W, CQ0 + 2 * W, DQ0, X0, Z0)]
        starts += [G0 + i * D + j * P for j in range(KT)]
    o["w_heads"] = col_slices(wi, starts)
    wb = [col_slices(w["w_branch"][0, b], range(0, D, P)) for b in range(N_BR)]
    o["w_br"] = np.stack(wb, 1).reshape(KT * N_BR, P, W)
    o["w_out"] = w["w_out"][0]
    g, u = (col_slices(w[n][0], range(0, D_FF, P)) for n in ("w_ffn_gate", "w_ffn_up"))
    o["w_gu"] = np.stack([g, u], 1).reshape(2 * FF_TILES, P, D)
    o["w_down"] = w["w_ffn_down"][0]
    o["ada_w"] = np.ascontiguousarray(
        w["ada_w_2"][0].reshape(KT, P, 3, D).transpose(0, 2, 1, 3)).reshape(3 * KT, P, D)
    wi = w["w_in_2"][0]
    starts = []
    for i in range(R_PAIRS):
        starts += [s + i * P for s in (TS0, TS0 + D, TS0 + 2 * D, VAL0, GATE0, OG0, ROG0, GC0, GR0)]
    o["w_rwkv"] = col_slices(wi, starts)
    o["w_lora"] = col_slices(wi, (TS0 + 3 * D,))[0]
    lo = np.concatenate([w["rwkv_w2_2"][0], w["rwkv_a2_2"][0]], 0)
    o["lora2"] = np.ascontiguousarray(lo.reshape(P, KT, P).transpose(1, 0, 2))
    y = [col_slices(w[n][0], range(0, D, P)) for n in ("w_conv_out_2", "w_rwkv_out_2")]
    o["w_y"] = np.stack(y, 1).reshape(2 * KT, P, D)
    o["w_out2"] = col_slices(w["w_out_2"][0], range(0, D, P))
    return {k: np.ascontiguousarray(v) for k, v in o.items()}


def kernel(**inputs):
    import concourse.bacc as bacc
    from concourse.bass_utils import run_bass_kernel_spmd

    arrays = layouts({k: np.asarray(v) for k, v in inputs.items()})
    nc = bacc.Bacc("TRN2", target_bir_lowering=False, num_devices=1)
    aps = {n: nc.dram_tensor("in_" + n, v.shape, mybir.dt.from_np(v.dtype), kind="ExternalInput").ap() for n, v in arrays.items()}
    out = nc.dram_tensor("out_y", (T, D), F32, kind="ExternalOutput").ap()
    build(nc, aps, out)
    r = run_bass_kernel_spmd(nc, [{"in_" + n: v for n, v in arrays.items()}], core_ids=[0])
    return r.results[0]["out_y"].reshape(1, T, D)
```

```python
import math
from contextlib import ExitStack

import numpy as np

import concourse.bass as bass
from concourse import mybir

F32 = mybir.dt.float32
ACT = mybir.ActivationFunctionType
ALU = mybir.AluOpType
AX = mybir.AxisListType

T = 256
D = 1024
P = 128
KT = D // P
TT = T // P
W = 512
HD = 64
NH = W // HD
PAIRS = NH // 2
N_BR = 4
GROUPS = 2
D_FF = 2816
FF_TILES = D_FF // P
REL_BUCKETS, REL_EXACT, REL_MAX = 32, 16, 1024
SWA_WINDOW = 128
CONV1 = 4
CONV2 = 31
R_PAIRS = D // P
LEVELS = 7
NEG = -1e30
LOGIT = T + 1
SROW = P + 1 + LOGIT
DECAY = math.exp(-0.5)
MID = 0.5 * P * DECAY

Z0, X0, B0, C0 = 0, 512, 1024, 1280
DT0, BQ0, CQ0, F0, DQ0, DK0, DV0, G0 = 1536, 1544, 3080, 4616, 4624, 5136, 5264, 5392
VAL0, GATE0, OG0, TS0, ROG0, GC0, GR0 = 0, 1024, 2048, 3072, 6272, 7296, 8320

def columns(*fields):
    at, out = 0, {}
    for name, n in fields:
        out[name] = at
        at += n
    return out, at


PCOL, NPCOL = columns(("norm_mix", KT), ("norm_ffn", KT), ("norm_final", KT), ("norm_g", KT),
                      ("final_g", KT), ("conv_w", 8 * CONV1), ("conv_b", 8), ("d_skip", PAIRS),
                      ("ssm_norm", PAIRS), ("ada_b", 24), ("c", KT), ("conv_k", KT * CONV2),
                      ("conv_b2", KT), ("ln_g", KT), ("ln_b", KT), ("mu", 25), ("a0", KT), ("k_k", KT),
                      ("k_a", KT), ("r_k", KT), ("gn_g", KT), ("gn_b", KT))
RCOL, NRCOL = columns(("dt_bias", NH), ("forget_bias", NH), ("a_log", NH), ("sinks", NH))
CCOL, NCCOL = columns(("ident", P), ("flip", P), ("upper", P), ("ones", P), ("upper2", P),
                      ("strict", P), ("pair", P), ("pick", NH), ("mid", 2),
                      ("onehot", 3 * P), ("gmask", 3 * P), ("off_first", P), ("off", LEVELS * P))
NKEPT = CCOL["onehot"]
NFIRST = CCOL["off_first"]


def shape_constants():
    c = np.zeros((P, NCCOL), np.float32)
    r, q = np.arange(P)[:, None], np.arange(P)[None, :]

    def put(name, a):
        c[:a.shape[0], CCOL[name]:CCOL[name] + a.shape[1]] = a

    put("ident", r == q)
    put("flip", r == P - 1 - q)
    put("upper", r <= q)
    put("ones", np.ones((P, P)))
    put("upper2", r <= q)
    put("strict", r < q)
    put("pair", r // HD == q // HD)
    put("off_first", (r == q + 1) & (r % 2 == 1))
    for l in range(LEVELS):
        s = 1 << l
        c[:, CCOL["off"] + l * P:CCOL["off"] + (l + 1) * P] = \
            (r // (2 * s) == q // (2 * s)) & (r // s % 2 == 0) & (q // s % 2 == 1)
    dist = T - 1 - np.arange(3 * P)
    d = np.maximum(dist, 1).astype(np.float32)
    large = REL_EXACT + (np.log(d / np.float32(REL_EXACT)) / np.float32(math.log(REL_MAX / REL_EXACT))
                         * np.float32(REL_BUCKETS - REL_EXACT)).astype(np.int32)
    bucket = np.where(dist < REL_EXACT, np.maximum(dist, 0), np.minimum(large, REL_BUCKETS - 1))
    put("onehot", np.arange(REL_BUCKETS)[:, None] == bucket[None, :])
    gmask = np.zeros((2 * NH + 1, 3 * P))
    gmask[:, dist < 0] = NEG
    gmask[NH:2 * NH, dist >= SWA_WINDOW] = NEG
    put("gmask", gmask)
    put("pick", np.eye(40, NH) + np.eye(40, NH, -32))
    put("mid", np.tile(np.array([[-MID, MID]]), (P, 1)))
    return c


class Step:
    def __init__(self, phase, engine, index, emit, after, prev, sem, lag):
        self.phase, self.engine, self.index, self.emit = phase, engine, index, emit
        self.after, self.prev, self.sem, self.lag = after, prev, sem, lag


class Phase:
    def __init__(self, name, trips, at, peel):
        self.name, self.trips, self.at, self.peel = name, trips, at, peel
        self.steps, self.per, self.base = [], {}, {}


class Program:
    ENGINES = ("pe", "act", "dve", "pool", "sp")
    START = 256

    def __init__(self, sems, new_sem):
        self.sems, self.new_sem, self.phases, self.named = sems, new_sem, [], {}

    def phase(self, name, trips=None, at=0, peel=""):
        self.phases.append(Phase(name, trips, at, peel))

    def add(self, engine, name, emit, after=(), prev=(), lag=1):
        ph = self.phases[-1]
        after = (after,) if isinstance(after, str) else tuple(after)
        prev = (prev,) if isinstance(prev, str) else tuple(prev)
        if ph.peel:
            after = tuple(n + ph.peel if n + ph.peel in self.named else n for n in after)
            after += tuple(n for n in prev if n in self.named)
            prev = ()
        ph.per[engine] = ph.per.get(engine, 0) + 1
        step = Step(ph, engine, ph.per[engine], emit, after, prev, self.sems[engine], lag)
        name += ph.peel
        assert name not in self.named, name
        self.named[name] = step
        ph.steps.append(step)
        return name

    def dma(self, name, emit, after=(), prev=(), engine="sp"):
        name = self.add(engine, name, emit, after, prev)
        self.phases[-1].per[engine] -= 1
        self.named[name].sem, self.named[name].index = self.new_sem("got_" + name.replace(".", "_")), None

    def run(self, engine, eng):
        sem = self.sems[engine]
        eng.sem_inc(sem, self.START)
        base = {e: self.START for e in self.ENGINES}
        for ph in self.phases:
            ph.base = dict(base)
            for e in self.ENGINES:
                base[e] += ph.per.get(e, 0) * (ph.trips or 1)
            steps = [s for s in ph.steps if s.engine == engine]
            if not steps:
                continue
            if ph.trips is None:
                self.emit(eng, steps, ph.at)
            else:
                with eng.Fori(0, ph.trips) as i:
                    self.emit(eng, steps, i)

    def emit(self, eng, steps, i):
        seen = {}
        for s in steps:
            ph, own = s.phase, s.engine
            if own in ("act", "dve", "pool") and s.index is not None:
                before = ph.base[own] + s.index - s.lag
                eng.wait_ge(self.sems[own], before if ph.trips is None else i * ph.per[own] + before)
                seen[id(self.sems[own])] = (1, s.index - s.lag)
            for names, back in ((s.after, 0), (s.prev, 1)):
                for name in names:
                    t = self.named[name]
                    here = t.phase is ph
                    assert here or not back, name
                    count, per, base = (16, 16, 0) if t.index is None else \
                        (t.index, t.phase.per[t.engine], t.phase.base[t.engine])
                    if here and ph.trips is not None:
                        rank = (1 - back, count)
                        value = i * per + (base + count - back * per)
                    else:
                        value = base + count + ((t.phase.trips or 1) - 1) * per
                        rank = (-1, value)
                    known = seen.get(id(t.sem), (-9, 0))
                    if known >= rank and not (rank[0] == -1 and known[0] == 0):
                        continue
                    eng.wait_ge(t.sem, value)
                    seen[id(t.sem)] = max(known, rank)
            s.emit(eng, i).then_inc(s.sem, 1 if s.index is not None else 16)


def build(nc, a, out):
    with ExitStack() as ctx:
        def sb(name, *shape):
            return ctx.enter_context(nc.sbuf_tensor(name, list(shape), F32))

        def sem(name):
            return ctx.enter_context(nc.semaphore(name))

        cst = sb("cst", P, NKEPT)
        par = sb("par", P, NPCOL)
        row = sb("row", 1, NRCOL)
        bank = [ctx.enter_context(nc.psum_tensor(f"bank{n}", [P, 512], F32)) for n in range(8)]
        N_SLOTS = 12
        slot = [sb(f"slot{n}", P, D) for n in range(N_SLOTS)]
        hT = sb("hT", P, KT, T)
        x = sb("x", P, TT, D)
        x3T = x[:, :, :].rearrange("p t d -> p (t d)").rearrange("p (k n) -> p k n", n=T)
        adaA = sb("adaA", P, 3 * D)
        stat = sb("stat", P, 6)
        small = sb("small", P, 48)

        def C(name, n=P, rows=P, off=0):
            return cst[0:rows, CCOL[name] + off:CCOL[name] + off + n]

        def PC(name, j=0):
            return par[:, PCOL[name] + j:PCOL[name] + j + 1]

        ident, flip, ones = C("ident"), C("flip"), C("ones")

        ARENA = 30800
        arena = sb("arena", P, ARENA)
        used = [0]

        def carve(*shape, rows=P):
            n = int(np.prod(shape))
            v = arena[0:rows, used[0]:used[0] + n]
            used[0] += n
            assert used[0] <= ARENA, used[0]
            if len(shape) == 2:
                v = v.rearrange("p (a b) -> p a b", a=shape[0])
            elif len(shape) == 3:
                v = v.rearrange("p (a b c) -> p a b c", a=shape[0], b=shape[1])
            return v

        p = Program({e: sem("steps_of_" + e) for e in Program.ENGINES}, sem)

        def view3(ap, n):
            return ap.rearrange("p (a b) -> p a b", b=n)

        freed = {}

        def load(name, n, src, after=(), prev=(), rows=P, width=D):
            p.dma(name, lambda e, i: e.dma_start(slot[n][0:rows, 0:width], src(i)),
                  after=tuple(after) + ((freed[n],) if n in freed else ()), prev=prev)

        def project(psum, w, rhs, kt=KT):
            def emit(e, i):
                for k in range(kt):
                    last = e.matmul(psum, w[:, k * P:(k + 1) * P], rhs[:, k, :], start=k == 0, stop=k == kt - 1)
                return last
            return emit

        def project_tokens(psum, w):
            def emit(e, i):
                for t in range(TT):
                    for k in range(KT):
                        last = e.matmul(psum[:, t * P:(t + 1) * P], hT[:, k, t * P:(t + 1) * P],
                                        w[:, k * P:(k + 1) * P], start=k == 0, stop=k == KT - 1)
                return last
            return emit

        def half(n):
            return bank[n][:, 0:T]

        def act(name, o, i_, f, after=(), prev=(), **kw):
            p.add("act", name, lambda e, i: e.activation(
                o(i) if callable(o) else o, i_(i) if callable(i_) else i_, f,
                **{k: v(i) if callable(v) else v for k, v in kw.items()}), after, prev)

        def on(v, i):
            return v(i) if callable(v) else v

        def copy(eng, name, o, i_, after=(), prev=()):
            p.add(eng, name, lambda e, i: e.tensor_copy(on(o, i), on(i_, i)), after, prev)

        def tt(name, o, x0, x1, op, after=(), prev=(), eng="dve", lag=1):
            p.add(eng, name, lambda e, i: e.tensor_tensor(on(o, i), on(x0, i), on(x1, i), op), after, prev, lag)

        def ts(name, o, x0, s1, s2, op0, op1=None, after=(), prev=(), eng="dve", lag=1):
            p.add(eng, name, lambda e, i: e.tensor_scalar(on(o, i), on(x0, i), on(s1, i), on(s2, i), op0,
                                                          **({"op1": op1} if op1 is not None else {})), after, prev, lag)

        def stt(name, o, x0, s, x1, op0, op1, after=(), prev=(), lag=1):
            p.add("dve", name, lambda e, i: e.scalar_tensor_tensor(
                out=on(o, i), in0=on(x0, i), scalar=on(s, i), in1=on(x1, i), op0=op0, op1=op1), after, prev, lag)

        def bc(ap, shape):
            return ap.to_broadcast(list(shape))

        p.phase("setup")
        for t in range(TT):
            p.dma(f"x{t}", lambda e, i, t=t: e.dma_start(x[:, t, :], a["x"][t * P:(t + 1) * P, :]))
        p.dma("cst", lambda e, i: e.dma_start(cst[:, :], a["cst"][:, 0:NKEPT]), engine="act")
        p.dma("par", lambda e, i: e.dma_start(par[:, :], a["par"]), engine="act")
        p.dma("row", lambda e, i: e.dma_start(row[:, :], a["row"]), engine="act")
        warm = sb("warm", P, 1)
        p.add("pool", "warm", lambda e, i: e.memset(warm[:, :], 1.0))
        relb = sb("relb", REL_BUCKETS, 2 * NH + 1)
        p.add("pool", "relb.zero", lambda e, i: e.memset(relb[:, :], 0.0))
        p.dma("relb", lambda e, i: e.dma_start(relb[:, 0:2 * NH], a["rel_bias"]), after="relb.zero")
        p.add("pool", "ada.zero", lambda e, i: e.memset(adaA[:, :], 0.0))
        sc = sb("sc", P, KT)
        cT = par[:, PCOL["c"]:PCOL["c"] + KT]


        def sqrt_table(tag):
            act(f"{tag}.table", warm[:, :], warm[:, :], ACT.Sqrt, after=("warm",))

        xn = arena[:, 8 * T:8 * T + TT * D].rearrange("p (t d) -> p t d", t=TT)

        def token_norm(tag, weight, target, after):
            ss, sd, rs = stat[:, 0:2], stat[:, 2:4], stat[:, 4:6]
            for t in range(TT):
                act(f"{tag}.sq{t}", xn[:, t, :], x[:, t, :], ACT.Square, after=after(t), accum_out=ss[:, t:t + 1])
            ts(f"{tag}.ms", sd, ss, 1.0 / D, 1e-6, ALU.mult, ALU.add, after=(f"{tag}.sq{TT - 1}",))
            act(f"{tag}.sd", sd, sd, ACT.Sqrt, after=(f"{tag}.ms",))
            p.add("dve", f"{tag}.rs", lambda e, i: e.reciprocal(rs, sd), after=(f"{tag}.sd",))
            for t in range(TT):
                ts(f"{tag}.xn{t}", xn[:, t, :], x[:, t, :], rs[:, t:t + 1], None, ALU.mult, after=(f"{tag}.rs",))
            for k in range(KT):
                def turn(e, i, k=k):
                    for t in range(TT):
                        last = e.transpose(half(k % 4)[:, t * P:(t + 1) * P], xn[:, t, k * P:(k + 1) * P], ident)
                    return last
                p.add("pe", f"{tag}.turn{k}", turn, after=(f"{tag}.xn1", "cst") + ((f"{tag}.h{k - 4}",) if k >= 4 else ()))
                ts(f"{tag}.h{k}", target[:, k, :], half(k % 4), PC(weight, k), None, ALU.mult,
                   after=(f"{tag}.turn{k}", "par"))

        sqrt_table("norm1")
        token_norm("norm1", "norm_mix", hT, after=lambda t: (f"x{t}",))
        act("sc.tanh", sc[:, :], cT, ACT.Tanh, after=("par",), scale=0.5)
        stt("sc.x", sc[:, :], sc[:, :], 1.0, cT, ALU.add, ALU.mult, after=("sc.tanh",))
        ts("sc", sc[:, :], sc[:, :], 0.5, None, ALU.mult, after=("sc.x",))

        p.phase("pre")
        padA = sb("padA", P, 30 + T)
        pad1 = padA[:, 0:CONV1 - 1 + T]
        conv = sb("conv", P, T)
        th = sb("th", P, T)
        gates = carve(N_BR * KT, T)
        YT = [carve(W // P, T) for _ in range(N_BR)]
        Hk = carve(2 * NH + 1, LOGIT)
        CBT = carve(PAIRS, 3 * P)
        BCT = gates[:, 0:4, :]
        dk = carve(PAIRS, T)
        dv = carve(PAIRS, TT, HD)
        dtc = carve(TT, NH)
        acum = carve(TT, NH)
        acumT = carve(T)
        fcumT = carve(T)
        cwh = carve(8 * CONV1 + 8)
        wsm = carve(KT, 2 * NH)
        lf, rf = carve(T), carve(T)
        block1_end = used[0]
        LF = carve(TT, 40)
        LA = carve(TT, NH)
        sp = [carve(TT, 2 * NH) for _ in range(6)]
        expA = carve(NH)
        gsb = carve(3 * P)
        cst1 = carve(NFIRST - NKEPT)
        onehot, gmask = cst1[0:REL_BUCKETS, 0:3 * P], cst1[0:2 * NH + 1, 3 * P:6 * P]
        p.dma("cst1", lambda e, i: e.dma_start(cst1, a["cst"][:, NKEPT:NFIRST]), engine="act")

        p.dma("wsm", lambda e, i: e.dma_start(wsm.rearrange("p a b -> p (a b)"), a["w_small"]))
        for n in range(7):
            load(f"pre.w{n}", n, lambda i, n=n: a["w_pre"][n, :, :])
        ts("cwh", cwh, par[:, PCOL["conv_w"]:PCOL["conv_w"] + 40], 0.5, None, ALU.mult, after=("par",))
        p.add("pool", "padA.zero", lambda e, i: e.memset(padA[:, :], 0.0))
        p.add("pool", "fcumT.zero", lambda e, i: e.memset(fcumT, 0.0))
        p.add("pool", "lf.zero", lambda e, i: e.memset(lf, 0.0))
        p.add("pool", "rf.zero", lambda e, i: e.memset(rf, 0.0))
        p.add("pool", "lf.ones", lambda e, i: e.memset(lf[0:NH, :], 1.0), after=("rf.zero",))
        p.add("pool", "rf.ones", lambda e, i: e.memset(rf[32:40, :], 1.0))
        p.add("pool", "LF.zero", lambda e, i: e.memset(LF, 0.0))

        def small_mm(e, i):
            for t in range(TT):
                e.matmul(bank[6][:, t * 16:(t + 1) * 16], ones[0:1, :], row[0:1, 0:2 * NH], start=True, stop=False)
                for k in range(KT):
                    last = e.matmul(bank[6][:, t * 16:(t + 1) * 16], hT[:, k, t * P:(t + 1) * P], wsm[:, k, :],
                                    start=False, stop=k == KT - 1)
            return last
        p.add("pe", "small", small_mm, after=("wsm", "row", "norm1.h7"))

        p.add("pe", "g.mm", lambda e, i: e.matmul(bank[7][0:2 * NH + 1, 0:3 * P], relb[:, :],
              onehot, start=True, stop=True), after=("relb", "cst1"))
        tt("g.mask", gsb[0:2 * NH + 1, :], bank[7][0:2 * NH + 1, 0:3 * P], gmask, ALU.add,
           after=("g.mm",))
        g_dram = nc.dram_tensor("g_scratch", [2 * NH + 1, 3 * P], F32, kind="Internal")
        p.dma("g.out", lambda e, i: e.dma_start(g_dram.ap(), gsb[0:2 * NH + 1, :]), after=("g.mask",))
        shifted = bass.AP(g_dram, 0, [[1, P], [3 * P, 2 * NH + 1], [1, T]])
        p.dma("g.in", lambda e, i: e.dma_start(Hk[:, :, 0:T], shifted), after=("g.out",))
        p.add("dve", "sink.none", lambda e, i: e.memset(Hk[:, :, T:LOGIT], NEG))
        p.add("pe", "sink.mm", lambda e, i: e.matmul(bank[7][:, 0:NH], ones[0:1, :],
              row[0:1, RCOL["sinks"]:RCOL["sinks"] + NH], start=True, stop=True), after=("row", "g.mask"))
        copy("dve", "sink", Hk[:, NH:2 * NH, T:LOGIT], bank[7][:, 0:NH].unsqueeze(2), after=("sink.mm", "sink.none"))

        rowA = row[0:1, RCOL["a_log"]:RCOL["a_log"] + NH]
        act("expA.row", rowA, rowA, ACT.Exp, after=("row",))
        p.add("pe", "expA.mm", lambda e, i: e.matmul(bank[6][:, 64:64 + NH], ones[0:1, :], rowA, start=True, stop=True),
              after=("expA.row",))
        v, nb, u, w1, d1, soft = sp
        ps_small = view3(bank[6][:, 0:32], 16)
        copy("dve", "expA", expA, bank[6][:, 64:64 + NH], after=("expA.mm",))
        copy("dve", "sp.v0", v[:, :, 0:NH], ps_small[:, :, 0:NH], after=("small",))
        ts("sp.v1", v[:, :, NH:], ps_small[:, :, NH:], -1.0, None, ALU.mult)
        stt("sp.nb", nb, v, -1.0, v, ALU.mult, ALU.min, after=("sp.v1",))
        act("sp.u", u, nb, ACT.Exp, after=("sp.nb",))
        ts("sp.w1", w1, u, 1.0, None, ALU.add, after=("sp.u",))
        act("sp.ln", soft, w1, ACT.Ln, after=("sp.w1",))
        ts("sp.d1", d1, w1, -1.0, 1e-30, ALU.add, ALU.max, after=("sp.w1",))
        p.add("dve", "sp.rd", lambda e, i: e.reciprocal(d1, d1), after=("sp.d1",))
        tt("sp.lnu", soft, soft, u, ALU.mult, after=("sp.ln",))
        tt("sp.lnr", soft, soft, d1, ALU.mult, after=("sp.lnu", "sp.rd"))
        stt("sp.tiny", u, w1, 1.0, u, ALU.is_equal, ALU.mult, after=("sp.lnr",))
        tt("sp.log1p", soft, soft, u, ALU.add, after=("sp.tiny",))
        stt("sp.soft", soft, v, 0.0, soft, ALU.max, ALU.add, after=("sp.log1p",))
        copy("dve", "dt", dtc, soft[:, :, 0:NH], after=("sp.soft",))
        stt("LA", LA, soft[:, :, 0:NH], -1.0, bc(expA.unsqueeze(1), (P, TT, NH)), ALU.mult, ALU.mult,
            after=("sp.soft", "expA"))
        copy("dve", "LF0", LF[:, :, 0:NH], soft[:, :, NH:], after=("LF.zero", "sp.soft"))
        ts("LF1", LF[:, :, 32:40], soft[:, :, NH:], -1.0, None, ALU.mult)

        def conv_tile(tag, tile, evac_after, target, wcol, eng_after=()):
            ts(f"{tag}.tap0", conv[:, :], pad1[:, 0:T], lambda i: cwh[:, wcol(i, 0)], lambda i: cwh[:, wcol(i, None)], ALU.mult, ALU.add, after=evac_after + ("cwh",))
            for j in range(1, CONV1):
                stt(f"{tag}.tap{j}", conv[:, :], pad1[:, j:j + T],
                    lambda i, j=j: cwh[:, wcol(i, j)], conv[:, :], ALU.mult, ALU.add,
                    after=(f"{tag}.tap{j - 1}",))
            act(f"{tag}.tanh", th[:, :], conv[:, :], ACT.Tanh, after=(f"{tag}.tap{CONV1 - 1}",))
            stt(f"{tag}.silu", target, th[:, :], 1.0, conv[:, :], ALU.add, ALU.mult, after=(f"{tag}.tanh",))

        last = None
        for n in range(4):
            p.add("pe", f"bc{n}", project(half(n), slot[n], hT), after=(f"pre.w{n}", "norm1.h7"))

        for n in range(4):
            act(f"bc{n}.pad", pad1[:, CONV1 - 1:], half(n), ACT.Copy,
                after=(f"bc{n}", "padA.zero") + ((f"bc{n - 1}.tap3",) if n else ()))
            conv_tile(f"bc{n}", n, (f"bc{n}.pad",), BCT[:, n, :],
                      lambda i, j, n=n: bass.ds(8 * CONV1 + 4 + n if j is None else (4 + n) * CONV1 + j, 1))
        for g in range(GROUPS):
            p.add("pe", f"dk{g}", project(half(4), slot[4 + g], hT),
                  after=(f"pre.w{4 + g}",) + (("dk01",) if g else ()))
            for n in range(2):
                act(f"dk{g}{n}", dk[:, 2 * g + n, :], half(4), ACT.Copy, after=(f"dk{g}",))
        p.add("pe", "dv", project_tokens(half(0), slot[6]), after=("pre.w6", "bc0.pad"))
        for n in range(PAIRS):
            act(f"dv{n}", dv[:, n, :, :], view3(half(0), P)[:, :, n // 2 * HD:n // 2 * HD + HD], ACT.Copy, after=("dv",))
        def cumulate(e, i):
            up, up1 = C("upper"), C("upper", 2 * P)
            e.matmul(bank[5][:, 0:NH], up, LA[:, 0, :], start=True, stop=True)
            e.matmul(bank[5][:, NH:2 * NH], ones, LA[:, 0, :], start=True, stop=False)
            e.matmul(bank[5][:, NH:2 * NH], up, LA[:, 1, :], start=False, stop=True)
            e.matmul(bank[5][0:NH, 256:512], LA[:, 0, :], up1, start=True, stop=False)
            e.matmul(bank[5][0:NH, 384:512], LA[:, 1, :], up, start=False, stop=True)
            e.matmul(bank[6][0:40, 256:512], LF[:, 0, :], up1, start=True, stop=False)
            return e.matmul(bank[6][0:40, 384:512], LF[:, 1, :], up, start=False, stop=True)
        p.add("pe", "cum", cumulate, after=("LA", "LF1"))
        copy("dve", "acum", acum, view3(bank[5][:, 0:2 * NH], NH), after=("cum",))
        copy("dve", "acumT", acumT[0:NH, :], bank[5][0:NH, 256:512])
        copy("dve", "fcumT", fcumT[0:40, :], bank[6][0:40, 256:512], after=("fcumT.zero",))

        for g in range(GROUPS):
            cb = bank[1 + g][:, 0:3 * P]

            def cb_mm(e, i, g=g, cb=cb):
                e.matmul(cb[:, 0:T], BCT[:, g, 0:P], BCT[:, 2 + g, :], start=True, stop=True)
                return e.matmul(cb[:, T:], BCT[:, g, P:T], BCT[:, 2 + g, P:T], start=True, stop=True)
            p.add("pe", f"cb{g}", cb_mm, after=("bc3.silu",))
            for n in range(2):
                tt(f"cbt{g}{n}", CBT[:, 2 * g + n, :], cb, C("upper", 3 * P), ALU.mult, after=(f"cb{g}",))
        for n in range(4):
            freed[n] = f"bc{n}"
        freed[4], freed[5], freed[6] = "dk0", "dk1", "dv"
        pre_steps = ("bc3.silu", "fcumT", "dv3", "cbt11", "g.in", "sink")

        p.phase("heads", PAIRS)
        used[0] = block1_end
        qs = {b: carve(T) for b in "bcd"}
        ks = {b: carve(T) for b in "bcd"}
        vs = {b: carve(TT, P) for b in "bc"}
        vd = carve(TT, HD)
        am = carve(T)
        Pr = carve(3, SROW)
        PT = [carve(3 * P) for _ in range(3)]
        mx = carve(6)
        sm = carve(6)
        xsT = carve(T)
        xdt = carve(TT, P)
        zs = carve(T)
        zt = carve(T)
        dec = carve(3 * P)
        MT1 = carve(3 * P)
        yx = carve(T)
        adaW = [carve(D) for _ in range(2)]
        heads_end = used[0]

        NW = 17
        BQ, BK, BV, CQ, CK, CV, DQ, XS, ZS = range(9)
        ORDER = (BQ, BK, CQ, CK, DQ, BV, CV, XS, ZS)
        for n in ORDER:
            load(f"w{n}", n, lambda i, n=n: a["w_heads"][i * NW + n, :, :], prev=(f"proj{n}",))

        last_gate = {0: 6, 1: 7, 2: 5}

        def load_gate(j):
            s = 9 + j % 3
            load(f"w{9 + j}", s, lambda i: a["w_heads"][i * NW + (9 + j), :, :],
                 after=(f"proj{9 + j - 3}",) if j >= 3 else (), prev=() if j >= 3 else (f"proj{9 + last_gate[j]}",))
        for j in range(4):
            load_gate(j)
        def load_ada(n):
            p.dma(f"adaw{n}", lambda e, i: e.dma_start(adaW[n % 2], a["ada_w"][i * 6 + n, :, :]),
                  after=(f"ada{n - 2}",) if n >= 2 else (), prev=() if n >= 2 else (f"ada{n + 4}",))
        for n in range(3):
            load_ada(n)
        for j in range(4, 8):
            load_gate(j)
        for n in range(3, 6):
            load_ada(n)

        halves = {}
        count = [0]

        def proj(n, evac, token=False):
            h = count[0] % 2
            count[0] += 1
            s = n if n < 9 else 9 + (n - 9) % 3
            waits = (f"w{n}",) + ((halves[h],) if h in halves else pre_steps)
            p.add("pe", f"proj{n}", project_tokens(half(h), slot[s]) if token else project(half(h), slot[s], hT),
                  after=waits, prev=(last_halves[h],) if h not in halves else ())
            halves[h] = evac
            return half(h)

        last_halves = {0: "gate7", 1: "gate6"}

        def gate(j):
            o = proj(9 + j, f"gate{j}")
            act(f"gate{j}", lambda i: gates[:, bass.ds(i * 8 + j, 1), :], o.unsqueeze(1), ACT.Tanh,
                after=(f"proj{9 + j}",), scale=0.5)

        for b, q, k in (("b", BQ, BK), ("c", CQ, CK)):
            oq = proj(q, f"q{b}")
            act(f"q{b}", qs[b], oq, ACT.Copy, after=(f"proj{q}",), scale=HD ** -0.5)
            ok = proj(k, f"k{b}")
            copy("dve", f"k{b}", ks[b], ok, after=(f"proj{k}",))
        oq = proj(DQ, "qd")
        act("qd", qs["d"], oq, ACT.Copy, after=(f"proj{DQ}",), scale=HD ** -0.5)
        copy("pool", "kd", ks["d"], lambda i: dk[:, bass.ds(i, 1), :].rearrange("p a n -> p (a n)"), prev=("s.d1",),
             after=pre_steps)
        copy("pool", "vd", vd, lambda i: dv[:, bass.ds(i, 1), :, :].rearrange("p a b c -> p (a b) c"), prev=("pv.d1",))
        ov = proj(BV, "vb", token=True)
        copy("dve", "vb", vs["b"], view3(ov, P), after=(f"proj{BV}",))
        ov = proj(CV, "vc", token=True)
        copy("dve", "vc", vs["c"], view3(ov, P), after=(f"proj{CV}",))

        S = {b: bank[2 + n] for n, b in enumerate("bcd")}

        def forget(hh):
            last = (f"s.c{hh - 1}",) if hh else ()
            ts(f"rf{hh}", rf[0:NH, :], fcumT[0:NH, :],
               lambda i: cst[0:NH, bass.ds(i * 2 + (CCOL["pick"] + hh), 1)], None, ALU.mult,
               after=last + ("rf.ones", "lf.ones", "fcumT"), prev=() if hh else ("s.c1",))
            ts(f"lf{hh}", lf[32:40, :], fcumT[32:40, :],
               lambda i: cst[32:40, bass.ds(i * 2 + (CCOL["pick"] + hh), 1)], None, ALU.mult)

        def scores(b, hh):
            lo = hh * HD
            q, k, o = qs[b], ks[b], S[b]

            def emit(e, i):
                r = {"b": i * 2 + hh, "c": 2 * NH, "d": i * 2 + (NH + hh)}[b]
                for t in range(TT):
                    at, n = (0, P) if t == 0 else (P + 1, T)
                    if b == "c":
                        bias = Hk[:, r, T - n:LOGIT]
                    else:
                        bias = Hk[:, bass.ds(r, 1), T - n:LOGIT].rearrange("p a n -> p (a n)")
                    e.matmul(o[:, at:at + n + 1], flip, bias, start=True, stop=False)
                    if b == "c":
                        e.matmul(o[:, at:at + n], lf[:, t * P:(t + 1) * P], rf[:, 0:n], start=False, stop=False)
                    last = e.matmul(o[:, at:at + n], q[lo:lo + HD, t * P:(t + 1) * P], k[lo:lo + HD, 0:n],
                                    start=False, stop=True)
                return last
            ready = {"b": ("qb", "kb"), "c": ("qc", "kc", f"lf{hh}"), "d": ("qd", "kd")}[b]
            free = (f"e.{b}0.1", "yx") if hh else ()
            p.add("pe", f"s.{b}{hh}", emit, after=ready + free + pre_steps, prev=() if hh else (f"e.{b}1.1", "y.ssd"))

        def softmax(hh):
            for n, b in enumerate("bcd"):
                for t in range(TT):
                    cols = S[b][:, 0:P + 1] if t == 0 else S[b][:, P + 1:SROW]
                    p.add("dve", f"mx.{b}{hh}{t}", lambda e, i, n=n, t=t, cols=cols: e.tensor_reduce(
                        mx[:, 2 * n + t:2 * n + t + 1], cols, AX.X, ALU.max, negate=True),
                        after=(f"s.{b}{hh}",) + ((f"e.{b}0.{t}",) if hh else ()), prev=() if hh else (f"e.{b}1.{t}",))
            for n, b in enumerate("bcd"):
                for t in range(TT):
                    cols = slice(0, P + 1) if t == 0 else slice(P + 1, SROW)
                    act(f"e.{b}{hh}.{t}", Pr[:, n, cols], S[b][:, cols], ACT.Exp,
                        after=(f"mx.{b}{hh}1",) + ((f"t.{b}0",) if hh else ()), prev=() if hh else (f"t.{b}1",),
                        bias=mx[:, 2 * n + t:2 * n + t + 1], accum_out=sm[:, 2 * n + t:2 * n + t + 1])
                p.add("dve", f"r.{b}{hh}", lambda e, i, n=n: e.reciprocal(sm[:, 2 * n:2 * n + 2], sm[:, 2 * n:2 * n + 2]),
                      after=(f"e.{b}{hh}.1",))
                for t in range(TT):
                    at, m = (0, P) if t == 0 else (P + 1, T)
                    ts(f"p.{b}{hh}.{t}", Pr[:, n, at:at + m], Pr[:, n, at:at + m], sm[:, 2 * n + t:2 * n + t + 1],
                       None, ALU.mult, after=(f"r.{b}{hh}",))

        def turn_p(hh):
            for n, b in enumerate("bcd"):
                tb = bank[5 + n % 2]

                def emit(e, i, n=n, tb=tb):
                    e.transpose(tb[:, 0:P], Pr[:, n, 0:P], ident)
                    e.transpose(tb[:, P:T], Pr[:, n, P + 1:T + 1], ident)
                    return e.transpose(tb[:, T:3 * P], Pr[:, n, T + 1:SROW - 1], ident)
                before = {0: ("pt.d0", "yt.c0") if hh else (), 1: ("pt.c0", "yt.d0") if hh else (), 2: (f"pt.b{hh}",)}[n]
                back = {0: () if hh else ("pt.d1", "yt.c1"), 1: () if hh else ("pt.c1", "yt.d1"), 2: ()}[n]
                p.add("pe", f"t.{b}{hh}", emit, after=(f"p.{b}{hh}.1",) + before, prev=back)
                o = PT[n]
                if b == "c":
                    copy("dve", f"pt.{b}{hh}", o, tb[:, 0:3 * P], after=(f"t.{b}{hh}",) + ((f"pv.{b}0",) if hh else ()),
                         prev=() if hh else (f"pv.{b}1",))
                else:
                    act(f"pt.{b}{hh}", o, tb[:, 0:3 * P], ACT.Copy, after=(f"t.{b}{hh}",) + ((f"pv.{b}0",) if hh else ()),
                        prev=() if hh else (f"pv.{b}1",))

        O = {"b": bank[7][:, 0:T], "c": bank[5][:, 0:T], "d": bank[6][:, 0:T]}

        def weigh(hh):
            lo = hh * HD
            for n, b in enumerate("bcd"):
                def emit(e, i, n=n, b=b):
                    v0, v1 = (vd[:, 0, :], vd[:, 1, :]) if b == "d" else \
                        (vs[b][:, 0, lo:lo + HD], vs[b][:, 1, lo:lo + HD])
                    e.matmul(O[b][lo:lo + HD, :], v0, PT[n][:, 0:T], start=True, stop=False)
                    return e.matmul(O[b][lo:lo + HD, P:T], v1, PT[n][:, T:3 * P], start=False, stop=True)
                ready = {"b": ("vb",), "c": ("vc", f"pt.d{hh}"), "d": ("vd", f"pt.c{hh}")}[b]
                p.add("pe", f"pv.{b}{hh}", emit, after=(f"pt.{b}{hh}",) + ready, prev=(f"yt.{b}1",) if hh == 0 else ())
                act(f"yt.{b}{hh}", lambda i, n=n: YT[1 + n][lo:lo + HD, bass.ds(i, 1), :], O[b][lo:lo + HD, :].unsqueeze(1),
                    ACT.Copy, after=(f"pv.{b}{hh}",), scale=0.5)

        def ada(n):
            third = adaA[:, n % 3 * D:(n % 3 + 1) * D]
            stt(f"ada{n}", third, adaW[n % 2], lambda i: sc[:, bass.ds(i * 2 + n // 3, 1)], third, ALU.mult, ALU.add,
                after=(f"adaw{n}", "sc", "ada.zero"))

        forget(0)
        for b in "bcd":
            scores(b, 0)
        softmax(0)
        ox = proj(XS, "xpad")
        act("xpad", pad1[:, CONV1 - 1:], ox, ACT.Copy, after=(f"proj{XS}", "bc3.silu"), prev=("xs.tap3",))
        conv_tile("xs", 0, ("xpad",), xsT,
                  lambda i, j: bass.ds(i + 8 * CONV1, 1) if j is None else bass.ds(i * CONV1 + j, 1))
        oz = proj(ZS, "zs")
        act("zt", zt, oz, ACT.Tanh, after=(f"proj{ZS}",), prev=("zs",), scale=0.5)
        stt("zs", zs, zt, 1.0, oz, ALU.add, ALU.mult, after=("zt",))
        gate(0)
        turn_p(0)
        def turn_x(e, i):
            e.transpose(bank[2][:, 0:P], xsT[:, 0:P], ident)
            return e.transpose(bank[2][:, P:T], xsT[:, P:T], ident)
        p.add("pe", "turn.x", turn_x, after=("xs.silu", "e.b0.1"))
        for hh in range(2):
            for t in range(TT):
                ts(f"xdt{hh}{t}", xdt[:, t, hh * HD:hh * HD + HD], bank[2][:, t * P + hh * HD:t * P + hh * HD + HD],
                   lambda i, hh=hh, t=t: dtc[:, t, bass.ds(i * 2 + hh, 1)], None, ALU.mult, after=("turn.x",))
        gate(1)
        for hh in range(2):
            lo = hh * HD
            ts(f"am{hh}", am[0:NH, :], acumT[0:NH, :], lambda i, hh=hh: cst[0:NH, bass.ds(i * 2 + (CCOL["pick"] + hh), 1)],
               None, ALU.mult, after=("rowb0",) if hh else (), prev=() if hh else ("rowb1",))
            rb = bank[3][:, 0:T]
            p.add("pe", f"rowb{hh}", lambda e, i, rb=rb: e.matmul(rb, ones[0:NH, :], am[0:NH, :], start=True, stop=True),
                  after=(f"am{hh}", "e.c0.1") + (("d1.0",) if hh else ()))
            for t, (at, n) in enumerate(((0, T), (T, P))):
                ts(f"d{t}.{hh}", dec[:, at:at + n], rb[:, T - n:T], lambda i, hh=hh, t=t: acum[:, t, bass.ds(i * 2 + hh, 1)],
                   0.0, ALU.subtract, ALU.min, after=(f"rowb{hh}",) + (("m0",) if hh else ()))
            act(f"dexp{hh}", dec, dec, ACT.Exp, after=(f"d1.{hh}",))
            tt(f"m{hh}", MT1, dec, lambda i: CBT[:, bass.ds(i, 1), :].rearrange("p a n -> p (a n)"), ALU.mult,
               after=(f"dexp{hh}",) + (("y0",) if hh else ()))
            gate(2 + hh)

            def y_mm(e, i, lo=lo):
                o = bank[4][lo:lo + HD, 0:T]
                e.matmul(o, xdt[:, 0, lo:lo + HD], MT1[:, 0:T], start=True, stop=False)
                return e.matmul(o[:, P:T], xdt[:, 1, lo:lo + HD], MT1[:, T:3 * P], start=False, stop=True)
            p.add("pe", f"y{hh}", y_mm, after=(f"m{hh}", "xdt11", "e.d0.1"))
        stt("yx", yx, xsT, lambda i: par[:, bass.ds(i + PCOL["d_skip"], 1)], bank[4][:, 0:T], ALU.mult, ALU.add, after=("y1",))
        tt("y.ssd", lambda i: YT[0][:, bass.ds(i, 1), :], yx.unsqueeze(1), zs.unsqueeze(1), ALU.mult, after=("yx", "zs"))

        forget(1)
        ada(0)
        ada(1)
        for b in "bcd":
            scores(b, 1)
        softmax(1)
        weigh(0)
        ada(2)
        ada(3)
        gate(4)
        gate(5)
        turn_p(1)
        ada(4)
        ada(5)
        gate(6)
        weigh(1)
        gate(7)
        freed.update({n: f"proj{n}" for n in range(9)})
        freed.update({9 + n: f"proj{9 + last_gate[n]}" for n in range(3)})

        p.phase("ssd norm")
        used[0] = block1_end
        sqs = carve(W // P, T)
        rsb = carve(T)
        sqrt_table("ya")
        tt("ya.sq", sqs, YT[0], YT[0], ALU.mult, after=("y.ssd", "pv.d1"))

        def mean_mm(e, i, psum=bank[0][:, 0:T], src=sqs, n=W // P, w=None):
            for k in range(n):
                last = e.matmul(psum, w if w is not None else ones, src[:, k, :], start=k == 0, stop=k == n - 1)
            return last
        p.add("pe", "ya.sum", mean_mm, after=("ya.sq", "gate7"))
        ts("ya.ms", rsb, bank[0][:, 0:T], 1.0 / W, 4e-6, ALU.mult, ALU.add, after=("ya.sum",))
        act("ya.sd", rsb, rsb, ACT.Sqrt, after=("ya.ms",))
        p.add("dve", "ya.rs", lambda e, i: e.reciprocal(rsb, rsb), after=("ya.sd",))
        ts("ya.half", rsb, rsb, 0.5, None, ALU.mult, after=("ya.rs",))
        for k in range(W // P):
            stt(f"ya.y{k}", YT[0][:, k, :], YT[0][:, k, :], PC("ssm_norm", k), rsb, ALU.mult, ALU.mult, after=("ya.half",))

        p.phase("mix", KT)
        mixT = carve(KT, T)
        tb = [carve(T) for _ in range(N_BR)]
        for s in (1, 2, 3, 0):
            load(f"wb{s}", s, lambda i, s=s: a["w_br"][i * 4 + s, :, :], prev=(f"br{s}",), width=W)
        for b in (1, 2, 3, 0):
            p.add("pe", f"br{b}", project(half(b), slot[b][:, 0:W], YT[b], kt=W // P), after=(f"wb{b}", "yt.d1") + (("ya.y3",) if b == 0 else ()),
                  prev=(f"br{b}.gate",))
            stt(f"br{b}.gate", tb[b].unsqueeze(1), lambda i, b=b: gates[:, bass.ds(i + b * KT, 1), :], 1.0,
                half(b).unsqueeze(1), ALU.add, ALU.mult, after=(f"br{b}",), prev=("mix",) if b == 1 else ())
            if b == 3:
                tt("mix23", tb[2], tb[2], tb[3], ALU.add, after=("br3.gate",), eng="pool")
        tt("mix01", tb[0], tb[0], tb[1], ALU.add, after=("br0.gate",), eng="pool")
        tt("mix", lambda i: mixT[:, bass.ds(i, 1), :], tb[0].unsqueeze(1), tb[2].unsqueeze(1), ALU.add, after=("mix01",),
           eng="pool")
        freed.update({s: f"br{s}" for s in range(4)})

        p.phase("w_out")
        quarter = [(t, h) for t in range(TT) for h in range(2)]

        def residual(name, after, banks):
            def emit(e, i):
                for n, (t, h) in enumerate(quarter):
                    last = e.matmul(banks[n][:, :], ident, x[:, t, h * 512:(h + 1) * 512], start=True, stop=False)
                return last
            p.add("pe", name, emit, after=after)

        def rows_times(w, lhs, banks, stop):
            def emit(e, i):
                for n, (t, h) in enumerate(quarter):
                    last = e.matmul(banks[n][:, :], lhs[:, t * P:(t + 1) * P], w[:, h * 512:(h + 1) * 512],
                                    start=False, stop=stop)
                return last
            return emit
        residual("x.in", ("mix",), bank[4:8])
        for k in range(KT):
            s = 4 + k
            load(f"wo{k}", s, lambda i, k=k: a["w_out"][k * P:(k + 1) * P, :])
            p.add("pe", f"out{k}", rows_times(slot[s], mixT[:, k, :], bank[4:8], k == KT - 1), after=(f"wo{k}",))
            freed[s] = f"out{k}"
        sqrt_table("norm2")
        for n, (t, h) in enumerate(quarter):
            o = x[:, t, h * 512:(h + 1) * 512]
            if n % 2:
                act(f"x1.{n}", o, bank[4 + n][:, :], ACT.Copy, after=("out7",))
            else:
                copy("dve", f"x1.{n}", o, bank[4 + n][:, :], after=("out7",))

        p.phase("ffn norm")
        mod = small[:, 0:24]
        gs = small[:, 24:32]
        a0h, oka = small[:, 32:40], small[:, 40:48]

        def ada_mm(e, i):
            for j in range(24):
                last = e.matmul(bank[3][:, T + j:T + j + 1], adaA[:, j * P:(j + 1) * P], ones[:, 0:1], start=True, stop=True)
            return last
        p.add("pe", "mod.mm", ada_mm, after=("ada5", "out7"))
        p.dma("g_row", lambda e, i: e.dma_start(slot[N_SLOTS - 2][0:1, :], a["g_final"]), after=(freed[N_SLOTS - 2],))
        load("wlora", N_SLOTS - 1, lambda i: a["w_lora"])
        token_norm("norm2", "norm_ffn", hT, after=lambda t: (f"x1.{2 * t}", f"x1.{2 * t + 1}"))
        tt("mod", mod, bank[3][:, T:T + 24], par[:, PCOL["ada_b"]:PCOL["ada_b"] + 24], ALU.add, after=("mod.mm",))
        stt("gs", gs, mod[:, KT:2 * KT], 1.0, par[:, PCOL["norm_g"]:PCOL["norm_g"] + KT], ALU.add, ALU.mult)
        ts("a0h", a0h, par[:, PCOL["a0"]:PCOL["a0"] + KT], 0.5, None, ALU.mult)
        ts("oka", oka, par[:, PCOL["k_a"]:PCOL["k_a"] + KT], -1.0, 1.0, ALU.mult, ALU.add)

        residual("x1.in", ("x1.2", "x1.3"), bank[4:8])
        FF_STEP = 2
        FF_TRIPS = FF_TILES // FF_STEP
        ud = [carve(T) for _ in range(FF_STEP)]
        gu = [carve(T) for _ in range(FF_STEP)]
        tg = [carve(T) for _ in range(FF_STEP)]

        def ffn(last):
            for f in range(FF_STEP):
                for n, what in enumerate(("g", "u")):
                    load(f"w{what}{f}", 3 * f + n, lambda i, f=f, n=n: a["w_gu"][i * 2 * FF_STEP + (2 * f + n), :, :],
                         prev=(f"{what}{f}",))
                load(f"wd{f}", 3 * f + 2, lambda i, f=f: a["w_down"][bass.ds(i * FF_STEP * P + f * P, P), :],
                     prev=(f"down{f}",))
            for f in range(FF_STEP):
                for n, what in enumerate(("g", "u")):
                    p.add("pe", f"{what}{f}", project(half(2 * f + n), slot[3 * f + n], hT),
                          after=(f"w{what}{f}", "norm2.h7", "mod"), prev=(f"tg2.{f}" if what == "g" else f"ud{f}",))
                act(f"tg{f}", tg[f], half(2 * f), ACT.Tanh, after=(f"g{f}",), prev=(f"tg2.{f}",), scale=0.5)
                act(f"ud{f}", ud[f], half(2 * f + 1), ACT.Copy, after=(f"u{f}",), prev=(f"gu{f}",), scale=0.5)
                stt(f"tg2.{f}", tg[f], tg[f], 1.0, half(2 * f), ALU.add, ALU.mult, after=(f"tg{f}",))
                tt(f"gu{f}", gu[f], tg[f], ud[f], ALU.mult, after=(f"tg2.{f}", f"ud{f}"), prev=(f"down{f}",))
            for f in range(FF_STEP):
                p.add("pe", f"down{f}", rows_times(slot[3 * f + 2], gu[f], bank[4:8], last and f == FF_STEP - 1),
                      after=(f"wd{f}", f"gu{f}"))
        p.phase("ffn", FF_TRIPS - 1)
        ffn(False)
        p.phase("ffn end", at=FF_TRIPS - 1, peel=".end")
        ffn(True)
        for f in range(FF_STEP):
            freed[3 * f], freed[3 * f + 1], freed[3 * f + 2] = f"g{f}.end", f"u{f}.end", f"down{f}.end"
        p.phase("x2")
        sqrt_table("norm3")
        for n, (t, h) in enumerate(quarter):
            o = x[:, t, h * 512:(h + 1) * 512]
            if n % 2:
                act(f"x2.{n}", o, bank[4 + n][:, :], ACT.Copy, after=("down1.end",))
            else:
                copy("dve", f"x2.{n}", o, bank[4 + n][:, :], after=("down1.end",))

        p.phase("block 2 norm")
        used[0] = 0
        YR, CU, OG, GC, GR = (carve(KT, T) for _ in range(5))
        TW, AL = carve(T), carve(T)
        rsc = carve(T)
        w0 = carve(D)
        cst2 = carve(NCCOL - NFIRST)
        padz = carve(1 + T)
        squares = OG
        xg = OG[:, :, :].rearrange("p k n -> p (k n)").rearrange("p (t d) -> p t d", t=TT)
        low = carve(T)
        pads = {n: carve(1 + T) for n in ("r", "k", "v")}
        Az = [carve(T) for _ in range(2)]
        Rz = [carve(T) for _ in range(2)]
        block2_end = used[0]
        p.dma("cst2", lambda e, i: e.dma_start(cst2, a["cst"][:, NFIRST:NCCOL]), after=("x2.2", "x2.3"))
        p.dma("w0row", lambda e, i: e.dma_start(w0[0:1, :], a["w0"]), after=("x2.2", "x2.3"))

        def mean_over_channels(tag, src, b, after):
            def emit(e, i):
                for k in range(KT):
                    last = e.matmul(bank[b][:, 0:T], ones, src[:, k, :], start=k == 0, stop=k == KT - 1)
                return last
            p.add("pe", tag, emit, after=after)

        def spread(e, i):
            for h in range(2):
                last = e.matmul(bank[h][:, :], ones[0:1, :], slot[N_SLOTS - 2][0:1, h * 512:(h + 1) * 512], start=True, stop=True)
            return last
        p.add("pe", "g_final", spread, after=("g_row", "u1.end"))

        def token_scales(tag, src, after):
            for t in range(TT):
                act(f"{tag}.sq{t}", xn[:, t, :], src[:, t, :], ACT.Square, after=after(t), accum_out=stat[:, t:t + 1])
            ts(f"{tag}.ms", stat[:, 2:4], stat[:, 0:2], 1.0 / D, 1e-6, ALU.mult, ALU.add, after=(f"{tag}.sq{TT - 1}",))
            act(f"{tag}.sd", stat[:, 2:4], stat[:, 2:4], ACT.Sqrt, after=(f"{tag}.ms",))
            p.add("dve", f"{tag}.rs", lambda e, i: e.reciprocal(stat[:, 4:6], stat[:, 2:4]), after=(f"{tag}.sd",))

        def turn(name, b, src, k, after):
            def emit(e, i):
                for t in range(TT):
                    last = e.transpose(bank[b][:, t * P:(t + 1) * P], src[:, t, k * P:(k + 1) * P], ident)
                return last
            p.add("pe", name, emit, after=after)

        token_scales("norm3", x, lambda t: (f"x2.{2 * t}", f"x2.{2 * t + 1}"))
        for n, (t, h) in enumerate(quarter):
            c = slice(h * 512, (h + 1) * 512)
            stt(f"norm3.x{n}", xg[:, t, c], x[:, t, c], stat[:, 4 + t:5 + t], bank[h][:, :], ALU.mult, ALU.mult,
                after=("norm3.rs", "g_final"), lag=1 if n == 0 else 2)
        for k in range(KT):
            turn(f"norm3.turn{k}", 2 + k % 4, xg, k, ("norm3.x3", "x2.1") + ((f"norm3.h{k - 4}",) if k >= 4 else ()))
        token_scales("norm4", xg, lambda t: (f"norm3.x{2 * t + 1}",))
        for t in range(TT):
            ts(f"norm4.x{t}", xn[:, t, :], xg[:, t, :], stat[:, 4 + t:5 + t], None, ALU.mult, after=("norm4.rs",))
        for k in range(KT):
            act(f"norm3.h{k}", x3T[:, k, :], half(2 + k % 4), ACT.Copy, after=(f"norm3.turn{k}",))
        for k in range(KT):
            b = (6, 7, 0, 1)[k % 4]
            turn(f"norm4.turn{k}", b, xn, k, ("norm4.x1", "x2.3") + ((f"norm4.s{k - 4}",) if k >= 4 else ()))
            ts(f"norm4.s{k}", hT[:, k, :], half(b), gs[:, k:k + 1], mod[:, k:k + 1], ALU.mult, ALU.add, after=(f"norm4.turn{k}",))

        p.add("pool", "TW.zero", lambda e, i: e.memset(TW, 0.0), after=("norm3.h7",))
        p.add("pool", "AL.zero", lambda e, i: e.memset(AL, 0.0))
        for n in "rkv":
            p.add("pool", f"pad.{n}.zero", lambda e, i, n=n: e.memset(pads[n], 0.0))
        for n, z in (("Az", Az), ("Rz", Rz)):
            for hh in range(2):
                p.add("pool", n + ".zero" if hh else n + "0.zero", lambda e, i, z=z, hh=hh: e.memset(z[hh], 0.0))
        p.add("pool", "pad2.zero", lambda e, i: e.memset(padA[:, :], 0.0))
        p.add("pool", "padz.zero", lambda e, i: e.memset(padz, 0.0))
        for k in range(KT):
            p.add("pe", f"lora{k}", lambda e, i, k=k: e.matmul(half(5), slot[N_SLOTS - 1][:, k * P:(k + 1) * P], hT[:, k, :],
                  start=k == 0, stop=k == KT - 1), after=("wlora", "norm3.h7", f"norm4.s{k}"))
        freed[N_SLOTS - 1] = "lora7"
        act("lora.pad", padz[:, 1:], half(5), ACT.Copy, after=("lora7", "padz.zero"))
        tt("lora.d", low, padz[:, 0:T], padz[:, 1:], ALU.subtract, after=("lora.pad",))
        stt("lora.s", low, low, PC("mu", 24), padz[:, 1:], ALU.mult, ALU.add)
        act("TW", TW[0:HD, :], low[0:HD, :], ACT.Tanh, after=("lora.s", "TW.zero"))
        copy("dve", "AL", AL[HD:P, :], low[HD:P, :], after=("AL.zero",))

        XW = {n: carve(T) for n in "rkv"}
        aT, kkr, kk, rn, t1, kp, bT = (carve(T) for _ in range(7))
        lw = carve(T)
        ex = carve(2 * T)
        en = carve(T)
        eT = carve(1)
        odd = carve(T)
        Bf, Kf = carve(T), carve(T)
        Nt, Mt, RBt, RKt = (carve(4, P) for _ in range(4))
        Nm = [carve(4, P) for _ in range(2)]
        Xs, Zs, Gs = (carve(4, P) for _ in range(3))
        tok = carve(4, P)
        Fs, Us, St = carve(P), carve(TT, P), carve(HD)
        bonus, Oc, osq, grs, rg, hv, cth = (carve(T) for _ in range(7))
        lo2 = carve(P)

        def off(l):
            return cst2[:, P + l * P:P + (l + 1) * P]

        def four(ap):
            return ap.unsqueeze(1).to_broadcast([P, 4, P])

        def pi(name, plus=0):
            return lambda i: par[:, bass.ds(i + (PCOL[name] + plus), 1)]

        rT, kT, vT = (XW[n] for n in "rkv")
        eI, eE = ex[:, 0:T], ex[:, T:2 * T]
        mid = cst[:, CCOL["mid"]:CCOL["mid"] + 2]
        NR = 9
        VAL, GATE, OGP, ROG, GCP, GRP = range(3, NR)
        FILL = dict(G1=10, turn=6, XZ1=4, G2=4, XZ2=2, G3=2, XZ3=3, G4=3, XZ4=2, G5=3,
                    XZ5=5, G6=3, XZ6=4, F0=4, U0=1, S=2, F1=1, U1=5, O=4, gn=4)
        assert sum(FILL.values()) == NR * KT

        def k_steps(name, n, b, k0, k1, after=(), prev=()):
            def emit(e, i):
                for k in range(k0, k1):
                    last = e.matmul(half(b), slot[n][:, k * P:(k + 1) * P], hT[:, k, :], start=k == 0, stop=k == KT - 1)
                return last
            p.add("pe", name, emit, after=after, prev=prev)

        def low_rank(next_, free):
            def low_mm(e, i):
                for t in range(TT):
                    o = bank[4][:, t * P:(t + 1) * P]
                    e.matmul(o, TW[:, t * P:(t + 1) * P], lo2, start=True, stop=False)
                    e.matmul(o, ones[0:1, :], w0[0:1, bass.ds((i + next_) * P, P)], start=False, stop=True)
                return e.matmul(bank[4][:, T:2 * T], lo2, AL, start=True, stop=True)
            p.add("pe", "low.mm", low_mm, after=("lo2", "TW", "w0row", "AL") + free, prev=("eT",))
            act("lw.tanh", lw, bank[4][:, 0:T], ACT.Tanh, after=("low.mm",), scale=0.5)
            act("a.tanh", aT, bank[4][:, T:2 * T], ACT.Tanh, after=("low.mm",), prev=("b",),
                bias=lambda i: a0h[:, bass.ds(i + next_, 1)], scale=0.5)

        def decays(next_):
            ts("lw", lw, lw, -0.5 * DECAY, -0.5 * DECAY, ALU.mult, ALU.add, after=("lw.tanh",))
            ts("a", aT, aT, 0.5, 0.5, ALU.mult, ALU.add, after=("a.tanh",), lag=2)

            def cw_mm(e, i):
                for m, tri in enumerate((C("upper"), C("strict"))):
                    for c in range(TT):
                        end = e.matmul(bank[4][:, m * T + c * P:m * T + c * P + P], lw[:, c * P:(c + 1) * P], tri,
                                       start=True, stop=True)
                return end
            p.add("pe", "cw.mm", cw_mm, after=("lw", "a.tanh"))
            act("en", en, bank[4][:, 0:T], ACT.Exp, after=("cw.mm",), prev=("B", "K"), bias=mid[:, 0:1], scale=-1.0)
            act("ex", ex, bank[4][:, :], ACT.Exp, prev=("R1", "A1"), bias=mid[:, 1:2])

        def whole_decay(free=()):
            act("eT", eT, bank[4][:, P - 1:P], ACT.Exp, after=("cw.mm",) + free)

        def shifts(next_, free, which="krv"):
            for n in which:
                yield lambda n=n: tt(f"sd.{n}", XW[n], pads[n][:, 0:T], pads[n][:, 1:], ALU.subtract,
                                     after=(f"pad.{n}", "pad.v.zero") + free)
            for n in which:
                j = "rkv".index(n)
                yield lambda j=j, n=n: stt(f"sh.{n}", XW[n], XW[n], lambda i: par[:, bass.ds(i + (next_ + PCOL["mu"] + 8 * j), 1)],
                                           pads[n][:, 1:], ALU.mult, ALU.add)

        def kk_norm(next_, free):
            yield lambda: ts("kkr", kkr, kT, pi("k_k", next_), None, ALU.mult)
            yield lambda: tt("kk.sq", rn, kkr, kkr, ALU.mult)

            def total():
                p.add("pe", "kk.sum", lambda e, i: e.matmul(bank[5][:, 0:T], C("pair"), rn, start=True, stop=True),
                      after=("kk.sq",) + free)
                act("kk.norm", rn, bank[5][:, 0:T], ACT.Sqrt, after=("kk.sum",))
            yield total

        def operands(next_, free_k, free_a):
            yield lambda: ts("t1", t1, aT, pi("k_a", next_), lambda i: oka[:, bass.ds(i + next_, 1)], ALU.mult, ALU.add)
            yield lambda: tt("kp", kp, kT, t1, ALU.mult)
            yield lambda: tt("K", Kf, kp, en, ALU.mult, after=("en",) + free_k)
            yield lambda: ts("kk.max", rn, rn, 1e-12, None, ALU.max, after=("kk.norm",))
            yield lambda: p.add("dve", "kk.rn", lambda e, i: e.reciprocal(rn, rn))
            yield lambda: tt("kk", kk, kkr, rn, ALU.mult)
            yield lambda: tt("b", bT, kk, aT, ALU.mult)
            yield lambda: tt("B", Bf, bT, en, ALU.mult)
            for hh in range(2):
                r = slice(hh * HD, hh * HD + HD)
                yield lambda hh=hh, r=r: stt(f"A{hh}", Az[hh][r, :], kk[r, :], -1.0, eE[r, :], ALU.mult, ALU.mult,
                                             after=("ex", "Az.zero", "Rz.zero") + free_a, lag=2)

        def receptances(free):
            for hh in range(2):
                r = slice(hh * HD, hh * HD + HD)
                tt(f"R{hh}", Rz[hh][r, :], rT[r, :], eI[r, :], ALU.mult, after=("ex", "Rz.zero") + free)

        def mask(l, eng="pool", after=()):
            tt(f"Nm{l}", Nm[l % 2], Nt, four(off(l)), ALU.mult, after=after, eng=eng)

        def n_products(loop):
            products("N.mm", 2, Bf, Az, ("A1", "B") + (("F1",) if loop else ()))
            products("N1.mm", 3, Az, Bf, ("U1",) if loop else ())
            act("N", Nt, quad(2), ACT.Copy, after=("N.mm",) + (("Nm6",) if loop else ()))

        def bonus_operand(next_):
            stt("rkr", t1, rT, pi("r_k", next_), kp, ALU.mult, ALU.mult, lag=2)

        def level_zero(loop):
            tt("X0.m", Xs, quad(3), four(cst2[:, 0:P]), ALU.mult, after=("N1.mm",))
            tt("X0", Xs, Xs, four(ident), ALU.add)
            tt("Z0.m", Zs, Nt, four(off(0)), ALU.mult, after=("N",) + (("U1.mm",) if loop else ()), eng="pool")
            tt("Z0", Zs, Zs, four(ident), ALU.add, eng="pool")
            mask(1, "dve", ("N",) + (("G5.mm",) if loop else ()))
            mask(2, "pool", ("G6.mm",) if loop else ())

        def products(name, b, lhs, rhs, after, prev=()):
            def emit(e, i):
                for q in range(4):
                    hh, c = q // 2, slice(q % 2 * P, q % 2 * P + P)
                    l = lhs[hh] if isinstance(lhs, list) else lhs
                    r = rhs[hh] if isinstance(rhs, list) else rhs
                    last = e.matmul(bank[b][:, q * P:(q + 1) * P], l[:, c], r[:, c], start=True, stop=True)
                return last
            p.add("pe", name, emit, after=after, prev=prev)

        def quad(b):
            return view3(bank[b][:, :], P)

        p.phase("first rkv", peel=".first")
        p.dma("lo2", lambda e, i: e.dma_start(lo2, a["lora2"][0, :, :]), after=("norm3.h7",))
        for j in range(3):
            load(f"rw{j}", j, lambda i, j=j: a["w_rwkv"][j, :, :])

        def first_projection(n, b, after):
            j = "rkv".index(n)
            k_steps(f"rp{j}", j, b, 0, KT, after=(f"rw{j}", "norm4.s7") + after)
            freed[j] = f"rp{j}.first"
            act(f"pad.{n}", pads[n][:, 1:], half(b), ACT.Copy, after=(f"rp{j}", "pad.v.zero"))
        first_projection("k", 1, ())
        low_rank(0, ())
        first_projection("r", 0, ("lora.pad",))
        decays(0)
        whole_decay()
        for step in (*shifts(0, (), "k"), *kk_norm(0, ())):
            step()
        first_projection("v", 1, ("pad.k",))
        for step in (*operands(0, (), ()), *shifts(0, (), "rv")):
            step()
        n_products(False)
        receptances(())
        products("RK.mm", 4, Kf, Rz, ("K", "R1", "eT"))
        level_zero(False)
        bonus_operand(0)

        def early_outputs(ns, ks, after=()):
            for n in ns:
                def emit(e, i, n=n):
                    for k in ks:
                        last = e.matmul(half(n), slot[n][:, k * P:(k + 1) * P], YR[:, k, :], start=k == 0, stop=k == KT - 1)
                    return last
                p.add("pe", f"r{n}.mm" if KT - 1 in ks else f"r{n}.early", emit,
                      after=(f"wr_early{n}.end",) + after)

        def rwkv(last):
            for n in range(3, NR):
                load(f"rw{n}", n, lambda i, n=n: a["w_rwkv"][i * NR + n, :, :], prev=(f"rp{n}.{KT}",))
                if n == 3 and not last:
                    p.dma("lo2", lambda e, i: e.dma_start(lo2, a["lora2"][i + 1, :, :]), after=("low.mm.first",), prev=("low.mm",))
            if not last:
                for n in range(3):
                    load(f"rw{n}", n, lambda i, n=n: a["w_rwkv"][i * NR + (n + NR), :, :], prev=(f"rp{n}.{KT}",))

            else:
                for n in range(4):
                    load(f"wr_early{n}", n, lambda i, n=n: a["w_y"][n * 2 + 1, :, :], prev=(f"rp{n}.{KT}",),
                         after=(f"rp{n}.{KT}.end",) if n == 3 else ())

            queue = []
            reader = {}

            def queued(n, evac, reads):
                b = len(queue) // KT % 2
                for k in range(KT):
                    queue.append((n, b, k, evac if k == KT - 1 else None,
                                  (reader[b],) if b in reader else (), () if b in reader else ({0: "gr", 1: "gc"}[b],)))
                reader[b] = reads

            def fill(n):
                while n and queue:
                    s, b, k, evac, before, back = queue[0]
                    m = min(n, sum(1 for q in queue[:KT] if q[0] == s))
                    first = ("pad.r.first", "pad.v.first") if k == 0 and back else ()
                    k_steps(f"rp{s}.{k + m}", s, b, k, k + m, after=(f"rw{s}",) + before + first, prev=back)
                    evac = queue[m - 1][3]
                    del queue[:m]
                    n -= m
                    if evac:
                        evac(half(b))

            def later(step):
                if last:
                    step()
                else:
                    side.insert(2, step)

            def store_tanh(name, dst, n, then=None):
                def evac(o):
                    act(name if then is None else name + ".th", dst, o.unsqueeze(1), ACT.Tanh, after=(f"rp{n}.{KT}",), scale=0.5)
                    if then:
                        later(lambda: stt(name, dst, dst, 1.0, o.unsqueeze(1), ALU.add, ALU.mult, after=(name + ".th",)))
                return evac

            def gate_evac(o):
                act("conv.th", cth, o, ACT.Tanh, after=(f"rp{GATE}.{KT}",), prev=("conv.u",), scale=0.5)
                stt("conv.u", padA[:, CONV2 - 1:], cth, 1.0, hv, ALU.add, ALU.mult, after=("conv.th", "hv", "pad2.zero"))

            def rog_evac(o):
                act("rg.th", rg, o, ACT.Tanh, after=(f"rp{ROG}.{KT}",), prev=("YR",), scale=0.5)
                later(lambda: stt("rg", rg, rg, 1.0, o, ALU.add, ALU.mult, after=("rg.th",)))
            queued(VAL, lambda o: act("hv", hv, o, ACT.Copy, after=(f"rp{VAL}.{KT}",), prev=("conv.u",), scale=0.5), "hv")
            queued(GATE, gate_evac, "conv.th")
            if not last:
                for j, n in enumerate("rkv"):
                    queued(j, lambda o, j=j, n=n: act(f"pad.{n}", pads[n][:, 1:], o, ACT.Copy, after=(f"rp{j}.{KT}", "sh.v.first"),
                                                     prev=(f"sh.{n}",)), f"pad.{n}")
            queued(OGP, store_tanh("og", lambda i: OG[:, bass.ds(i, 1), :], OGP, True), "og")
            queued(ROG, rog_evac, "rg")
            queued(GCP, store_tanh("gc", lambda i: GC[:, bass.ds(i, 1), :], GCP), "gc")
            queued(GRP, store_tanh("gr", lambda i: GR[:, bass.ds(i, 1), :], GRP), "gr")

            products("M.mm", 6, Kf, Az, ("B.first",), ("St",))

            def turn_tok(e, i):
                for n, src in enumerate((Bf[:, 0:P], Kf[:, 0:P], vT[:, 0:P], vT[:, P:T])):
                    end = e.transpose(bank[5][:, n * P:(n + 1) * P], src, ident)
                return end

            def bonus_products():
                products("RB.mm", 7, Bf, Rz, ("R1.first",), ("O.copy",))
                p.add("pe", "bonus.sum", lambda e, i: e.matmul(bank[5][:, 0:T], C("pair"), t1, start=True, stop=True),
                      after=("rkr.first", "kk.norm.first"), prev=("gn.ms", "rkr"))

            def turn_and_mask():
                tt("M", Mt, quad(6), four(C("strict")), ALU.mult, after=("M.mm",), lag=2)
                tt("bonus", bonus, vT, bank[5][:, 0:T], ALU.mult, after=("bonus.sum",), lag=2)
                p.add("pe", "turn.tok", turn_tok, after=("bonus",))
                act("tok", tok, quad(5), ACT.Copy, after=("turn.tok",))

            def tap(j):
                w = lambda i: par[:, bass.ds(i * CONV2 + (PCOL["conv_k"] + j), 1)]
                o = odd.unsqueeze(1) if j % 2 else lambda i: CU[:, bass.ds(i, 1), :]
                src = padA[:, j:j + T].unsqueeze(1)
                if j == 0:
                    ts("tap0", o, src, w, pi("conv_b2"), ALU.mult, ALU.add)
                elif j == 1:
                    ts("tap1", o, src, w, None, ALU.mult, lag=2)
                else:
                    stt(f"tap{j}", o, src, w, o, ALU.mult, ALU.add, lag=2)
            side = [lambda: tt("RB", RBt, quad(7), four(C("upper")), ALU.mult, after=("RB.mm",)),
                    lambda: tt("RK", RKt, quad(4), four(C("upper")), ALU.mult,
                               after=("RK.mm.first",), prev=("RK.mm",), lag=2)]
            taps = [lambda j=j: tap(j) for j in range(CONV2)]
            taps.append(lambda: tt("taps", lambda i: CU[:, bass.ds(i, 1), :], lambda i: CU[:, bass.ds(i, 1), :],
                                   odd.unsqueeze(1), ALU.add))
            if not last:
                free = ("turn.tok",)
                after_taps = [*shifts(1, free), *kk_norm(1, ("tok",)), *operands(1, (), ("F1.mm",))]
            else:
                after_taps = []

            def aside(n):
                for _ in range(min(n, len(side))):
                    side.pop(0)()

            for l in range(1, LEVELS):
                top = l == LEVELS - 1
                first, second = slice(0, HD), slice(HD, P)

                def g_mm(e, i, l=l, top=top, first=first, second=second):
                    if top:
                        for q in range(4):
                            end = e.matmul(bank[2][second, q * HD:(q + 1) * HD], Nm[l % 2][:, q, second], Xs[:, q, first],
                                           start=True, stop=True)
                        return end
                    for q in range(4):
                        end = e.matmul(bank[2][:, q * P:(q + 1) * P], Nm[l % 2][:, q, :], Xs[:, q, :], start=True, stop=True)
                    return end
                made = ("X0", "Z0", "Nm1", "Nm2", "N") if l == 1 else ()
                p.add("pe", f"G{l}.mm", g_mm, after=tuple(n + ".first" for n in made) + ((f"Nm{l}",) if l > 2 else ())
                      + ((f"X{l - 1}", f"G{l - 1}") if l > 1 else ()), prev=made)
                if l == 1:
                    bonus_products()
                fill(FILL[f"G{l}"])
                if top:
                    copy("dve", f"G{l}", Gs[second, :, first], view3(bank[2][second, 0:T], HD), after=(f"G{l}.mm",))
                else:
                    tt(f"G{l}", Gs, quad(2), four(ident), ALU.add, after=(f"G{l}.mm",))
                if l + 2 < LEVELS:
                    mask(l + 2, "pool", (f"G{l}.mm",))
                if l == 2 and not last:
                    decays(1)
                if l == 1:
                    turn_and_mask()
                    fill(FILL["turn"])
                aside(3)

                size = 2 ** l

                def columns_of(ap, half_of, size=size):
                    return ap.rearrange("p (n two s) -> p n two s", two=2, s=size)[:, :, half_of, :]

                def joined(b):
                    return bank[b][:, 0:2 * P].rearrange("p (n s) -> p n s", s=size)

                def xz_mm(e, i, l=l, columns_of=columns_of, size=size, top=top, first=first, second=second):
                    if top:
                        for q in range(4):
                            end = e.matmul(bank[6][first, q * HD:(q + 1) * HD], Gs[:, q, first], Zs[:, q, second],
                                           start=True, stop=True)
                        return end
                    for b, lhs, rhs, half_of in ((3, Zs, Gs, 0), (6, Gs, Zs, 1)):
                        for q in range(4):
                            end = e.matmul(bank[b][:, q * HD:(q + 1) * HD].rearrange("p (n s) -> p n s", s=size),
                                           lhs[:, q, :], columns_of(rhs[:, q, :], half_of), start=True, stop=True)
                    return end
                p.add("pe", f"XZ{l}.mm", xz_mm, after=(f"G{l}", "M") + ((f"X{l - 1}", f"Z{l - 1}") if l > 1 else ()))
                fill(FILL[f"XZ{l}"])
                if l < LEVELS - 1:
                    act(f"X{l}", columns_of(Xs.rearrange("p q n -> p (q n)"), 0), joined(3), ACT.Copy, after=(f"XZ{l}.mm",))
                if top:
                    copy("dve", f"Z{l}", Zs[first, :, second], view3(bank[6][first, 0:T], HD), after=(f"XZ{l}.mm",))
                else:
                    copy("dve", f"Z{l}", columns_of(Zs.rearrange("p q n -> p (q n)"), 1), joined(6), after=(f"XZ{l}.mm",))
                if l == 1:
                    side += taps[:24] + after_taps[:8] + taps[24:28] + after_taps[8:9] + taps[28:] + after_taps[9:]
                    if not last:
                        low_rank(1, ("RK",))
                aside(3)

            def V(c, hh):
                return tok[:, 2 + c, hh * HD:hh * HD + HD]

            for c in range(TT):
                def f_mm(e, i, c=c):
                    for hh in range(2):
                        o = bank[2][:, hh * HD:hh * HD + HD]
                        if c:
                            e.matmul(o, Az[hh][:, P:T], St, start=True, stop=False)
                        end = e.matmul(o, Mt[:, 2 * hh + c, :], V(c, hh), start=not c, stop=True)
                    return end
                p.add("pe", f"F{c}.mm", f_mm, after=("M", "tok", "G6") + (("St",) if c else ()))
                fill(FILL[f"F{c}"])
                copy("dve", f"F{c}", Fs, bank[2][:, 0:P], after=(f"F{c}.mm",))
                aside(3)

                def u_mm(e, i, c=c):
                    for hh in range(2):
                        end = e.matmul(bank[3][:, hh * HD:hh * HD + HD], Zs[:, 2 * hh + c, :], Fs[:, hh * HD:hh * HD + HD],
                                       start=True, stop=True)
                    return end
                p.add("pe", f"U{c}.mm", u_mm, after=(f"F{c}", "Z6", "X5"))
                fill(FILL[f"U{c}"])
                copy("dve", f"U{c}", Us[:, c, :], bank[3][:, 0:P], after=(f"U{c}.mm",))
                aside(3)
                if c == 0:
                    def s_mm(e, i):
                        for hh in range(2):
                            r = slice(hh * HD, hh * HD + HD)
                            e.matmul(bank[6][r, 0:HD], tok[:, 0, r], Us[:, 0, r], start=True, stop=False)
                            end = e.matmul(bank[6][r, 0:HD], tok[:, 1, r], V(0, hh), start=False, stop=True)
                        return end
                    p.add("pe", "S.mm", s_mm, after=("U0", "Z6"))
                    fill(FILL["S"])
                    ts("St", St, bank[6][:, 0:HD], eT, None, ALU.mult, after=("S.mm", "eT.first"), prev=("eT",))
                    if not last:
                        whole_decay(("St",))
                    aside(3)

            def o_mm(e, i):
                for c in range(TT):
                    for hh in range(2):
                        r = slice(hh * HD, hh * HD + HD)
                        o = bank[7][r, c * P:(c + 1) * P]
                        e.matmul(o, V(c, hh), RKt[:, 2 * hh + c, :], start=True, stop=False)
                        if c:
                            e.matmul(o, St, Rz[hh][:, P:T], start=False, stop=False)
                        end = e.matmul(o, Us[:, c, r], RBt[:, 2 * hh + c, :], start=False, stop=True)
                return end
            p.add("pe", "O.mm", o_mm, after=("U1", "RK", "RB"))
            fill(FILL["O"])
            if last:
                aside(99)
                mean_over_channels("ln.sum", CU, 4, ("taps", "RK"))
                ts("ln.mean", t1, bank[4][:, 0:T], 1.0 / D, None, ALU.mult, after=("ln.sum",))
                for h in range(2):
                    c = CU[:, h * 4:h * 4 + 4, :]
                    tt(f"ln.c{h}", c, c, t1.unsqueeze(1).to_broadcast([P, 4, T]), ALU.subtract, after=("ln.mean",), eng="pool")
            aside(99)
            act("O.copy", Oc, bank[7][:, 0:T], ACT.Copy, after=("O.mm",))
            if last:
                for h in range(2):
                    act(f"ln.sq{h}", hT[:, h * 4:h * 4 + 4, :], CU[:, h * 4:h * 4 + 4, :], ACT.Square, after=(f"ln.c{h}", "gr", "gc"))
            if not last:
                n_products(True)
                receptances(("O.mm",))
            p.add("pe", "gn.sum", lambda e, i: e.matmul(bank[5][:, 0:T], C("pair"), Oc, start=True, stop=True),
                  after=("O.copy", "tok") + (() if last else ("kk.norm",)))
            fill(FILL["gn"])
            if not last:
                products("RK.mm", 4, Kf, Rz, ("K", "R1", "eT"))
            stt("gn.c", Oc, bank[5][:, 0:T], -1.0 / HD, Oc, ALU.mult, ALU.add, after=("gn.sum",))
            tt("gn.sq", osq, Oc, Oc, ALU.mult)
            if not last:
                level_zero(True)
                bonus_operand(1)
            p.add("pe", "gn.var", lambda e, i: e.matmul(bank[5][:, 0:T], C("pair"), osq, start=True, stop=True), after=("gn.sq",))
            ts("gn.ms", grs, bank[5][:, 0:T], 1.0 / HD, 64e-5, ALU.mult, ALU.add, after=("gn.var",))
            act("gn.sd", grs, grs, ACT.Sqrt, after=("gn.ms",))
            if last:
                early_outputs((0, 1), range(KT - 1), ("YR", "gr", "gc"))
                mean_over_channels("ln.var", hT, 4, ("ln.sq1", "ln.mean"))
                early_outputs((2, 3), range(KT - 1), ("U1",))
            p.add("dve", "gn.rs", lambda e, i: e.reciprocal(grs, grs), after=("gn.sd",))
            stt("gn.y", Oc, Oc, pi("gn_g"), grs, ALU.mult, ALU.mult)
            stt("gn.b", Oc, Oc, pi("gn_b"), bonus, ALU.add, ALU.add)
            tt("YR", lambda i: YR[:, bass.ds(i, 1), :], Oc.unsqueeze(1), rg.unsqueeze(1), ALU.mult, after=("rg",))
            if last:
                ts("ln.ms", rsc, bank[4][:, 0:T], 1.0 / D, 1e-5, ALU.mult, ALU.add, after=("ln.var",))
                act("ln.sd", rsc, rsc, ACT.Sqrt, after=("ln.ms",))
                p.add("dve", "ln.rs", lambda e, i: e.reciprocal(rsc, rsc), after=("ln.sd",))
            assert not queue and not side

        p.phase("rwkv", R_PAIRS - 1)
        rwkv(False)
        p.phase("rwkv end", at=R_PAIRS - 1, peel=".end")
        rwkv(True)
        for n in range(3, NR):
            freed[n] = f"rp{n}.{KT}.end"
        for n in range(3):
            freed[n] = f"rp{n}.{KT}"

        p.phase("conv norm")
        used[0] = block2_end
        cv2 = carve(KT, T)
        mT = carve(KT, T)
        m0 = carve(T)
        ts("gate", mod[:, 16:24], mod[:, 16:24], 0.25, None, ALU.mult)

        QUAD = 4

        def out_products(tag, src, weight, n, after):
            load(f"w{tag}{n}", n, lambda i: weight(i * QUAD + n), prev=(f"{tag}{n}.mm",))
            p.add("pe", f"{tag}{n}.mm", project(half(n), slot[n], src), after=(f"w{tag}{n}",) + after, prev=(f"{tag}{n}",))
            freed[n] = f"{tag}{n}.mm"

        def tile(ap, n):
            return lambda i: ap[:, bass.ds(i * QUAD + n, 1), :]

        def norm_tiles():
            par_col = lambda name, n: (lambda i: par[:, bass.ds(i * QUAD + (n + PCOL[name]), 1)])
            four_tiles = [(n, tile(CU, n), tile(cv2, n)) for n in range(QUAD)]
            for n, c, v in four_tiles:
                stt(f"ln.g{n}", c, c, par_col("ln_g", n), rsc.unsqueeze(1), ALU.mult, ALU.mult, lag=min(1 + n, 2))
            for n, c, v in four_tiles:
                ts(f"ln.b{n}", c, c, par_col("ln_b", n), None, ALU.add, lag=QUAD)
                act(f"ln.th{n}", v, c, ACT.Tanh, after=(f"ln.b{n}",), scale=0.5)
            yield
            for n, c, v in four_tiles:
                stt(f"ln.si{n}", c, v, 1.0, c, ALU.add, ALU.mult, after=(f"ln.th{n}",))
            for n, c, v in four_tiles:
                tt(f"ln.y{n}", c, c, tile(OG, n), ALU.mult, lag=QUAD)
            yield

        for half_of, name in enumerate((".first", ".second")):
            p.phase("rwkv out" + name, at=half_of, peel=name)
            stages = norm_tiles()
            next(stages)
            if half_of == 0:
                early_outputs(range(4), [KT - 1], ("YR.end",))
            for n in range(QUAD):
                if half_of:
                    out_products("r", YR, lambda j: a["w_y"][j * 2 + 1, :, :], n, (f"r{n}.first",))
                stt(f"r{n}", tile(mT, n), tile(GR, n), 1.0, half(n).unsqueeze(1), ALU.add, ALU.mult, after=(f"r{n}.mm",),
                    lag=min(1 + n, 2))
                freed[n] = f"r{n}.mm" + name
                if n == 1:
                    next(stages)
        p.phase("gated", KT // QUAD)
        for n in range(QUAD):
            out_products("c", CU, lambda j: a["w_y"][j * 2, :, :], n, ("ln.y3.second", f"r{n}.second"))
            stt(f"c{n}.g", m0.unsqueeze(1), tile(GC, n), 1.0, half(n).unsqueeze(1), ALU.add, ALU.mult, after=(f"c{n}.mm",))
            stt(f"c{n}", tile(mT, n), m0.unsqueeze(1), 0.5, tile(mT, n), ALU.mult, ALU.add)

        p.phase("w_out2")
        sqrt_table("norm5")
        z_bank = (0, 1, 2)
        xf, sqf = ([carve(T) for _ in range(QUAD)] for _ in range(2))

        def turn_and_sum(k):
            def emit(e, i):
                for t in range(TT):
                    c = slice(t * P, (t + 1) * P)
                    e.transpose(bank[4 + 2 * t + k % 2][:, k // 2 * P:(k // 2 + 1) * P], xf[k % QUAD][:, c], ident)
                for t in range(TT):
                    c = slice(t * P, (t + 1) * P)
                    last = e.matmul(bank[3][:, t * KT + k:t * KT + k + 1], sqf[k % QUAD][:, c], ones[:, 0:1],
                                    start=True, stop=True)
                return last
            p.add("pe", f"z{k}.turn", emit, after=(f"z{k}.g", f"z{k}.sq"))

        for k in range(KT):
            n, b = k % QUAD, z_bank[k % 3]
            load(f"wz{k}", n, lambda i, k=k: a["w_out2"][k, :, :])
            p.add("pe", f"z{k}.mm", project(half(b), slot[n], mT), after=(f"wz{k}", "c3") + ((f"z{k - 3}",) if k > 2 else ()))
            freed[n] = f"z{k}.mm"
            if k:
                turn_and_sum(k - 1)
            xk = x3T[:, k, :]
            stt(f"z{k}", xk, half(b), mod[:, 16 + k:17 + k], xk, ALU.mult, ALU.add, after=(f"z{k}.mm",))
            free = (f"z{k - QUAD}.turn",) if k >= QUAD else ()
            act(f"z{k}.sq", sqf[n], xk, ACT.Square, after=(f"z{k}",) + free)
            ts(f"z{k}.g", xf[n], xk, PC("final_g", k), None, ALU.mult, after=free)
        turn_and_sum(KT - 1)

        p.phase("final")
        p.add("dve", "norm5.ss", lambda e, i: e.tensor_reduce(
            out=stat[:, 0:2], in_=bank[3][:, 0:TT * KT].rearrange("p (t k) -> p t k", t=TT), op=ALU.add, axis=AX.X),
            after=(f"z{KT - 1}.turn",))
        ts("norm5.ms", stat[:, 2:4], stat[:, 0:2], 1.0 / D, 1e-6, ALU.mult, ALU.add)
        act("norm5.sd", stat[:, 2:4], stat[:, 2:4], ACT.Sqrt, after=("norm5.ms",))
        p.add("dve", "norm5.rs", lambda e, i: e.reciprocal(stat[:, 4:6], stat[:, 2:4]), after=("norm5.sd",))
        ytok = hT[:, :, :].rearrange("p k n -> p (k n)").rearrange("p (t d) -> p t d", t=TT)
        for t in range(TT):
            y = ytok[:, t, :].rearrange("p (m two c) -> p two m c", two=2, c=P)
            for odd_k, b in enumerate(bank[4 + 2 * t:6 + 2 * t]):
                if odd_k:
                    act(f"y{t}.odd", y[:, 1], view3(b[:, :], P), ACT.Copy, after=("norm5.rs",), scale=stat[:, 4 + t:5 + t])
                else:
                    ts(f"y{t}.even", y[:, 0], view3(b[:, :], P), stat[:, 4 + t:5 + t], None, ALU.mult)
            p.dma(f"y_out{t}", lambda e, i, t=t: e.dma_start(out[t * P:(t + 1) * P, :], ytok[:, t, :]),
                  after=(f"y{t}.odd", f"y{t}.even"))

        block = ctx.enter_context(nc.Block())

        @block.tensor
        def _(e):
            p.run("pe", e)

        @block.scalar
        def _(e):
            p.run("act", e)

        @block.vector
        def _(e):
            p.run("dve", e)

        @block.gpsimd
        def _(e):
            p.run("pool", e)

        @block.sync
        def _(e):
            p.run("sp", e)
            for t in range(TT):
                e.wait_ge(p.named[f"y_out{t}"].sem, 16)


def col_slices(w, starts):
    k = w.shape[0] // P
    return np.stack([np.ascontiguousarray(w[:, s:s + P].reshape(k, P, P).transpose(1, 0, 2)).reshape(P, k * P)
                     for s in starts])


def by_partition(v):
    return np.ascontiguousarray(v.reshape(-1, P).T)


def layouts(w):
    o = {"x": w["x"][0], "cst": shape_constants(), "rel_bias": w["rel_bias"]}
    par = np.zeros((P, NPCOL), np.float32)
    convw = np.stack([w["conv_w"][0][j].reshape(8, P) for j in range(CONV1)], 1)
    convk = np.stack([w["conv_k_2"][0][j].reshape(KT, P) for j in range(CONV2)], 1)
    for name, v in (("norm_mix", by_partition(w["norm_mix"][0])), ("norm_ffn", by_partition(w["norm_ffn"][0])),
                    ("norm_final", by_partition(w["norm_final"])), ("norm_g", by_partition(w["norm_g_2"][0])),
                    ("final_g", by_partition(w["final_g_2"])), ("conv_w", convw.reshape(8 * CONV1, P).T),
                    ("conv_b", by_partition(w["conv_b"][0])), ("d_skip", by_partition(np.repeat(w["d_skip"][0], HD))),
                    ("ssm_norm", by_partition(w["ssm_norm_w"][0])), ("ada_b", by_partition(w["ada_b_2"][0])),
                    ("c", by_partition(w["c_2"][0])), ("conv_k", convk.reshape(KT * CONV2, P).T),
                    ("conv_b2", by_partition(w["conv_b_2"][0])), ("ln_g", by_partition(w["conv_ln_g_2"][0])),
                    ("ln_b", by_partition(w["conv_ln_b_2"][0])), ("mu", by_partition(w["rwkv_mu_2"][0])),
                    ("a0", by_partition(w["rwkv_a0_2"][0])), ("k_k", by_partition(w["rwkv_k_k_2"][0])),
                    ("k_a", by_partition(w["rwkv_k_a_2"][0])), ("r_k", by_partition(w["rwkv_r_k_2"][0].reshape(-1))),
                    ("gn_g", by_partition(w["rwkv_gn_g_2"][0])), ("gn_b", by_partition(w["rwkv_gn_b_2"][0]))):
        par[:, PCOL[name]:PCOL[name] + v.shape[1]] = v
    o["par"] = par
    o["row"] = np.concatenate([w["dt_bias"][0], w["forget_bias"][0], w["a_log"][0], w["sinks"][0]])[None, :]
    o["w0"] = w["rwkv_w0_2"]
    o["g_final"] = w["norm_final"].reshape(1, D)
    wi = w["w_in"][0]
    both = lambda s: np.concatenate([wi[:, s:s + HD]] * 2, 1)
    o["w_pre"] = np.concatenate([col_slices(wi, (B0, B0 + P, C0, C0 + P)), col_slices(both(DK0), (0,)),
                                 col_slices(both(DK0 + HD), (0,)), col_slices(wi, (DV0,))])
    ws = np.concatenate([wi[:, DT0:DT0 + NH], wi[:, F0:F0 + NH]], 1)
    o["w_small"] = np.ascontiguousarray(ws.reshape(KT, P, 2 * NH).transpose(1, 0, 2)).reshape(P, -1)
    starts = []
    for i in range(PAIRS):
        starts += [s + i * P for s in (BQ0, BQ0 + W, BQ0 + 2 * W, CQ0, CQ0 + W, CQ0 + 2 * W, DQ0, X0, Z0)]
        starts += [G0 + i * D + j * P for j in range(KT)]
    o["w_heads"] = col_slices(wi, starts)
    wb = [col_slices(w["w_branch"][0, b], range(0, D, P)) for b in range(N_BR)]
    o["w_br"] = np.stack(wb, 1).reshape(KT * N_BR, P, W)
    o["w_out"] = w["w_out"][0]
    g, u = (col_slices(w[n][0], range(0, D_FF, P)) for n in ("w_ffn_gate", "w_ffn_up"))
    o["w_gu"] = np.stack([g, u], 1).reshape(2 * FF_TILES, P, D)
    o["w_down"] = w["w_ffn_down"][0]
    o["ada_w"] = np.ascontiguousarray(
        w["ada_w_2"][0].reshape(KT, P, 3, D).transpose(0, 2, 1, 3)).reshape(3 * KT, P, D)
    wi = w["w_in_2"][0]
    starts = []
    for i in range(R_PAIRS):
        starts += [s + i * P for s in (TS0, TS0 + D, TS0 + 2 * D, VAL0, GATE0, OG0, ROG0, GC0, GR0)]
    o["w_rwkv"] = col_slices(wi, starts)
    o["w_lora"] = col_slices(wi, (TS0 + 3 * D,))[0]
    lo = np.concatenate([w["rwkv_w2_2"][0], w["rwkv_a2_2"][0]], 0)
    o["lora2"] = np.ascontiguousarray(lo.reshape(P, KT, P).transpose(1, 0, 2))
    y = [col_slices(w[n][0], range(0, D, P)) for n in ("w_conv_out_2", "w_rwkv_out_2")]
    o["w_y"] = np.stack(y, 1).reshape(2 * KT, P, D)
    o["w_out2"] = col_slices(w["w_out_2"][0], range(0, D, P))
    return {k: np.ascontiguousarray(v) for k, v in o.items()}


def kernel(**inputs):
    import concourse.bacc as bacc
    from concourse.bass_utils import run_bass_kernel_spmd

    arrays = layouts({k: np.asarray(v) for k, v in inputs.items()})
    nc = bacc.Bacc("TRN2", target_bir_lowering=False, num_devices=1)
    aps = {n: nc.dram_tensor("in_" + n, v.shape, mybir.dt.from_np(v.dtype), kind="ExternalInput").ap() for n, v in arrays.items()}
    out = nc.dram_tensor("out_y", (T, D), F32, kind="ExternalOutput").ap()
    build(nc, aps, out)
    r = run_bass_kernel_spmd(nc, [{"in_" + n: v for n, v in arrays.items()}], core_ids=[0])
    return r.results[0]["out_y"].reshape(1, T, D)
```
